# Optimizing a Trainium2 kernel written in Bass

```python
import jax, jax.numpy as jnp
from jax import lax
import numpy as np

D_MODEL = 1024
BATCH = 1
SEQ = 256
DEPTH = 2

CTX_LEN = 256
GRID_W = 64
MLA_H = 6
Q_RANK = 256
KV_RANK = 128
NOPE_D = 64
ROPE_D = 32
V_D = 64
QK_D = NOPE_D + ROPE_D
ROPE_BASE = 10000.0
ML_H = 4
ML_D = 96
ML_W = ML_H * ML_D
ML_CONV = 3
ML_CHUNK = 64
NA_H = 4
NA_D = 64
NA_W = NA_H * NA_D
WIN_R = 8
WIN_C = 16
MLA_W = MLA_H * V_D
D_MIX = MLA_W + ML_W + NA_W
SPLIT_SIZES = (Q_RANK, KV_RANK, ROPE_D, ML_W, ML_W, 4 * ML_H, NA_W, NA_W, NA_W)
N_IN = Q_RANK + KV_RANK + ROPE_D + 2 * ML_W + 4 * ML_H + 3 * NA_W
N_EXPERTS = 16
N_GROUPS = 4
EXPERTS_PER_GROUP = N_EXPERTS // N_GROUPS
TOP_K = 2
D_FF_EXPERT = 256
Q_BLOCK = 128
EPS = 1e-6

kernel_name = "hybrid_mla_mlstm_natten_moe_dit"

def rmsnorm(x, g):
    xf = x.astype(jnp.float32)
    y = xf * lax.rsqrt(jnp.mean(xf * xf, axis=-1, keepdims=True) + EPS)
    return (y * g.astype(jnp.float32)).astype(x.dtype)

def head_layernorm(x, g):
    xf = x.astype(jnp.float32)
    mu = jnp.mean(xf, axis=-1, keepdims=True)
    var = jnp.mean(jnp.square(xf - mu), axis=-1, keepdims=True)
    y = (xf - mu) * lax.rsqrt(var + EPS)
    return (y * g.astype(jnp.float32).reshape(x.shape[-2:])).astype(x.dtype)

def heads_first(a):
    return jnp.transpose(a, (0, 2, 1, 3))

def merge_heads(o):
    B, H, L, d = o.shape
    return jnp.transpose(o, (0, 2, 1, 3)).reshape(B, L, H * d)

def split_cols(p):
    cuts = [int(v) for v in np.cumsum(SPLIT_SIZES)[:-1]]
    return jnp.split(p, cuts, axis=-1)

def axial_rope_tables(L, dtype):
    t = jnp.arange(L)
    row = (t // GRID_W).astype(jnp.float32)
    col = (t % GRID_W).astype(jnp.float32)
    quarter = ROPE_D // 4
    inv = ROPE_BASE ** (-jnp.arange(quarter, dtype=jnp.float32) / quarter)
    ar = row[:, None] * inv
    ac = col[:, None] * inv
    ang = jnp.concatenate([ar, ar, ac, ac], axis=-1)
    return jnp.cos(ang).astype(dtype), jnp.sin(ang).astype(dtype)

def apply_rope(a, cos, sin):
    a4 = a.reshape(a.shape[:-1] + (2, 2, ROPE_D // 4))
    rot = jnp.stack([-a4[..., 1, :], a4[..., 0, :]], axis=-2).reshape(a.shape)
    return a * cos[:, None, :] + rot * sin[:, None, :]

def with_rope(a, rope):
    if rope is None:
        return a
    cos, sin = rope
    return jnp.concatenate([a[..., :NOPE_D], apply_rope(a[..., NOPE_D:], cos, sin)], axis=-1)

def attend_blocks(q, k, v):
    B, H, Lq, d = q.shape
    scale = d ** -0.5
    nb = Lq // Q_BLOCK
    qb = jnp.moveaxis(q.reshape(B, H, nb, Q_BLOCK, d), 2, 0)

    def one(qi):
        s = jnp.einsum('bhqd,bhkd->bhqk', qi, k).astype(jnp.float32) * scale
        p = jax.nn.softmax(s, axis=-1)
        return jnp.einsum('bhqk,bhkd->bhqd', p.astype(v.dtype), v)

    o = lax.map(one, qb)
    return jnp.moveaxis(o, 0, 2).reshape(B, H, Lq, v.shape[-1])

def mla_q(q_c, qnorm_g, w_uq, q_g, rope):
    B, L, _ = q_c.shape
    q = (rmsnorm(q_c, qnorm_g) @ w_uq).reshape(B, L, MLA_H, QK_D)
    return heads_first(with_rope(rmsnorm(q, q_g), rope))

def mla_kv(c_kv, k_r, kvnorm_g, w_ukv, k_g, rope):
    B, L, _ = c_kv.shape
    kv = (rmsnorm(c_kv, kvnorm_g) @ w_ukv).reshape(B, L, MLA_H, NOPE_D + V_D)
    k = jnp.concatenate([kv[..., :NOPE_D], jnp.broadcast_to(k_r[:, :, None, :], (B, L, MLA_H, ROPE_D))], axis=-1)
    k = with_rope(rmsnorm(k, k_g), rope)
    return heads_first(k), heads_first(kv[..., NOPE_D:])

def ml_conv(u, w, b):
    out = lax.conv_general_dilated(u, w[:, None, :], window_strides=(1,),
                                   padding=[(ML_CONV // 2, ML_CONV // 2)],
                                   dimension_numbers=('NWC', 'WIO', 'NWC'),
                                   feature_group_count=u.shape[-1])
    return out + b

def ml_qkv(u, conv_w, conv_b, w_q, w_k, w_v):
    B, L, _ = u.shape
    uc = jax.nn.silu(ml_conv(u, conv_w, conv_b))
    uch = uc.reshape(B, L, ML_H, ML_D)
    uh = u.reshape(B, L, ML_H, ML_D)
    q = jnp.einsum('blhd,hde->bhle', uch, w_q)
    k = jnp.einsum('blhd,hde->bhle', uch, w_k) * (ML_D ** -0.5)
    v = jnp.einsum('blhd,hde->bhle', uh, w_v)
    return uc, q, k, v

def ml_gates(g, gate_b):
    B, L, _ = g.shape
    gg = (g + gate_b).astype(jnp.float32).reshape(B, L, 4, ML_H)
    gg = jnp.transpose(gg, (2, 0, 3, 1))
    return gg[0], gg[1], gg[2], gg[3]

def mlstm_chunkwise(q, k, v, i_pre, f_pre, state):
    B, H, L, d = q.shape
    nc = L // ML_CHUNK
    f32 = jnp.float32

    def chunks(a):
        a = a.reshape((B, H, nc, ML_CHUNK) + a.shape[3:])
        return jnp.moveaxis(a, 2, 0)

    xs = (chunks(q.astype(f32)), chunks(k.astype(f32)), chunks(v.astype(f32)),
          chunks(i_pre), chunks(jax.nn.log_sigmoid(f_pre)))
    tril = jnp.tril(jnp.ones((ML_CHUNK, ML_CHUNK), dtype=bool))

    def step(carry, inp):
        C, n, m = carry
        qc, kc, vc, ic, lf = inp
        b = jnp.cumsum(lf, axis=-1)
        dlog = jnp.where(tril, b[..., :, None] - b[..., None, :] + ic[..., None, :], -jnp.inf)
        inter = b + m[..., None]
        m_t = jnp.maximum(inter, jnp.max(dlog, axis=-1))
        dw = jnp.exp(dlog - m_t[..., None])
        iw = jnp.exp(inter - m_t)
        s = jnp.einsum('bhtd,bhsd->bhts', qc, kc) * dw
        num = iw[..., None] * jnp.einsum('bhed,bhtd->bhte', C, qc) + jnp.einsum('bhts,bhse->bhte', s, vc)
        nq = iw * jnp.einsum('bhd,bhtd->bht', n, qc) + jnp.sum(s, axis=-1)
        h = num / jnp.maximum(jnp.abs(nq), jnp.exp(-m_t))[..., None]
        b_end = b[..., -1]
        wlog = b_end[..., None] - b + ic
        m_new = jnp.maximum(b_end + m, jnp.max(wlog, axis=-1))
        a = jnp.exp(b_end + m - m_new)
        ws = jnp.exp(wlog - m_new[..., None])
        C_new = a[..., None, None] * C + jnp.einsum('bhs,bhse,bhsd->bhed', ws, vc, kc)
        n_new = a[..., None] * n + jnp.einsum('bhs,bhsd->bhd', ws, kc)
        return (C_new, n_new, m_new), h

    state, hs = lax.scan(step, state, xs)
    h = jnp.moveaxis(hs, 0, 2).reshape(B, H, L, d)
    return h.astype(q.dtype), state

def ml_out(h, uc, z, norm_g, skip):
    B, H, L, d = h.shape
    hn = head_layernorm(jnp.transpose(h, (0, 2, 1, 3)), norm_g).reshape(B, L, ML_W)
    return (hn + skip * uc) * jax.nn.silu(z)

def mlstm_mixer(u_x, z_x, g_x, u_y, z_y, g_y, conv_w, conv_b, w_q, w_k, w_v, gate_b, norm_g, skip, need_ctx):
    ucx, qx, kx, vx = ml_qkv(u_x, conv_w, conv_b, w_q, w_k, w_v)
    ucy, qy, ky, vy = ml_qkv(u_y, conv_w, conv_b, w_q, w_k, w_v)
    ifx, ffx, ibx, fbx = ml_gates(g_x, gate_b)
    ify, ffy, iby, fby = ml_gates(g_y, gate_b)
    B = u_y.shape[0]
    zero = (jnp.zeros((B, ML_H, ML_D, ML_D), jnp.float32), jnp.zeros((B, ML_H, ML_D), jnp.float32),
            jnp.zeros((B, ML_H), jnp.float32))
    rev = lambda a: jnp.flip(a, axis=2)
    hyf, st_f = mlstm_chunkwise(qy, ky, vy, ify, ffy, zero)
    hyb, st_b = mlstm_chunkwise(rev(qy), rev(ky), rev(vy), rev(iby), rev(fby), zero)
    hxf, _ = mlstm_chunkwise(qx, kx, vx, ifx, ffx, st_f)
    hxb, _ = mlstm_chunkwise(rev(qx), rev(kx), rev(vx), rev(ibx), rev(fbx), st_b)
    out_x = ml_out(hxf + rev(hxb), ucx, z_x, norm_g, skip)
    out_y = ml_out(hyf + rev(hyb), ucy, z_y, norm_g, skip) if need_ctx else None
    return out_x, out_y

def na_proj(a, g):
    B, L, _ = a.shape
    a = a.reshape(B, L, NA_H, NA_D)
    if g is not None:
        a = rmsnorm(a, g)
    return heads_first(a)

def na_latent(q, k, v, kc, vc, rpb):
    B, H, L, d = q.shape
    rows = L // GRID_W
    kh = min(WIN_R, rows)
    scale = d ** -0.5
    qg = q.reshape(B, H, rows, GRID_W, d)
    kg = k.reshape(B, H, rows, GRID_W, d)
    vg = v.reshape(B, H, rows, GRID_W, d)
    r = jnp.arange(rows)
    rs = jnp.clip(r - kh // 2, 0, rows - kh)
    ridx = rs[:, None] + jnp.arange(kh)[None, :]
    kb = kg[:, :, ridx]
    vb = vg[:, :, ridx]
    cq = jnp.arange(GRID_W)
    cs = jnp.clip(cq - WIN_C // 2, 0, GRID_W - WIN_C)
    col_ok = (cq[None, :] >= cs[:, None]) & (cq[None, :] < cs[:, None] + WIN_C)
    dr = ridx - r[:, None] + (WIN_R - 1)
    dc = jnp.clip(cq[None, :] - cq[:, None], -(WIN_C - 1), WIN_C - 1) + (WIN_C - 1)
    bias = rpb[:, dr[:, None, :, None], dc[None, :, None, :]].astype(jnp.float32)
    s_loc = jnp.einsum('bhrqd,bhrjkd->bhrqjk', qg, kb).astype(jnp.float32) * scale + bias[None]
    s_loc = jnp.where(col_ok[:, None, :], s_loc, -jnp.inf)
    s_ctx = jnp.einsum('bhrqd,bhcd->bhrqc', qg, kc).astype(jnp.float32) * scale
    nloc = kh * GRID_W
    s = jnp.concatenate([s_loc.reshape(B, H, rows, GRID_W, nloc), s_ctx], axis=-1)
    p = jax.nn.softmax(s, axis=-1)
    p_loc = p[..., :nloc].reshape(B, H, rows, GRID_W, kh, GRID_W).astype(v.dtype)
    p_ctx = p[..., nloc:].astype(v.dtype)
    o = jnp.einsum('bhrqjk,bhrjkd->bhrqd', p_loc, vb) + jnp.einsum('bhrqc,bhcd->bhrqd', p_ctx, vc)
    return o.reshape(B, H, L, d)

def moe(h, router_w, router_b, w1, w3, w2):
    B, L, D = h.shape
    t = h.reshape(-1, D)
    aff = jax.nn.sigmoid((t @ router_w).astype(jnp.float32))
    sel = aff + router_b.astype(jnp.float32)
    grp_score = jnp.sum(lax.top_k(sel.reshape(-1, N_GROUPS, EXPERTS_PER_GROUP), TOP_K)[0], axis=-1)
    best = jnp.argmax(grp_score, axis=-1)
    in_group = (jnp.arange(N_EXPERTS) // EXPERTS_PER_GROUP)[None, :] == best[:, None]
    _, idx = lax.top_k(jnp.where(in_group, sel, -jnp.inf), TOP_K)
    wsel = jnp.take_along_axis(aff, idx, axis=-1)
    wsel = wsel / jnp.sum(wsel, axis=-1, keepdims=True)
    gates = jnp.sum(jax.nn.one_hot(idx, N_EXPERTS, dtype=jnp.float32) * wsel[..., None], axis=1)
    a = jnp.einsum('nd,edf->nef', t, w1)
    b = jnp.einsum('nd,edf->nef', t, w3)
    hid = jax.nn.silu(a) * b * gates[..., None].astype(t.dtype)
    return jnp.einsum('nef,efd->nd', hid, w2).reshape(B, L, D)

def layer(x, y, mod_x, mod_y, rope, need_ctx,
          norm1_g, norm2_g, w_in, w_out,
          mla_qnorm_g, mla_w_uq, mla_kvnorm_g, mla_w_ukv, mla_q_g, mla_k_g,
          ml_conv_w, ml_conv_b, ml_w_q, ml_w_k, ml_w_v, ml_gate_b, ml_norm_g, ml_skip,
          na_q_g, na_k_g, na_rpb,
          router_w, router_b, moe_w1, moe_w3, moe_w2):
    sh1x, sc1x, g1x, sh2x, sc2x, g2x = [m[:, None, :] for m in jnp.split(mod_x, 6, axis=-1)]
    sh1y, sc1y, g1y, sh2y, sc2y, g2y = jnp.split(mod_y, 6, axis=-1)
    xn = rmsnorm(x, norm1_g) * (1 + sc1x) + sh1x
    yn = rmsnorm(y, norm1_g) * (1 + sc1y) + sh1y
    px = split_cols(xn @ w_in)
    py = split_cols(yn @ w_in)

    qx = mla_q(px[0], mla_qnorm_g, mla_w_uq, mla_q_g, rope)
    kx, vx = mla_kv(px[1], px[2], mla_kvnorm_g, mla_w_ukv, mla_k_g, rope)
    ky, vy = mla_kv(py[1], py[2], mla_kvnorm_g, mla_w_ukv, mla_k_g, None)
    mla_x = merge_heads(attend_blocks(qx, jnp.concatenate([kx, ky], axis=2), jnp.concatenate([vx, vy], axis=2)))

    ml_x, ml_y = mlstm_mixer(px[3], px[4], px[5], py[3], py[4], py[5],
                             ml_conv_w, ml_conv_b, ml_w_q, ml_w_k, ml_w_v, ml_gate_b, ml_norm_g, ml_skip, need_ctx)

    nkx, nvx = na_proj(px[7], na_k_g), na_proj(px[8], None)
    nky, nvy = na_proj(py[7], na_k_g), na_proj(py[8], None)
    na_x = merge_heads(na_latent(na_proj(px[6], na_q_g), nkx, nvx, nky, nvy, na_rpb))

    x = x + g1x * (jnp.concatenate([mla_x, ml_x, na_x], axis=-1) @ w_out)
    x = x + g2x * moe(rmsnorm(x, norm2_g) * (1 + sc2x) + sh2x, router_w, router_b, moe_w1, moe_w3, moe_w2)
    if not need_ctx:
        return x, None

    qy = mla_q(py[0], mla_qnorm_g, mla_w_uq, mla_q_g, None)
    mla_y = merge_heads(attend_blocks(qy, ky, vy))
    na_y = merge_heads(attend_blocks(na_proj(py[6], na_q_g), nky, nvy))
    y = y + g1y * (jnp.concatenate([mla_y, ml_y, na_y], axis=-1) @ w_out)
    y = y + g2y * moe(rmsnorm(y, norm2_g) * (1 + sc2y) + sh2y, router_w, router_b, moe_w1, moe_w3, moe_w2)
    return x, y

def setup_inputs(seed: int = 0) -> dict:
    key = jax.random.key(seed)
    ks = iter(list(jax.random.split(key, 48)))

    def nrm(shape, scale):
        return jax.random.normal(next(ks), shape, jnp.float32) * scale

    def gain(shape):
        return 1.0 + nrm(shape, 0.02)

    D = D_MODEL
    fb = jnp.linspace(3.0, 6.0, ML_H, dtype=jnp.float32)
    zh = jnp.zeros((ML_H,), jnp.float32)
    gate_base = jnp.concatenate([zh, fb, zh, fb])
    return {
        "x": nrm((BATCH, SEQ, D), 1.0),
        "c": nrm((BATCH, D), 1.0),
        "ctx": nrm((BATCH, CTX_LEN, D), 1.0),
        "c_ctx": nrm((D,), 1.0),
        "w_mod": nrm((DEPTH, D, 6 * D), 0.5 * D ** -0.5),
        "b_mod": nrm((DEPTH, 6 * D), 0.02),
        "norm1_g": gain((DEPTH, D)),
        "norm2_g": gain((DEPTH, D)),
        "w_in": nrm((DEPTH, D, N_IN), D ** -0.5),
        "w_out": nrm((DEPTH, D_MIX, D), D_MIX ** -0.5),
        "mla_qnorm_g": gain((DEPTH, Q_RANK)),
        "mla_w_uq": nrm((DEPTH, Q_RANK, MLA_H * QK_D), Q_RANK ** -0.5),
        "mla_kvnorm_g": gain((DEPTH, KV_RANK)),
        "mla_w_ukv": nrm((DEPTH, KV_RANK, MLA_H * (NOPE_D + V_D)), KV_RANK ** -0.5),
        "mla_q_g": gain((DEPTH, QK_D)),
        "mla_k_g": gain((DEPTH, QK_D)),
        "ml_conv_w": nrm((DEPTH, ML_CONV, ML_W), ML_CONV ** -0.5),
        "ml_conv_b": nrm((DEPTH, ML_W), 0.02),
        "ml_w_q": nrm((DEPTH, ML_H, ML_D, ML_D), ML_D ** -0.5),
        "ml_w_k": nrm((DEPTH, ML_H, ML_D, ML_D), ML_D ** -0.5),
        "ml_w_v": nrm((DEPTH, ML_H, ML_D, ML_D), ML_D ** -0.5),
        "ml_gate_b": gate_base[None, :] + nrm((DEPTH, 4 * ML_H), 0.1),
        "ml_norm_g": gain((DEPTH, ML_W)),
        "ml_skip": gain((DEPTH, ML_W)),
        "na_q_g": gain((DEPTH, NA_D)),
        "na_k_g": gain((DEPTH, NA_D)),
        "na_rpb": nrm((DEPTH, NA_H, 2 * WIN_R - 1, 2 * WIN_C - 1), 0.02),
        "router_w": nrm((D, N_EXPERTS), D ** -0.5),
        "router_b": nrm((N_EXPERTS,), 0.01),
        "moe_w1": nrm((DEPTH, N_EXPERTS, D, D_FF_EXPERT), D ** -0.5),
        "moe_w3": nrm((DEPTH, N_EXPERTS, D, D_FF_EXPERT), D ** -0.5),
        "moe_w2": nrm((DEPTH, N_EXPERTS, D_FF_EXPERT, D), D_FF_EXPERT ** -0.5),
    }

def reference(x, c, ctx, c_ctx, w_mod, b_mod, norm1_g, norm2_g, w_in, w_out,
              mla_qnorm_g, mla_w_uq, mla_kvnorm_g, mla_w_ukv, mla_q_g, mla_k_g,
              ml_conv_w, ml_conv_b, ml_w_q, ml_w_k, ml_w_v, ml_gate_b, ml_norm_g, ml_skip,
              na_q_g, na_k_g, na_rpb, router_w, router_b, moe_w1, moe_w3, moe_w2):
    rope = axial_rope_tables(x.shape[1], x.dtype)
    sc = jax.nn.silu(c)
    scc = jax.nn.silu(c_ctx)
    y = ctx
    for l in range(DEPTH):
        mod_x = sc @ w_mod[l] + b_mod[l]
        mod_y = scc @ w_mod[l] + b_mod[l]
        x, y = layer(x, y, mod_x, mod_y, rope, l < DEPTH - 1,
                     norm1_g[l], norm2_g[l], w_in[l], w_out[l],
                     mla_qnorm_g[l], mla_w_uq[l], mla_kvnorm_g[l], mla_w_ukv[l], mla_q_g[l], mla_k_g[l],
                     ml_conv_w[l], ml_conv_b[l], ml_w_q[l], ml_w_k[l], ml_w_v[l], ml_gate_b[l], ml_norm_g[l], ml_skip[l],
                     na_q_g[l], na_k_g[l], na_rpb[l],
                     router_w, router_b, moe_w1[l], moe_w3[l], moe_w2[l])
    return x


_drawn_inputs = setup_inputs


def setup_inputs(seed=0):
    import zlib

    import numpy as np

    out = dict(_drawn_inputs(seed))
    spreads = {}
    factors = {'mla_qnorm_g': 8.0,
     'mla_kvnorm_g': 8.0,
     'mla_q_g': 8.0,
     'mla_k_g': 8.0,
     'ml_conv_b': 3.69,
     'ml_norm_g': 8.0,
     'ml_skip': 6.163,
     'na_q_g': 8.0,
     'na_k_g': 8.0,
     'na_rpb': 64.0}
    for name, (base, spread) in spreads.items():
        noise = np.random.default_rng([zlib.crc32(name.encode()), seed]).standard_normal(out[name].shape)
        drawn = base * np.exp(spread * noise) if base else spread * noise
        out[name] = __import__('jax').numpy.asarray(drawn.astype(out[name].dtype))
    for name, factor in factors.items():
        out[name] = (out[name] * factor).astype(out[name].dtype)
    return out
```

```python
from contextlib import ExitStack

import numpy as np

import concourse.bass as bass
from concourse import mybir

F32 = mybir.dt.float32
ALU = mybir.AluOpType
ACT = mybir.ActivationFunctionType
AX = mybir.AxisListType

P = 128
D = 1024
KD = D // P
DEPTH = 2
L = 256
T = 4
TOK = T * P
EPS = 1e-6
Q_RANK, KV_RANK, ROPE_D, NOPE_D, V_D = 256, 128, 32, 64, 64
QK_D = NOPE_D + ROPE_D
MLA_H = 6
ML_H, ML_D = 4, 96
ML_W = ML_H * ML_D
NA_H, NA_D = 4, 64
NA_W = NA_H * NA_D
GRID = 64
WIN_R, WIN_C = 8, 16
ROWS = L // GRID
N_E, N_G, FF = 16, 4, 256
OFF_Q = 0
OFF_U = Q_RANK + KV_RANK + ROPE_D
OFF_Z = OFF_U + ML_W
OFF_G = OFF_Z + ML_W
OFF_NQ = OFF_G + 4 * ML_H
OFF_NK = OFF_NQ + NA_W
N_IN = OFF_NK + 2 * NA_W
NEG = -1e30
BIG = 1e30

PA, PG, PNQ, PNK, PNV = 0, OFF_U, OFF_U + 16, OFF_U + 16 + NA_W, OFF_U + 16 + 2 * NA_W
PW = OFF_U + 16 + 3 * NA_W
CHUNK = {"A": (OFF_Q, OFF_U, PA), "B": (OFF_G, 16 + NA_W, PG), "C": (OFF_NK, 2 * NA_W, PNK)}


def tiles_q(l):
    return [0, 1, 2, 3] if l < DEPTH - 1 else [2, 3]


def allowed(d, t, j):
    if t // 2 != j // 2:
        return t >= 2
    return j <= t if d == 0 else j >= t


def runs(l, d, j, diagonal):
    ts = [t for t in tiles_q(l) if allowed(d, t, j) and (diagonal or t != j)]
    out = []
    for t in ts:
        if out and out[-1][1] == t:
            out[-1][1] = t + 1
        else:
            out.append([t, t + 1])
    return out


def layer_of(s):
    return s[2] if s[0] in ("S", "PV", "OT") else s[1]


def p_cols(s):
    _, l, w, t = s
    c, n = CHUNK[w][2], CHUNK[w][1]
    if t not in tiles_q(l):
        if w == "A":
            return Q_RANK, n - Q_RANK
        if w == "B":
            return PG, 16
    return c, n


def keys_of(s):
    return TOK if s[3] >= 2 else L


def qkT_jobs(s):
    return [s + (w, i) for w in ("q", "k") if w == "k" or s[2] in tiles_q(s[1]) for i in (0, 1)]


PACK_DMAS = DEPTH * 9 + 2
PARAM_DMAS = DEPTH * 5 + 3
MODS = 12
MOD_FIRST = 4


def weight_pieces():
    out = []
    out += [("mod", 0, i) for i in range(MOD_FIRST)]
    for l in range(DEPTH):
        out += [("w_u", l), ("w_B", l), ("w_A", l), ("w_C", l), ("w_z", l)]
        out += late_mods(l)
        out += [("wo_mla", l), ("wo_ml", l), ("wo_na", l)]
        out += [("w13", l, e) for e in range(N_E)]
    return out


def late_mods(l):
    if l:
        return []
    return [("mod", 0, i) for i in range(MOD_FIRST, MODS)] + [("mod", m, i) for m in range(1, DEPTH)
                                                              for i in range(MODS)]


def spread(steps, fill):
    out, done = [], 0
    n = len(steps) - 8
    for i, st in enumerate(steps):
        out.append(st)
        if st[0] in ("mst", "mgrid") or st[0] == "mpv" and st[3] == 0:
            continue
        while done < len(fill) and (done + 1) * n <= (i + 1) * len(fill):
            out += fill[done]
            done += 1
    assert done == len(fill)
    return out


def make_schedule():
    s = []
    for l in range(DEPTH):
        tq = tiles_q(l)
        sq = sorted({t // 2 for t in tq})
        if l == 0:
            s += [(k, l, i) for i in range(MOD_FIRST) for k in ("mod", "modT")] + [("modfin", l, 1)]
        s += [("norm", l, 1, t) for t in range(T)]
        s += [("hT", l, 1, st, kp) for st in (0, 1) for kp in range(4)]
        s += [("pu", l, h) for h in range(ML_H)]
        s += [("pP", l, w, t) for w in "BAC" for t in range(T)]
        s += [("pz", l, h) for h in range(ML_H)]
        s += [("gates", l), ("rows", l), ("cols", l)]
        s += [("mv", l, t) for t in range(T)]
        s += [("conv", l, h) for h in range(ML_H)]
        s += [("mqk", l, h) for h in range(ML_H)]
        start = len(s)
        for h in range(ML_H):
            s += [("mst", l, h)]
            s += [("mgrid", l, h, d) for d in (0, 1)]
            s += [("mpv", l, h, d) for d in (0, 1)]
        s += [("mln", l)] + [("mlT", l, h) for h in range(ML_H)]
        s += [("cnorm", l, t) for t in range(T)]
        for t in range(T):
            s += [("cT", l, t), ("uqk", l, t), ("qkT", l, t)]
        s += [("nan", l, t) for t in range(T)] + [("nT", l, t) for t in range(T)]
        units = [u for u in UNITS if u[1] == l]
        for i, u in enumerate(units):
            s += [("S",) + u]
            if i >= 1:
                s += [("PV",) + units[i - 1]]
                if units[i - 1][4]:
                    s += [("OT",) + units[i - 1]]
        s += [("PV",) + units[-1], ("OT",) + units[-1]]
        late = late_mods(l)
        fill = [[p] + ([("modT",) + late[i - 1][1:]] if i else []) for i, p in enumerate(late)]
        if fill:
            fill[-1].append(("modT",) + late[-1][1:])
        s[start:] = spread(s[start:], fill)
        if l == 0:
            s += [("modfin", 0, 2)] + [("modfin", m, w) for m in range(1, DEPTH) for w in (1, 2)]
        s += [("gbc", l, 1, st) for st in sq]
        s += [("wo", l, t) for t in tq]
        s += [("norm", l, 2, t) for t in tq]
        s += [("hT", l, 2, st, kp) for st in sq for kp in range(4)]
        s += [("router", l), ("gbc2", l)]
        for e in range(N_E):
            for i, t in enumerate(tq):
                s += [("ab", l, e, t)]
                if i:
                    s += [("y", l, e, tq[i - 1])]
            s += [("y", l, e, tq[-1])]
        s += [("moe_out", l, t) for t in tq]
    return s


UNITS = [(b, l, t, h, h == nh - 1) for l in range(DEPTH) for b, nh in ((0, MLA_H), (1, NA_H))
         for t in tiles_q(l) for h in range(nh)]
UNIT_AT = {u: i for i, u in enumerate(UNITS)}


def build(nc, a):
    pieces = weight_pieces()
    piece_at = {p: i for i, p in enumerate(pieces)}
    SLOTS = 3
    schedule = make_schedule()

    RING = 6
    jobs = []
    last_job_of_piece = {}

    def add(key, piece=None):
        jobs.append(key)
        if piece is not None:
            last_job_of_piece[piece] = key

    for st in schedule:
        k, l = st[0], layer_of(st)
        if k == "mod":
            add(st, st)
        elif k == "modT":
            add(st)
        elif k == "hT":
            add(st)
        elif k == "pu":
            add(st, ("w_u", l))
        elif k == "pz":
            add(st, ("w_z", l))
        elif k == "pP":
            add(st, ("w_" + st[2], l))
        elif k in ("gates", "cols"):
            add(st)
        elif k == "mv":
            add(st)
        elif k == "mqk":
            add(st + ("q",))
            add(st + ("k",))
        elif k == "mst":
            for j in range(T):
                add(st + (j,))
        elif k == "mgrid":
            add(st)
        elif k == "mlT":
            add(st)
        elif k == "cT":
            add(st)
        elif k == "uqk":
            if st[2] in tiles_q(l):
                add(st + ("q", 0))
                add(st + ("q", 1))
            add(st + ("k", 0))
            add(st + ("k", 1))
        elif k == "qkT":
            if st[2] in tiles_q(l):
                add(st + ("q", 0))
                add(st + ("q", 1))
            add(st + ("k", 0))
            add(st + ("k", 1))
        elif k == "nT":
            add(st)
        elif k in ("S", "PV"):
            if k == "S":
                add(st)
            else:
                add(("ET",) + st[1:])
        elif k == "OT":
            add(st)
        elif k == "gbc":
            add(st + (0,))
            add(st + (1,))
        elif k == "wo":
            for n in (0, 1):
                add(st + (n,))
                for p in ("wo_mla", "wo_ml", "wo_na"):
                    last_job_of_piece[(p, l)] = st + (n,)
        elif k == "router":
            add(st)
        elif k == "gbc2":
            for s_ in sorted({t // 2 for t in tiles_q(l)}):
                add(st + (s_, 0))
                add(st + (s_, 1))
        elif k == "ab":
            add(st, ("w13", l, st[2]))
        elif k == "y":
            add(st + ("T",))
            add(st + (0,))
            add(st + (1,), ("w2", l, st[2]))
    job_at = {k: i for i, k in enumerate(jobs)}
    assert len(job_at) == len(jobs)
    acc_jobs = [st for st in schedule if st[0] == "mpv" or st[0] == "OT"]
    acc_at = {k: i for i, k in enumerate(acc_jobs)}
    pv_steps = [st for st in schedule if st[0] in ("mpv", "PV")]
    pv_at = {k: i + 1 for i, k in enumerate(pv_steps)}

    ctx = ExitStack()
    with ctx:
        def sb(name, cols, parts=P):
            return ctx.enter_context(nc.sbuf_tensor(name, [parts, cols], F32))

        def sem(name):
            return ctx.enter_context(nc.semaphore(name))

        bank = [ctx.enter_context(nc.psum_tensor(f"bank{i}", [P, 512], F32)) for i in range(8)]

        def view(reg, off, *shape, parts=P):
            n = int(np.prod(shape))
            ap = reg[0:parts, off:off + n]
            if len(shape) == 2:
                return ap.rearrange("p (a b) -> p a b", a=shape[0])
            if len(shape) == 3:
                return ap.rearrange("p (a b c) -> p a b c", a=shape[0], b=shape[1])
            return ap

        X = sb("X", T * D)
        Xv = view(X, 0, T, D)
        WORK = sb("WORK", 4096)
        XS = view(WORK, 0, T, D)
        H = sb("H", 4608)
        HT = view(H, 0, KD, TOK)
        MLAT = view(H, 0, 3, TOK)
        MLT = view(H, 1536, ML_H, TOK, parts=ML_D)
        NAT = view(H, 3584, 2, TOK)
        PR = sb("PROJ", T * PW)
        PRv = view(PR, 0, T, PW)
        M = sb("BRANCH", 9984)
        UT = view(M, 0, ML_H, TOK, parts=ML_D)
        MQ = UT
        ZS = view(M, 2048, ML_H, TOK, parts=ML_D)
        UC = view(M, 4096, ML_H, TOK, parts=ML_D)
        MK = view(M, 6144, ML_H, TOK, parts=ML_D)
        MV = view(M, 8192, T, ML_H, 97)
        CT = view(M, 0, 3, TOK)
        QTM = [view(M, 1536 + 576 * i, MLA_H, QK_D) for i in (0, 1)]
        KTM = [view(M, 2688 + 576 * i, MLA_H, QK_D) for i in (0, 1)]
        QT = view(M, 3840, MLA_H, TOK, parts=QK_D)
        KT = view(M, 6912, MLA_H, TOK, parts=QK_D)
        VV = PRv[:, :, 0:MLA_H * V_D].rearrange("p t (h e) -> p t h e", h=MLA_H)
        ACC = view(M, 0, T, D)
        GB = view(M, 4096, 2, D)
        HID = [view(M, 6144 + 256 * i, FF) for i in (0, 1)]
        HIDT = [view(M, 6656 + 256 * i, 2, P) for i in (0, 1)]
        TH = [view(M, 7168 + 256 * i, FF) for i in (0, 1)]
        YT = view(M, 7680, 512)
        N_R = sb("NA", 4096)
        HS = view(N_R, 0, T, ML_W)
        NQT = view(N_R, 0, 2, TOK)
        NKT = view(N_R, 1024, 2, TOK)
        BIAS = view(N_R, 2048, 2, NA_H, L)
        RINGW = sb("RINGW", SLOTS * 4096)
        W2R = sb("W2R", 2 * 2048)
        MROW = [W2R[0:2, 3072 + 512 * i:3584 + 512 * i] for i in (0, 1)]
        NEGMU = sb("NEGMU", 2 * TOK, ML_H)
        NEGMUv = view(NEGMU, 0, 2, TOK, parts=ML_H)
        ROW = view(WORK, 0, 4, TOK, parts=ML_H)
        GEM = view(WORK, 2048, 4, TOK, parts=ML_H)
        GRIDB = [view(WORK, 2048 * i, T, TOK) for i in (0, 1)]
        E = [view(WORK, 512 * i, TOK) for i in (0, 1)]
        PT = [view(WORK, 1024 + 512 * i, 4, P) for i in (0, 1)]
        OM = view(WORK, 2048, MLA_H * V_D)
        TMP = view(WORK, 2560, 1536)
        IDENT = sb("IDENT", P)
        PACK = M[:, 9984 - 3 * P:9984]
        COLS = sb("COLS", 3 * P)
        MODC = sb("MODC", DEPTH * 96)
        MODv = [view(MODC, 96 * l, 48, 2) for l in range(DEPTH)]
        AMOD = sb("AMOD", DEPTH * 32)
        AMv = [view(AMOD, 32 * l, 2, KD, 2) for l in range(DEPTH)]
        CS = sb("CS", 16)
        CSv = CS[:, :].rearrange("p (j k) -> p k j", j=2)
        TRI = sb("TRI", 2 * P)
        ROPE = sb("ROPE", 2 * 2 * ROPE_D + 16)
        RANK = ROPE[:, 2 * 2 * ROPE_D:]
        ROv = view(ROPE, 0, 2, 2, ROPE_D)
        BC = sb("BC", 2 * 352 + 16)
        GEMC = sb("GEMC", 4 * T * ML_H)
        GC = view(GEMC, 0, 4, T, ML_H)
        ST = sb("ST", 256)
        PAD = sb("PAD", 128, 56)
        RWT = sb("RWT", KD * N_E)
        RW = view(RWT, 0, KD, N_E)
        GATE = sb("GATE", T * N_E)
        GATEv = view(GATE, 0, T, N_E)
        RT = sb("RT", 448)
        assert nc.sbuf_bytes_remaining >= 0

        c2 = lambda r: COLS[:, P + r:P + r + 1]
        c96 = lambda r, n=1: COLS[0:ML_D, 2 * P + r:2 * P + r + n]
        bc_qg = lambda l: BC[:, 352 * l:352 * l + 96]
        bc_kg = lambda l: BC[:, 352 * l + 96:352 * l + 192]
        bc_nq = lambda l: BC[:, 352 * l + 192:352 * l + 256]
        bc_nk = lambda l: BC[:, 352 * l + 256:352 * l + 320]
        bc_gb = lambda l: BC[:, 352 * l + 320:352 * l + 336]
        bc_rb = BC[:, 704:720]

        SHIFT = 2 * GRID + 1
        BROW = GRID * SHIFT
        scratch = nc.dram_tensor("bias_rows", [2 * NA_H * 7, BROW], F32, kind="Internal").ap()

        full = [sem(f"bank_full_{i}") for i in range(RING)]
        free = [sem(f"bank_free_{i}") for i in range(RING)]
        slot_loaded = [sem(f"slot_loaded_{i}") for i in range(SLOTS)]
        w2_loaded = [sem(f"w2_loaded_{i}") for i in range(2)]
        pack_loaded = sem("pack_loaded")
        params_loaded = sem("params_loaded")
        small_loaded = sem("small_loaded")
        x_loaded = sem("x_loaded")
        pad_loaded = sem("pad_loaded")
        rows_stored = sem("rows_stored")
        bias_loaded = [sem(f"bias_loaded_{l}") for l in range(DEPTH)]
        bias_masked = sem("bias_masked")
        const_ready = sem("const_ready")
        pack_zero = sem("pack_zero")
        cols_full = sem("cols_full")
        cols_ready = sem("cols_ready")
        csilu_ready = sem("csilu_ready")
        mod_ready = sem("mod_ready")
        ssq_ready = sem("ssq_ready")
        mean_ready = sem("mean_ready")
        rstd_ready = sem("rstd_ready")
        xs_ready = sem("xs_ready")
        lf_ready = sem("lf_ready")
        lfa_ready = sem("lfa_ready")
        gates_ready = sem("gates_ready")
        rows_ready = sem("rows_ready")
        mv_ready = sem("mv_ready")
        conv_acc = sem("conv_acc")
        conv_tanh = sem("conv_tanh")
        uc_ready = sem("uc_ready")
        diag_ready = sem("diag_ready")
        grid_exp = sem("grid_exp")
        grid_ready = sem("grid_ready")
        pv_done = sem("pv_done")
        acc_free = sem("acc_free")
        hn_ready = sem("hn_ready")
        zs_tanh = sem("zs_tanh")
        cn_ready = sem("cn_ready")
        qk_ready = sem("qk_ready")
        na_ready = sem("na_ready")
        nmax_ready = sem("nmax_ready")
        exp_ready = sem("exp_ready")
        om_ready = sem("om_ready")
        resid_ready = sem("resid_ready")
        router_tanh = sem("router_tanh")
        gate_ready = sem("gate_ready")
        moe_tanh = sem("moe_tanh")
        hid_ready = sem("hid_ready")
        y_done = sem("y_done")
        out_ready = sem("out_ready")
        out_stored = sem("out_stored")
        em_in = sem("em_in")
        em_ready = sem("em_ready")
        gc_ready = sem("gc_ready")
        hn_used = sem("hn_used")
        mlt_ready = sem("mlt_ready")
        gate_filled = sem("gate_filled")
        gate_copied = sem("gate_copied")
        dve_step = sem("dve_step")
        act_step = sem("act_step")
        pool_step = sem("pool_step")

        block = ctx.enter_context(nc.Block())

        def bank_of(key):
            return bank[job_at[key] % RING]

        def full_of(key):
            n = job_at[key]
            return full[n % RING], n // RING + 1

        def free_of(key):
            n = job_at[key]
            return free[n % RING], n // RING + 1

        def slot(p):
            i = piece_at[p]
            return RINGW[:, 4096 * (i % SLOTS):4096 * (i % SLOTS + 1)]

        def loaded(p):
            i = piece_at[p]
            return slot_loaded[i % SLOTS], 16 * loads_upto[i]

        parts_of = {"w13": 2}
        loads_upto = []
        seen = [0] * SLOTS
        for i, p in enumerate(pieces):
            seen[i % SLOTS] += parts_of.get(p[0], 1)
            loads_upto.append(seen[i % SLOTS])

        def tick(eng, s):
            eng.sem_inc(s, 1)

        rstd_keys = []
        for s in schedule:
            if s[0] in ("norm", "mln", "cnorm"):
                rstd_keys.append(s)
            elif s[0] in ("uqk", "nan"):
                rstd_keys.append(s)
        rstd_at = {k: i + 1 for i, k in enumerate(rstd_keys)}
        ssq_keys = [s for s in schedule if s[0] in ("norm", "cnorm")]
        ssq_at = {k: i + 1 for i, k in enumerate(ssq_keys)}

        def order(kind):
            return {s: i + 1 for i, s in enumerate(x for x in schedule if x[0] == kind)}

        norm_n, mv_n, conv_n, mqk_n = order("norm"), order("mv"), order("conv"), order("mqk")
        grid_n, mlT_n, cn_n, uqk_n = order("mgrid"), order("mlT"), order("cnorm"), order("uqk")
        nan_n, wo_n, ab_n, y_n, pz_n = order("nan"), order("wo"), order("ab"), order("y"), order("pz")
        S_n, OT_n = order("S"), order("OT")
        mod_n, modfin_n = order("mod"), order("modfin")
        mod_key = {n: s for s, n in mod_n.items()}
        grid_key = {n: s for s, n in grid_n.items()}
        OT_key = {n: s for s, n in OT_n.items()}
        y_key = {n: s for s, n in y_n.items()}

        resid_at, c = {}, 0
        for s in schedule:
            if s[0] == "wo" or (s[0] == "moe_out" and s[1] < DEPTH - 1):
                c += 1
                resid_at[s] = c

        def resid_for(s):
            return resid_at[("wo", s[1], s[3])] if s[2] == 2 else resid_at[("moe_out", s[1] - 1, s[3])]

        def mpv_before(s):
            g = grid_key[grid_n[s] - 2]
            return pv_at[("mpv",) + g[1:]]

        def diagonal(s):
            t0 = tiles_q(s[1])[0]
            o = 2048 * (grid_n[s] % 2) + t0 * (TOK + P)
            b = WORK[:, o:o + P]
            return bass.AP(tensor=b.tensor, offset=b.offset,
                           ap=[list(b.ap[0]), [TOK + P, len(tiles_q(s[1]))], [1, P]])

        def conv_tmp(s):
            return WORK[0:ML_D, 512 * (s[2] % 2):512 * (s[2] % 2) + TOK]

        def ssq_cols(s):
            o = 176 + 2 * (ssq_at[s] % 4)
            return ST[:, o:o + 2]

        def neg_max(u):
            return ST[:, 192 + u % 4:193 + u % 4]

        def exp_sums(u, n):
            b, l, t, h, _ = UNITS[u]
            o = 200 + 8 * (OT_n[("OT", b, l, t, (MLA_H, NA_H)[b] - 1, True)] % 4) + h
            return ST[:, o:o + n]

        def stat(n, w=16):
            return ST[:, 16 * (n % 4):16 * (n % 4) + w], ST[:, 64 + 16 * (n % 4):64 + 16 * (n % 4) + w]

        POOL_HALF = RT[:, 432:448]

        def rstd_width(s):
            if s[0] == "norm":
                return 1
            if s[0] == "mln":
                return 4 * len(tiles_q(s[1]))
            if s[0] == "cnorm":
                return 2
            return 12 if s[0] == "uqk" else 8

        SMALL_PARTS = 5

        def small_views(l):
            s = W2R
            wq = s[0:ML_D, 0:384].rearrange("p (h e) -> p h e", h=ML_H)
            wk = s[0:ML_D, 384:768].rearrange("p (h e) -> p h e", h=ML_H)
            wv = s[0:ML_D, 768:1152].rearrange("p (h e) -> p h e", h=ML_H)
            uq = s[:, 1152:2304].rearrange("p (k n) -> p k n", k=2)
            ukv = s[:, 2304:3072]
            return wq, wk, wv, uq, ukv

        @block.sync
        def _(sp):
            sp.dma_start(Xv[:, 0:2, :], a["ctx"].rearrange("b (t p) d -> p (b t) d", p=P)).then_inc(x_loaded, 16)
            sp.dma_start(Xv[:, 2:4, :], a["x"].rearrange("b (t p) d -> p (b t) d", p=P)).then_inc(x_loaded, 16)
            w2_keys = [(l, e) for l in range(DEPTH) for e in range(N_E)]
            for i, p in enumerate(pieces):
                if p[0] == "w_z":
                    if p[1]:
                        for e in (N_E - 2, N_E - 1):
                            sp.wait_ge(*full_of(last_job_of_piece[("w2", p[1] - 1, e)]))
                    wq, wk, wv, uq, ukv = small_views(p[1])
                    for w, name in ((wq, "ml_w_q"), (wk, "ml_w_k"), (wv, "ml_w_v")):
                        sp.dma_start(w, a[name][p[1]].rearrange("h d e -> d h e")).then_inc(small_loaded, 16)
                    sp.dma_start(uq, a["mla_w_uq"][p[1]].rearrange("(k p) n -> p k n", p=P)).then_inc(
                        small_loaded, 16)
                    sp.dma_start(ukv, a["mla_w_ukv"][p[1]]).then_inc(small_loaded, 16)
                if i >= SLOTS:
                    s, v = full_of(last_job_of_piece[pieces[i - SLOTS]])
                    sp.wait_ge(s, v)
                dst, k, l = slot(p), p[0], p[1]
                done = slot_loaded[i % SLOTS]
                w_in = a["w_in"][l].rearrange("(k p) n -> p k n", p=P)
                if k == "mod":
                    c = 512 * p[2]
                    sp.dma_start(dst.rearrange("p (k n) -> p k n", k=KD),
                                 a["w_mod"][l].rearrange("(k p) n -> p k n", p=P)[:, :, c:c + 512]).then_inc(done, 16)
                elif k in ("w_u", "w_z", "w_A", "w_B", "w_C"):
                    c, n = {"w_u": (OFF_U, ML_W), "w_z": (OFF_Z, ML_W)}.get(k) or CHUNK[k[-1]][:2]
                    sp.dma_start(dst[:, 0:KD * n].rearrange("p (k n) -> p k n", k=KD),
                                 w_in[:, :, c:c + n]).then_inc(done, 16)
                elif k == "wo_mla":
                    sp.dma_start(dst[:, 0:3 * D].rearrange("p (k n) -> p k n", k=3),
                                 a["w_out"][l][0:384, :].rearrange("(k p) n -> p k n", p=P)).then_inc(done, 16)
                elif k == "wo_ml":
                    sp.dma_start(dst[0:ML_D, :].rearrange("p (k n) -> p k n", k=ML_H),
                                 a["w_out"][l][384:768, :].rearrange("(k p) n -> p k n", p=ML_D)).then_inc(done, 16)
                elif k == "wo_na":
                    sp.dma_start(dst[:, 0:2 * D].rearrange("p (k n) -> p k n", k=2),
                                 a["w_out"][l][768:1024, :].rearrange("(k p) n -> p k n", p=P)).then_inc(done, 16)
                else:
                    e = p[2]
                    w13 = dst.rearrange("p (k n) -> p k n", k=KD)
                    sp.dma_start(w13[:, :, 0:FF], a["moe_w1"][l, e].rearrange("(k p) f -> p k f", p=P)).then_inc(
                        done, 16)
                    sp.dma_start(w13[:, :, FF:2 * FF], a["moe_w3"][l, e].rearrange("(k p) f -> p k f", p=P)).then_inc(
                        done, 16)
                    n = w2_keys.index((l, e))
                    if e >= 2:
                        sp.wait_ge(*full_of(last_job_of_piece[("w2",) + w2_keys[n - 2]]))
                    elif e == 0:
                        sp.wait_ge(*full_of(("uqk", l, T - 1, "k", 1)))
                        for m in late_mods(l)[-2:]:
                            sp.wait_ge(*full_of(("modT",) + m[1:]))
                    sp.dma_start(W2R[:, 2048 * (n % 2):2048 * (n % 2 + 1)].rearrange("p (k n) -> p k n", k=2),
                                 a["moe_w2"][l, e].rearrange("(k p) n -> p k n", p=P)).then_inc(w2_loaded[n % 2], 16)
            for i in range(2):
                sp.wait_ge(out_ready, i + 1)
                sp.dma_start(a["out"][0, i * P:(i + 1) * P, :], Xv[:, 2 + i, :]).then_inc(out_stored, 16)
            sp.wait_ge(out_stored, 32)

        def w2_of(l, e):
            n = l * N_E + e
            return (W2R[:, 2048 * (n % 2):2048 * (n % 2 + 1)].rearrange("p (k n) -> p k n", k=2),
                    w2_loaded[n % 2], 16 * (n // 2 + 1))

        @block.gpsimd
        def _(pool):
            step = [0]

            def link(ins):
                step[0] += 1
                ins.then_inc(pool_step, 1)
                pool.wait_ge(pool_step, step[0])

            link(pool.memset(IDENT[:, :], 0.0))
            link(pool.affine_select(out=IDENT[:, :], in_=IDENT[:, :], compare_op=ALU.not_equal, fill=1.0, base=0,
                                    pattern=[[-1, P]], channel_multiplier=1))
            link(pool.memset(TRI[:, :], 0.0))
            link(pool.affine_select(out=TRI[:, 0:P], in_=TRI[:, 0:P], compare_op=ALU.is_ge, fill=NEG, base=0,
                                    pattern=[[1, P]], channel_multiplier=-1))
            link(pool.affine_select(out=TRI[:, P:2 * P], in_=TRI[:, P:2 * P], compare_op=ALU.is_ge, fill=NEG,
                                    base=0, pattern=[[-1, P]], channel_multiplier=1))
            link(pool.memset(POOL_HALF, -0.5))
            link(pool.memset(PAD[:, :], 0.0))
            pool.memset(PACK[:, :], 0.0).then_inc(const_ready, 1)
            pool.wait_ge(const_ready, 1)
            for l in range(DEPTH):
                for dst, name in ((bc_qg(l), "mla_q_g"), (bc_kg(l), "mla_k_g"), (bc_nq(l), "na_q_g"),
                                  (bc_nk(l), "na_k_g"), (bc_gb(l), "ml_gate_b")):
                    pool.dma_start(dst, a[name][l].partition_broadcast(P)).then_inc(params_loaded, 16)
            pool.dma_start(bc_rb, a["router_b"].partition_broadcast(P)).then_inc(params_loaded, 16)
            pool.dma_start(RW, a["router_w"].rearrange("(k p) n -> p k n", p=P)).then_inc(params_loaded, 16)
            pool.dma_start(ROPE[:, :], a["rope"]).then_inc(params_loaded, 16)
            lo = GRID - 1 - (WIN_C - 1)
            for l in range(DEPTH):
                for h in range(NA_H):
                    pool.dma_start(PAD[28 * l + 7 * h:28 * l + 7 * h + 7, lo:lo + 2 * WIN_C - 1],
                                   a["na_rpb"][l, h, WIN_R - ROWS:WIN_R + ROWS - 1, :]).then_inc(pad_loaded, 16)
            pool.wait_ge(pad_loaded, 16 * DEPTH * NA_H)
            pool.dma_start(scratch.rearrange("r (c i) -> r c i", i=SHIFT)[:, :, 0:2 * GRID - 1],
                           PAD[:, 0:2 * GRID - 1].unsqueeze(1).broadcast_to([2 * NA_H * 7, GRID, 2 * GRID - 1])
                           ).then_inc(rows_stored, 16)
            pool.wait_ge(rows_stored, 16)

            def load_bias(l):
                for r in range(ROWS):
                    for h in range(NA_H):
                        src = bass.AP(tensor=scratch.tensor,
                                      offset=(28 * l + 7 * h + ROWS - 1 - r) * BROW + GRID - 1,
                                      ap=[[2 * GRID, GRID], [BROW, ROWS], [1, GRID]])
                        q0 = (r % 2) * GRID
                        pool.dma_start(BIAS[q0:q0 + GRID, r // 2, h, :].rearrange("p (j c) -> p j c", j=ROWS),
                                       src).then_inc(bias_loaded[l], 16)
                pool.wait_ge(bias_loaded[l], 16 * ROWS * NA_H)
                for q0 in (0, GRID):
                    b = N_R[q0:q0 + GRID, 2048:4096].rearrange("p (m c) -> p m c", c=GRID)
                    lowc = GRID - WIN_C
                    link(pool.affine_select(out=b[:, :, 0:lowc], in_=b[:, :, 0:lowc], compare_op=ALU.is_ge, fill=NEG,
                                            base=WIN_C // 2, pattern=[[0, 32], [1, lowc]], channel_multiplier=-1))
                    ins = pool.affine_select(out=b[:, :, WIN_C:], in_=b[:, :, WIN_C:], compare_op=ALU.is_ge,
                                             fill=NEG, base=WIN_C // 2 - 1 - WIN_C,
                                             pattern=[[0, 32], [-1, lowc]], channel_multiplier=1)
                    ins.then_inc(bias_masked, 1)
                    pool.wait_ge(bias_masked, 2 * l + (1 if q0 == 0 else 2))

            for s in schedule:
                if s in rstd_at:
                    m, r = stat(rstd_at[s])
                    w = rstd_width(s)
                    pool.wait_ge(mean_ready, rstd_at[s])
                    pool.tensor_tensor(r[:, 0:w], m[:, 0:w], POOL_HALF[:, 0:w], ALU.pow).then_inc(rstd_ready, 1)
                if s == ("gates", 0):
                    load_bias(0)
                if s == ("gbc", 0, 1, 1):
                    pool.wait_ge(nmax_ready, max(UNIT_AT[u] for u in UNITS if u[1] == 0) + 1)
                    load_bias(1)

        @block.scalar
        def _(act):
            step = [0]

            def link(ins):
                step[0] += 1
                ins.then_inc(act_step, 1)
                act.wait_ge(act_step, step[0])

            act.wait_ge(const_ready, 1)

            def pack(r0, r1, c, n, src):
                act.dma_start(PACK[r0:r1, c:c + n], src).then_inc(pack_loaded, 16)

            pack(0, 8, P, P, a["c_ctx"].rearrange("(r p) -> r p", p=P))
            pack(8, 16, P, P, a["c"][0].rearrange("(r p) -> r p", p=P))
            for l in range(DEPTH):
                r = 64 * l
                pack(r, r + 48, 0, P, a["b_mod"][l].rearrange("(r p) -> r p", p=P))
                pack(r + 48, r + 56, 0, P, a["norm1_g"][l].rearrange("(r p) -> r p", p=P))
                pack(r + 56, r + 64, 0, P, a["norm2_g"][l].rearrange("(r p) -> r p", p=P))
                pack(16 + 3 * l, 18 + 3 * l, P, P, a["mla_qnorm_g"][l].rearrange("(r p) -> r p", p=P))
                pack(18 + 3 * l, 19 + 3 * l, P, P, a["mla_kvnorm_g"][l:l + 1, :])
                q = 24 * l
                for o, name in ((0, "ml_norm_g"), (4, "ml_skip"), (8, "ml_conv_b")):
                    pack(q + o, q + o + 4, 2 * P, ML_D, a[name][l].rearrange("(r p) -> r p", p=ML_D))
                pack(q + 12, q + 24, 2 * P, ML_D, a["ml_conv_w"][l].rearrange("k (r p) -> (k r) p", p=ML_D))
            act.wait_ge(cols_ready, 1)
            act.activation(RT[:, 0:16], COLS[:, P:P + 16], ACT.Tanh, scale=0.5).then_inc(csilu_ready, 1)
            for s in schedule:
                k, l = s[0], layer_of(s)
                if k == "mod":
                    n = mod_n[s]
                    act.wait_ge(*full_of(s))
                    if n > 2:
                        act.wait_ge(*full_of(("modT",) + mod_key[n - 2][1:]))
                    act.activation(MROW[n % 2], bank_of(s)[0:2, :], ACT.Copy).then_inc(free_of(s)[0], 1)
                elif k == "norm":
                    t = s[3]
                    if (l, s[2]) == (0, 1):
                        act.wait_ge(x_loaded, 32)
                    else:
                        act.wait_ge(resid_ready, resid_for(s))
                    if ssq_at[s] > 4:
                        act.wait_ge(mean_ready, rstd_at[ssq_keys[ssq_at[s] - 5]])
                    m = ssq_cols(s)
                    act.activation(XS[:, t, :], Xv[:, t, :], ACT.Square, accum_out=m[:, 0:1]).then_inc(ssq_ready, 1)
                elif k == "hT" and s[4] % 2:
                    _, _, w, st, kp = s
                    act.wait_ge(*full_of(s))
                    act.wait_ge(mod_ready, modfin_n[("modfin", l, w)])
                    for i in (0, 1):
                        kk = 2 * kp + i
                        ins = act.activation(HT[:, kk, st * L:(st + 1) * L], bank_of(s)[:, i * L:(i + 1) * L],
                                             ACT.Identity, scale=AMv[l][:, w - 1, kk, st:st + 1],
                                             bias=MODv[l][:, 24 * (w - 1) + kk, st:st + 1])
                    ins.then_inc(free_of(s)[0], 1)
                elif k == "pu" and s[2] % 2:
                    act.wait_ge(*full_of(s))
                    act.activation(UT[:, s[2], :], bank_of(s)[0:ML_D, :], ACT.Copy).then_inc(free_of(s)[0], 1)
                elif k == "pP" and s[3] % 2:
                    act.wait_ge(*full_of(s))
                    c, n = p_cols(s)
                    act.activation(PRv[:, s[3], c:c + n], bank_of(s)[:, 0:n], ACT.Copy).then_inc(free_of(s)[0], 1)
                elif k == "pz":
                    act.wait_ge(*full_of(s))
                    c0 = 0 if l < DEPTH - 1 else L
                    act.activation(ZS[:, s[2], c0:TOK], bank_of(s)[0:ML_D, c0:TOK], ACT.Tanh, scale=0.5).then_inc(
                        zs_tanh, 1)
                elif k == "rows":
                    act.wait_ge(lfa_ready, l + 1)
                    fa = GEM[:, 0:2, :]
                    link(act.activation(fa, fa, ACT.Exp, scale=-1.0))
                    act.activation(fa, fa, ACT.Ln, bias=1.0).then_inc(lf_ready, 1)
                    act.wait_ge(em_in, l + 1)
                    act.activation(GEM[:, 2:4, :], GEM[:, 2:4, :], ACT.Exp, scale=-1.0).then_inc(em_ready, 1)
                elif k == "mv" and s[2] % 2:
                    act.wait_ge(*full_of(s))
                    act.activation(MV[:, s[2], :, 0:ML_D],
                                   bank_of(s)[:, 0:ML_W].rearrange("p (h e) -> p h e", h=ML_H),
                                   ACT.Copy).then_inc(free_of(s)[0], 1)
                elif k == "conv":
                    act.wait_ge(conv_acc, conv_n[s])
                    act.activation(conv_tmp(s), UC[:, s[2], :], ACT.Tanh).then_inc(conv_tanh, 1)
                elif k == "mqk":
                    key = s + ("k",)
                    act.wait_ge(*full_of(key))
                    act.activation(MK[:, s[2], :], bank_of(key)[0:ML_D, :], ACT.Copy,
                                   scale=ML_D ** -0.5).then_inc(free_of(key)[0], 1)
                elif k == "mgrid":
                    _, _, h, d = s
                    g = GRIDB[grid_n[s] % 2]
                    mu = bank_of(s)
                    act.wait_ge(*full_of(s))
                    if grid_n[s] > 2:
                        act.wait_ge(pv_done, mpv_before(s))
                    act.wait_ge(diag_ready, grid_n[s])
                    act.wait_ge(gc_ready, l + 1)
                    for j in range(T):
                        for t0, t1 in runs(l, d, j, False):
                            act.activation(g[:, j, t0 * P:t1 * P], mu[:, t0 * P:t1 * P], ACT.Exp,
                                           bias=GC[:, d, j, h:h + 1])
                    act.activation(diagonal(s), diagonal(s), ACT.Exp).then_inc(grid_exp, 1)
                elif k == "cnorm":
                    t = s[2]
                    m = ssq_cols(s)
                    act.wait_ge(*free_of(("pP", l, "A", t)))
                    if s[2] == 0:
                        act.wait_ge(hn_used, l + 1)
                    act.wait_ge(mean_ready, rstd_at[ssq_keys[ssq_at[s] - 5]])
                    act.wait_ge(ssq_ready, ssq_at[s] - 1)
                    if t in tiles_q(l):
                        link(act.activation(TMP[:, 0:Q_RANK], PRv[:, t, 0:Q_RANK], ACT.Square,
                                            accum_out=m[:, 0:1]))
                    act.activation(TMP[:, Q_RANK:384], PRv[:, t, Q_RANK:384], ACT.Square,
                                   accum_out=m[:, 1:2]).then_inc(ssq_ready, 1)
                elif k == "qkT":
                    for key in qkT_jobs(s):
                        if key[3] == "k":
                            act.wait_ge(*full_of(key))
                            hh = 3 * key[4]
                            act.activation(KT[:, hh:hh + 3, s[2] * P:(s[2] + 1) * P],
                                           bank_of(key)[0:QK_D, 0:384].rearrange("p (h t) -> p h t", h=3),
                                           ACT.Copy).then_inc(free_of(key)[0], 1)
                elif k == "S":
                    u = UNIT_AT[s[1:]]
                    nk = keys_of(s)
                    act.wait_ge(nmax_ready, u + 1)
                    if u >= 2:
                        act.wait_ge(*full_of(("ET",) + UNITS[u - 2]))
                    act.activation(E[u % 2][:, 0:nk], bank_of(s)[:, 0:nk], ACT.Exp, bias=neg_max(u),
                                   accum_out=exp_sums(u, 1)).then_inc(free_of(s)[0], 1)
                elif k == "router":
                    act.wait_ge(*full_of(s))
                    nt = len(tiles_q(l))
                    act.activation(RT[:, 0:16 * nt], bank_of(s)[:, 0:16 * nt], ACT.Tanh, scale=0.5).then_inc(
                        free_of(s)[0], 1)
                elif k == "gbc":
                    for i in (0, 1):
                        act.wait_ge(*full_of(s + (i,)))
                        act.activation(GB[:, s[3], 512 * i:512 * i + 512], bank_of(s + (i,))[:, :],
                                       ACT.Copy).then_inc(free_of(s + (i,))[0], 1)
                elif k == "gbc2":
                    act.wait_ge(resid_ready, resid_at[("wo", l, tiles_q(l)[-1])])
                    for st in sorted({t // 2 for t in tiles_q(l)}):
                        for i in (0, 1):
                            key = s + (st, i)
                            act.wait_ge(*full_of(key))
                            act.activation(GB[:, st, 512 * i:512 * i + 512], bank_of(key)[:, :],
                                           ACT.Copy).then_inc(free_of(key)[0], 1)
                elif k == "ab":
                    act.wait_ge(*full_of(s))
                    n = ab_n[s]
                    if n > 2:
                        act.wait_ge(hid_ready, n - 2)
                    act.activation(TH[n % 2], bank_of(s)[:, 0:FF], ACT.Tanh, scale=0.5).then_inc(moe_tanh, 1)
                elif k == "y":
                    key = s + ("T",)
                    n = y_n[s]
                    act.wait_ge(*full_of(key))
                    if n > 2:
                        act.wait_ge(*full_of(y_key[n - 2] + (1,)))
                    act.activation(HIDT[n % 2].rearrange("p k t -> p (k t)"), bank_of(key)[:, 0:FF],
                                   ACT.Copy).then_inc(free_of(key)[0], 1)

        @block.tensor
        def _(pe):
            def open_bank(key):
                n = job_at[key]
                if n >= RING:
                    pe.wait_ge(free[n % RING], n // RING)

            def flip(out, in_):
                k = in_.shape[0]
                return pe.transpose(out, in_, IDENT[0:k, 0:k])

            def open_acc(key):
                n = acc_at[key]
                if n >= 2:
                    pe.wait_ge(acc_free, n - 1)
                return bank[6 + n % 2]

            pe.wait_ge(pack_loaded, 16 * PACK_DMAS)
            pe.wait_ge(const_ready, 1)
            for i in range(3):
                ins = flip(bank[6][:, i * P:(i + 1) * P], PACK[:, i * P:(i + 1) * P])
            ins.then_inc(cols_full, 1)
            pe.wait_ge(csilu_ready, 2)
            for s in schedule:
                k, l = s[0], layer_of(s)
                tq = tiles_q(l)
                c0 = 0 if l < DEPTH - 1 else L
                if k == "mod":
                    open_bank(s)
                    pe.wait_ge(*loaded(s))
                    w = slot(s).rearrange("p (k n) -> p k n", k=KD)
                    for kk in range(KD):
                        ins = pe.matmul(bank_of(s)[0:2, :], CSv[:, kk, :], w[:, kk, :], start=kk == 0,
                                        stop=kk == KD - 1)
                    ins.then_inc(full_of(s)[0], 1)
                elif k == "modT":
                    key = ("mod",) + s[1:]
                    open_bank(s)
                    pe.wait_ge(*free_of(key))
                    for c in range(4):
                        ins = flip(bank_of(s)[:, 2 * c:2 * c + 2], MROW[mod_n[key] % 2][:, c * P:(c + 1) * P])
                    ins.then_inc(full_of(s)[0], 1)
                elif k == "hT":
                    _, _, w, st, kp = s
                    open_bank(s)
                    pe.wait_ge(xs_ready, norm_n[("norm", l, w, 2 * st + 1)])
                    for i in (0, 1):
                        for tt in (0, 1):
                            kk = 2 * kp + i
                            ins = flip(bank_of(s)[:, i * L + tt * P:i * L + (tt + 1) * P],
                                       XS[:, 2 * st + tt, kk * P:(kk + 1) * P])
                    ins.then_inc(full_of(s)[0], 1)
                elif k in ("pu", "pz"):
                    open_bank(s)
                    piece = ("w_" + k[1], l)
                    pe.wait_ge(*loaded(piece))
                    if k == "pu" and s[2] == 0:
                        for st in (0, 1):
                            for kp in range(4):
                                pe.wait_ge(*free_of(("hT", l, 1, st, kp)))
                    w = slot(piece)[:, 0:KD * ML_W].rearrange("p (k n) -> p k n", k=KD)
                    b0 = 0 if k == "pu" else c0
                    for kk in range(KD):
                        ins = pe.matmul(bank_of(s)[0:ML_D, b0:TOK], w[:, kk, s[2] * ML_D:(s[2] + 1) * ML_D],
                                        HT[:, kk, b0:TOK], start=kk == 0, stop=kk == KD - 1)
                    ins.then_inc(full_of(s)[0], 1)
                elif k == "pP":
                    _, _, w, t = s
                    open_bank(s)
                    pe.wait_ge(*loaded(("w_" + w, l)))
                    n = CHUNK[w][1]
                    wv = slot(("w_" + w, l))[:, 0:KD * n].rearrange("p (k n) -> p k n", k=KD)
                    c, nn = p_cols(s)
                    off = c - CHUNK[w][2]
                    for kk in range(KD):
                        ins = pe.matmul(bank_of(s)[:, 0:nn], HT[:, kk, t * P:(t + 1) * P], wv[:, kk, off:off + nn],
                                        start=kk == 0, stop=kk == KD - 1)
                    ins.then_inc(full_of(s)[0], 1)
                elif k == "gates":
                    open_bank(s)
                    pe.wait_ge(gates_ready, l + 1)
                    for t in range(T):
                        if t:
                            pe.wait_ge(gate_copied, 3 * l + t)
                        for q in range(4):
                            ins = flip(bank_of(s)[0:ML_H, q * P:(q + 1) * P], PRv[:, t, PG + 4 * q:PG + 4 * q + 4])
                        ins.then_inc(gate_filled if t < T - 1 else full_of(s)[0], 1)
                elif k == "cols":
                    open_bank(s)
                    pe.wait_ge(rows_ready, l + 1)
                    for q in range(4):
                        for t in range(T):
                            o = (q * T + t) * ML_H
                            ins = flip(bank_of(s)[:, o:o + ML_H], GEM[:, q, t * P:(t + 1) * P])
                    ins.then_inc(full_of(s)[0], 1)
                elif k == "mv":
                    t = s[2]
                    open_bank(s)
                    pe.wait_ge(small_loaded, 16 * SMALL_PARTS * (l + 1))
                    if t == 0:
                        for h in range(ML_H):
                            pe.wait_ge(*free_of(("pu", l, h)))
                    wv = small_views(l)[2]
                    for h in range(ML_H):
                        ins = pe.matmul(bank_of(s)[:, h * ML_D:(h + 1) * ML_D], UT[:, h, t * P:(t + 1) * P],
                                        wv[:, h, :], start=True, stop=True)
                    ins.then_inc(full_of(s)[0], 1)
                elif k == "mqk":
                    h = s[2]
                    wq, wk = small_views(l)[0:2]
                    pe.wait_ge(uc_ready, conv_n[("conv", l, h)])
                    open_bank(s + ("q",))
                    pe.matmul(bank_of(s + ("q",))[0:ML_D, c0:TOK], wq[:, h, :], UC[:, h, c0:TOK], start=True,
                              stop=True).then_inc(full_of(s + ("q",))[0], 1)
                    open_bank(s + ("k",))
                    pe.matmul(bank_of(s + ("k",))[0:ML_D, :], wk[:, h, :], UC[:, h, :], start=True,
                              stop=True).then_inc(full_of(s + ("k",))[0], 1)
                elif k == "mst":
                    h = s[2]
                    pe.wait_ge(*free_of(("mqk", l, h, "q")))
                    pe.wait_ge(*free_of(("mqk", l, h, "k")))
                    for j in range(T):
                        q0 = c0 if j < 2 else L
                        open_bank(s + (j,))
                        pe.matmul(bank_of(s + (j,))[:, q0:TOK], MK[:, h, j * P:(j + 1) * P], MQ[:, h, q0:TOK],
                                  start=True, stop=True).then_inc(full_of(s + (j,))[0], 1)
                elif k == "mgrid":
                    open_bank(s)
                    pe.wait_ge(rows_ready, l + 1)
                    pe.matmul(bank_of(s)[:, c0:TOK], IDENT[0:ML_H, s[2]:s[2] + 1].broadcast_to([ML_H, P]), NEGMUv[:, s[3], c0:TOK], start=True,
                              stop=True).then_inc(full_of(s)[0], 1)
                elif k == "mpv":
                    _, _, h, d = s
                    acc = open_acc(s)
                    pe.wait_ge(grid_ready, grid_n[("mgrid", l, h, d)])
                    if h == 0 and d == 0:
                        for t in range(T):
                            pe.wait_ge(*free_of(("mv", l, t)))
                        pe.wait_ge(mv_ready, l + 1)
                    g = GRIDB[grid_n[("mgrid", l, h, d)] % 2]
                    for t in tq:
                        js = [j for j in range(T) if allowed(d, t, j)]
                        for j in js:
                            ins = pe.matmul(acc[:, t * 97:t * 97 + 97], g[:, j, t * P:(t + 1) * P],
                                            MV[:, j, h, :], start=j == js[0], stop=j == js[-1])
                    ins.then_inc(pv_done, 1)
                elif k == "mlT":
                    h = s[2]
                    open_bank(s)
                    pe.wait_ge(hn_ready, l + 1)
                    for t in tq:
                        ins = flip(bank_of(s)[0:ML_D, t * P:(t + 1) * P], HS[:, t, h * ML_D:(h + 1) * ML_D])
                    ins.then_inc(full_of(s)[0], 1)
                elif k == "cT":
                    t = s[2]
                    open_bank(s)
                    pe.wait_ge(cn_ready, cn_n[("cnorm", l, t)])
                    for c in range(0 if t in tq else 2, 3):
                        ins = flip(bank_of(s)[:, c * P:(c + 1) * P], PRv[:, t, c * P:(c + 1) * P])
                    ins.then_inc(full_of(s)[0], 1)
                elif k == "uqk":
                    t = s[2]
                    uq, ukv = small_views(l)[3:5]
                    pe.wait_ge(*free_of(("cT", l, t)))
                    if t in tq:
                        for i in (0, 1):
                            key = s + ("q", i)
                            open_bank(key)
                            for kk in (0, 1):
                                ins = pe.matmul(bank_of(key)[:, 0:288], CT[:, kk, t * P:(t + 1) * P],
                                                uq[:, kk, 288 * i:288 * i + 288], start=kk == 0, stop=kk == 1)
                            ins.then_inc(full_of(key)[0], 1)
                    for i in (0, 1):
                        key = s + ("k", i)
                        open_bank(key)
                        pe.matmul(bank_of(key)[:, 0:384], CT[:, 2, t * P:(t + 1) * P],
                                  ukv[:, 384 * i:384 * i + 384], start=True, stop=True).then_inc(full_of(key)[0], 1)
                elif k == "qkT":
                    t = s[2]
                    pe.wait_ge(qk_ready, uqk_n[("uqk", l, t)])
                    for key in qkT_jobs(s):
                        src = (QTM if key[3] == "q" else KTM)[t % 2]
                        open_bank(key)
                        for i in range(3):
                            ins = flip(bank_of(key)[0:QK_D, i * P:(i + 1) * P], src[:, 3 * key[4] + i, :])
                        ins.then_inc(full_of(key)[0], 1)
                elif k == "nT":
                    t = s[2]
                    open_bank(s)
                    pe.wait_ge(na_ready, nan_n[("nan", l, t)])
                    for i in range(0 if t in tq else 2, 4):
                        ins = flip(bank_of(s)[:, i * P:(i + 1) * P], PRv[:, t, PNQ + i * P:PNQ + (i + 1) * P])
                    ins.then_inc(full_of(s)[0], 1)
                elif k == "S":
                    _, b, _, t, h, _ = s
                    open_bank(s)
                    nk = keys_of(s)
                    if h == 0 and t == tq[0]:
                        for tt in range(T):
                            if b == 0:
                                for key in qkT_jobs(("qkT", l, tt)):
                                    pe.wait_ge(*free_of(key))
                            else:
                                pe.wait_ge(*free_of(("nT", l, tt)))
                    if b == 0:
                        q, kk = QT[:, h, t * P:(t + 1) * P], KT[:, h, 0:nk]
                    else:
                        r = (h % 2) * NA_D
                        q = NQT[r:r + NA_D, h // 2, t * P:(t + 1) * P]
                        kk = NKT[r:r + NA_D, h // 2, 0:nk]
                    pe.matmul(bank_of(s)[:, 0:nk], q, kk, start=True, stop=True).then_inc(full_of(s)[0], 1)
                elif k == "PV":
                    u = UNIT_AT[s[1:]]
                    _, b, _, t, h, lasth = s
                    nkt = keys_of(s) // P
                    key = ("ET",) + s[1:]
                    open_bank(key)
                    pe.wait_ge(*free_of(("S",) + s[1:]))
                    for i in range(nkt):
                        ins = flip(bank_of(key)[:, i * P:(i + 1) * P], E[u % 2][:, i * P:(i + 1) * P])
                    ins.then_inc(full_of(key)[0], 1)
                    akey = ("OT", b, l, t, (MLA_H, NA_H)[b] - 1, True)
                    acc = bank[6 + acc_at[akey] % 2]
                    if h == 0:
                        open_acc(akey)
                    pe.wait_ge(*free_of(key))
                    for i in range(nkt):
                        v = VV[:, i, h, :] if b == 0 else PRv[:, i, PNV + h * NA_D:PNV + (h + 1) * NA_D]
                        ins = pe.matmul(acc[:, h * 64:h * 64 + 64], PT[u % 2][:, i, :], v, start=i == 0,
                                        stop=i == nkt - 1)
                    ins.then_inc(pv_done, 1)
                elif k == "OT":
                    _, b, _, t, h, _ = s
                    open_bank(s)
                    pe.wait_ge(om_ready, OT_n[s])
                    for i in range((3, 2)[b]):
                        ins = flip(bank_of(s)[:, i * P:(i + 1) * P], OM[:, i * P:(i + 1) * P])
                    ins.then_inc(full_of(s)[0], 1)
                elif k == "gbc" or k == "gbc2":
                    keys = [s + (i,) for i in (0, 1)] if k == "gbc" else [
                        s + (st, i) for st in sorted({t // 2 for t in tq}) for i in (0, 1)]
                    v = 16 if k == "gbc" else 40
                    for i in (v // 4, v // 4 + 1):
                        pe.wait_ge(*free_of(("modT", l, i)))
                    for key in keys:
                        st = key[3] if k == "gbc" else key[2]
                        i = key[-1]
                        open_bank(key)
                        for c in range(4):
                            col = MODv[l][:, v + 4 * i + c, st:st + 1].broadcast_to([P, P])
                            ins = pe.matmul(bank_of(key)[:, c * P:(c + 1) * P], col, IDENT[:, :], start=True,
                                            stop=True, is_transpose=True)
                        ins.then_inc(full_of(key)[0], 1)
                elif k == "wo":
                    t = s[2]
                    if t == tq[0]:
                        for p in ("wo_mla", "wo_ml", "wo_na"):
                            pe.wait_ge(*loaded((p, l)))
                        pe.wait_ge(mlt_ready, ML_H * (l + 1))
                        for u in schedule:
                            if u[0] == "OT" and u[2] == l:
                                pe.wait_ge(*free_of(u))
                    wm = slot(("wo_mla", l))[:, 0:3 * D].rearrange("p (k n) -> p k n", k=3)
                    wl = slot(("wo_ml", l))[0:ML_D, :].rearrange("p (k n) -> p k n", k=ML_H)
                    wn = slot(("wo_na", l))[:, 0:2 * D].rearrange("p (k n) -> p k n", k=2)
                    terms = [(MLAT, wm, i) for i in range(3)] + [(MLT, wl, i) for i in range(4)] + [
                        (NAT, wn, i) for i in range(2)]
                    for n in (0, 1):
                        open_bank(s + (n,))
                        for i, (m, w, c) in enumerate(terms):
                            ins = pe.matmul(bank_of(s + (n,))[:, :], m[:, c, t * P:(t + 1) * P],
                                            w[:, c, 512 * n:512 * n + 512], start=i == 0, stop=i == len(terms) - 1)
                        ins.then_inc(full_of(s + (n,))[0], 1)
                elif k == "router":
                    open_bank(s)
                    for st in sorted({t // 2 for t in tq}):
                        for kp in range(4):
                            pe.wait_ge(*free_of(("hT", l, 2, st, kp)))
                    for i, t in enumerate(tq):
                        for kk in range(KD):
                            ins = pe.matmul(bank_of(s)[:, 16 * i:16 * i + 16], HT[:, kk, t * P:(t + 1) * P],
                                            RW[:, kk, :], start=kk == 0, stop=kk == KD - 1)
                    ins.then_inc(full_of(s)[0], 1)
                elif k == "ab":
                    _, _, e, t = s
                    open_bank(s)
                    pe.wait_ge(*loaded(("w13", l, e)))
                    w = slot(("w13", l, e)).rearrange("p (k n) -> p k n", k=KD)
                    for kk in range(KD):
                        ins = pe.matmul(bank_of(s)[:, :], HT[:, kk, t * P:(t + 1) * P], w[:, kk, :],
                                        start=kk == 0, stop=kk == KD - 1)
                    ins.then_inc(full_of(s)[0], 1)
                elif k == "y":
                    _, _, e, t = s
                    n = y_n[s]
                    key = s + ("T",)
                    open_bank(key)
                    pe.wait_ge(hid_ready, n)
                    for i in (0, 1):
                        ins = flip(bank_of(key)[:, i * P:(i + 1) * P], HID[n % 2][:, i * P:(i + 1) * P])
                    ins.then_inc(full_of(key)[0], 1)
                    w2, sm, v = w2_of(l, e)
                    pe.wait_ge(sm, v)
                    pe.wait_ge(*free_of(key))
                    for nn in (0, 1):
                        open_bank(s + (nn,))
                        for i in (0, 1):
                            ins = pe.matmul(bank_of(s + (nn,))[:, :], HIDT[n % 2][:, i, :],
                                            w2[:, i, 512 * nn:512 * nn + 512], start=i == 0, stop=i == 1)
                        ins.then_inc(full_of(s + (nn,))[0], 1)

        @block.vector
        def _(dve):
            step = [0]

            def link(ins):
                step[0] += 1
                ins.then_inc(dve_step, 1)
                dve.wait_ge(dve_step, step[0])

            dve.wait_ge(cols_full, 1)
            dve.tensor_copy(COLS[:, :], bank[6][:, 0:3 * P]).then_inc(cols_ready, 1)
            dve.wait_ge(cols_ready, 1)
            dve.wait_ge(params_loaded, 16 * PARAM_DMAS)
            for l in range(DEPTH):
                q = 2 * P + 24 * l
                link(dve.tensor_scalar(COLS[0:ML_D, q + 8:q + 24], COLS[0:ML_D, q + 8:q + 24], 0.5, None, ALU.mult))
                link(dve.tensor_scalar(bc_qg(l), bc_qg(l), QK_D ** -0.5, None, ALU.mult))
                link(dve.tensor_scalar(bc_nq(l), bc_nq(l), NA_D ** -0.5, None, ALU.mult))
            dve.wait_ge(csilu_ready, 1)
            link(dve.scalar_tensor_tensor(CS[:, :], RT[:, 0:16], 1.0, COLS[:, P:P + 16], ALU.add, ALU.mult))
            dve.tensor_scalar(CS[:, :], CS[:, :], 0.5, None, ALU.mult).then_inc(csilu_ready, 1)

            def rstd(s, n):
                w = rstd_width(s)
                m, r = stat(rstd_at[s])
                return m[:, 0:w], r[:, 0:w]

            def bcast(ap, n):
                return ap.unsqueeze(2).broadcast_to([ap.shape[0], ap.shape[1], n])

            for s in schedule:
                k, l = s[0], layer_of(s)
                tq = tiles_q(l)
                c0 = 0 if l < DEPTH - 1 else L
                if k == "modT":
                    i = s[2]
                    dve.wait_ge(*full_of(s))
                    link_to = dve.tensor_tensor(MODv[l][:, 4 * i:4 * i + 4, :],
                                                bank_of(s)[:, 0:8].rearrange("p (c j) -> p c j", j=2),
                                                bcast(COLS[:, 64 * l + 4 * i:64 * l + 4 * i + 4], 2), ALU.add)
                    link_to.then_inc(free_of(s)[0], 1)
                elif k == "modfin":
                    w = s[2] - 1
                    for i in range(6 * w, 6 * w + 4):
                        dve.wait_ge(*free_of(("modT", l, i)))
                    link(dve.scalar_tensor_tensor(AMv[l][:, w, :, 0], MODv[l][:, 24 * w + 8:24 * w + 16, 0], 1.0,
                                                  COLS[:, 64 * l + 48 + 8 * w:64 * l + 56 + 8 * w], ALU.add,
                                                  ALU.mult))
                    dve.scalar_tensor_tensor(AMv[l][:, w, :, 1], MODv[l][:, 24 * w + 8:24 * w + 16, 1], 1.0,
                                             COLS[:, 64 * l + 48 + 8 * w:64 * l + 56 + 8 * w], ALU.add,
                                             ALU.mult).then_inc(mod_ready, 1)
                elif k == "norm":
                    t, w = s[3], s[2]
                    dve.wait_ge(ssq_ready, ssq_at[s])
                    m = ssq_cols(s)
                    mm, rr = rstd(s, D)
                    dve.tensor_scalar(mm, m[:, 0:1], 1.0 / D, EPS, ALU.mult, ALU.add).then_inc(mean_ready, 1)
                    dve.wait_ge(rstd_ready, rstd_at[s])
                    dve.tensor_scalar(XS[:, t, :], Xv[:, t, :], rr, None, ALU.mult).then_inc(xs_ready, 1)
                elif k == "hT" and s[4] % 2 == 0:
                    _, _, w, st, kp = s
                    dve.wait_ge(*full_of(s))
                    dve.wait_ge(mod_ready, modfin_n[("modfin", l, w)])
                    for i in (0, 1):
                        kk = 2 * kp + i
                        ins = dve.tensor_scalar(HT[:, kk, st * L:(st + 1) * L], bank_of(s)[:, i * L:(i + 1) * L],
                                                AMv[l][:, w - 1, kk, st:st + 1], MODv[l][:, 24 * (w - 1) + kk, st:st + 1],
                                                ALU.mult, ALU.add)
                    ins.then_inc(free_of(s)[0], 1)
                elif k == "pu" and s[2] % 2 == 0:
                    dve.wait_ge(*full_of(s))
                    dve.tensor_copy(UT[:, s[2], :], bank_of(s)[0:ML_D, :]).then_inc(free_of(s)[0], 1)
                elif k == "pP" and s[3] % 2 == 0:
                    dve.wait_ge(*full_of(s))
                    c, n = p_cols(s)
                    dve.tensor_copy(PRv[:, s[3], c:c + n], bank_of(s)[:, 0:n]).then_inc(free_of(s)[0], 1)
                elif k == "pz":
                    dve.wait_ge(zs_tanh, pz_n[s])
                    dve.scalar_tensor_tensor(ZS[:, s[2], c0:TOK], ZS[:, s[2], c0:TOK], 1.0,
                                             bank_of(s)[0:ML_D, c0:TOK], ALU.add, ALU.mult).then_inc(
                        free_of(s)[0], 1)
                elif k == "gates":
                    for t in range(T):
                        dve.wait_ge(*free_of(("pP", l, "B", t)))
                    g = PRv[:, :, PG:PG + 16]
                    dve.tensor_tensor(g, g, bc_gb(l).unsqueeze(1).broadcast_to([P, T, 16]), ALU.add).then_inc(
                        gates_ready, 1)
                    bk = bank_of(s)[0:ML_H, :].rearrange("p (q t) -> p q t", q=4)
                    for t in range(T):
                        if t < T - 1:
                            dve.wait_ge(gate_filled, 3 * l + t + 1)
                        else:
                            dve.wait_ge(*full_of(s))
                        r0 = (t // 2) * L + (1 - t % 2) * P
                        dve.tensor_copy(ROW[:, 0:2, t * P:(t + 1) * P], bk[:, 0:2, :])
                        ins = dve.tensor_copy(ROW[:, 2:4, r0:r0 + P], bk[:, 2:4, ::-1])
                        ins.then_inc(gate_copied if t < T - 1 else free_of(s)[0], 1)
                elif k == "rows":
                    dve.wait_ge(*free_of(("gates", l)))
                    f = ROW[:, 1::2, :]
                    dve.scalar_tensor_tensor(GEM[:, 0:2, :], f, -1.0, f, ALU.mult, ALU.max).then_inc(lfa_ready, 1)
                    link(dve.memset(GEM[:, 2:3, :], 1.0))
                    dve.wait_ge(lf_ready, l + 1)
                    link(dve.scalar_tensor_tensor(f, f, 0.0, GEM[:, 0:2, :], ALU.min, ALU.subtract))
                    for d in (0, 1):
                        link(dve.tensor_tensor_scan(GEM[:, d, :], GEM[:, 2, :], ROW[:, 2 * d + 1, :], 0.0, ALU.mult,
                                                    ALU.add))
                    for d in (0, 1):
                        link(dve.tensor_tensor(ROW[:, 2 * d, :], ROW[:, 2 * d, :], GEM[:, d, :], ALU.subtract))
                        link(dve.tensor_tensor_scan(ROW[:, 2 * d + 1, :], ROW[:, 2 * d, :], ROW[:, 2 * d, :], 0.0,
                                                    ALU.max, ALU.max))
                    def nat(ap, d):
                        return ap if d == 0 else ap.rearrange("p (s t) -> p s t", s=2)[:, :, ::-1]

                    def plain(ap, d):
                        return ap if d == 0 else ap.rearrange("p (s t) -> p s t", s=2)
                    for d in (0, 1):
                        link(dve.tensor_tensor(plain(GEM[:, 2 + d, :], d), nat(GEM[:, d, :], d),
                                               nat(ROW[:, 2 * d + 1, :], d), ALU.add))
                    for d in (0, 1):
                        link(dve.tensor_copy(plain(GEM[:, d, :], d), nat(ROW[:, 2 * d, :], d)))
                        ins = dve.tensor_scalar(plain(NEGMUv[:, d, :], d), nat(ROW[:, 2 * d + 1, :], d), -1.0, None,
                                                ALU.mult)
                        if d == 0:
                            link(ins)
                    ins.then_inc(em_in, 1)
                    dve.wait_ge(em_ready, l + 1)
                    dve.wait_ge(em_in, l + 1)
                    dve.memset(MV[:, :, :, 96:97].rearrange("p t h o -> p (t h) o"), 1.0).then_inc(mv_ready, 1)
                    dve.wait_ge(mv_ready, l + 1)
                    tick(dve, rows_ready)
                elif k == "cols":
                    dve.wait_ge(*full_of(s))
                    dve.tensor_copy(GEMC[:, :], bank_of(s)[:, 0:64]).then_inc(gc_ready, 1)
                    dve.wait_ge(gc_ready, l + 1)
                    tick(dve, free_of(s)[0])
                elif k == "mv" and s[2] % 2 == 0:
                    dve.wait_ge(*full_of(s))
                    dve.tensor_copy(MV[:, s[2], :, 0:ML_D],
                                    bank_of(s)[:, 0:ML_W].rearrange("p (h e) -> p h e", h=ML_H)).then_inc(
                        free_of(s)[0], 1)
                elif k == "conv":
                    h = s[2]
                    dve.wait_ge(*free_of(("pu", l, h)))
                    q = 24 * l
                    b, w0, w1, w2 = (c96(q + 8 + h), c96(q + 12 + h), c96(q + 16 + h), c96(q + 20 + h))
                    u2 = UT[:, h, :].rearrange("p (s t) -> p s t", s=2)
                    o2 = UC[:, h, :].rearrange("p (s t) -> p s t", s=2)
                    link(dve.tensor_scalar(UC[:, h, :], UT[:, h, :], w1, b, ALU.mult, ALU.add))
                    link(dve.scalar_tensor_tensor(o2[:, :, 1:L], u2[:, :, 0:L - 1], w0, o2[:, :, 1:L], ALU.mult,
                                                  ALU.add))
                    dve.scalar_tensor_tensor(o2[:, :, 0:L - 1], u2[:, :, 1:L], w2, o2[:, :, 0:L - 1], ALU.mult,
                                             ALU.add).then_inc(conv_acc, 1)
                    dve.wait_ge(conv_tanh, conv_n[s])
                    dve.wait_ge(conv_acc, conv_n[s])
                    dve.scalar_tensor_tensor(UC[:, h, :], conv_tmp(s), 1.0, UC[:, h, :], ALU.add,
                                             ALU.mult).then_inc(uc_ready, 1)
                elif k == "mqk":
                    h = s[2]
                    key = s + ("q",)
                    dve.wait_ge(*full_of(key))
                    dve.tensor_copy(MQ[:, h, c0:TOK], bank_of(key)[0:ML_D, c0:TOK]).then_inc(free_of(key)[0], 1)
                    dve.wait_ge(*full_of(s + ("k",)))
                    link(dve.tensor_scalar(UC[:, h, :], UC[:, h, :], c96(24 * l + 4 + h), None, ALU.mult))
                elif k == "mgrid":
                    _, _, h, d = s
                    n = grid_n[s]
                    g = GRIDB[n % 2]
                    mu = bank_of(s)
                    dve.wait_ge(*full_of(s))
                    dve.wait_ge(gc_ready, l + 1)
                    if n > 2:
                        dve.wait_ge(pv_done, mpv_before(s))
                    for t in tq:
                        ins = dve.scalar_tensor_tensor(g[:, t, t * P:(t + 1) * P], mu[:, t * P:(t + 1) * P],
                                                       GC[:, d, t, h:h + 1], TRI[:, d * P:(d + 1) * P], ALU.add,
                                                       ALU.add)
                    ins.then_inc(diag_ready, 1)
                    dve.wait_ge(grid_exp, n)
                    todo = [(j, t0, t1) for j in range(T) for t0, t1 in runs(l, d, j, True)]
                    for j, t0, t1 in todo:
                        if d == 0:
                            dve.wait_ge(*full_of(("mst", l, h, j)))
                        ins = dve.tensor_tensor(g[:, j, t0 * P:t1 * P], g[:, j, t0 * P:t1 * P],
                                                bank_of(("mst", l, h, j))[:, t0 * P:t1 * P], ALU.mult)
                    ins.then_inc(grid_ready, 1)
                    dve.wait_ge(grid_ready, n)
                    tick(dve, free_of(s)[0])
                    if d == 1:
                        for j in range(T):
                            tick(dve, free_of(("mst", l, h, j))[0])
                elif k == "mpv":
                    _, _, h, d = s
                    acc = bank[6 + acc_at[s] % 2]
                    nt = len(tq)
                    av = acc[:, tq[0] * 97:(tq[0] + nt) * 97].rearrange("p (t e) -> p t e", e=97)
                    dve.wait_ge(pv_done, pv_at[s])
                    den = ST[:, 128:128 + nt]
                    link(dve.scalar_tensor_tensor(den, av[:, :, 96], -1.0, GC[:, 2 + d, tq[0]:tq[0] + nt, h],
                                                  ALU.mult, ALU.max))
                    link(dve.tensor_tensor(den, den, av[:, :, 96], ALU.max))
                    link(dve.reciprocal(den, den))
                    hs = HS[:, tq[0]:tq[0] + nt, h * ML_D:(h + 1) * ML_D]
                    if d == 0:
                        dve.tensor_tensor(hs, av[:, :, 0:ML_D], bcast(den, ML_D), ALU.mult).then_inc(acc_free, 1)
                        dve.wait_ge(acc_free, acc_at[s] + 1)
                    else:
                        tmp = RT[:, 0:384].rearrange("p (t e) -> p t e", t=4)[:, 0:nt, :]
                        dve.tensor_tensor(tmp, av[:, :, 0:ML_D], bcast(den, ML_D), ALU.mult).then_inc(acc_free, 1)
                        dve.wait_ge(acc_free, acc_at[s] + 1)
                        link(dve.tensor_tensor(hs, hs, tmp, ALU.add))
                elif k == "mln":
                    nt = len(tq)
                    hs = HS[:, tq[0]:tq[0] + nt, :].rearrange("p t (h e) -> p (t h) e", e=ML_D)
                    nn = nt * ML_H
                    sq = view(WORK, 2560, nn, ML_D)
                    mu = ST[:, 128:128 + nn]
                    link(dve.tensor_reduce(mu, hs, AX.X, ALU.add))
                    link(dve.tensor_scalar(mu, mu, 1.0 / ML_D, None, ALU.mult))
                    link(dve.tensor_tensor(hs, hs, bcast(mu, ML_D), ALU.subtract))
                    dve.wait_ge(pv_done, pv_at[("mpv", l, ML_H - 1, 1)])
                    link(dve.tensor_tensor(sq, hs, hs, ALU.mult))
                    link(dve.tensor_reduce(mu, sq, AX.X, ALU.add))
                    m, r = rstd(s, ML_D)
                    dve.tensor_scalar(m, mu, 1.0 / ML_D, EPS, ALU.mult, ALU.add).then_inc(mean_ready, 1)
                    dve.wait_ge(rstd_ready, rstd_at[s])
                    dve.tensor_tensor(hs, hs, bcast(r, ML_D), ALU.mult).then_inc(hn_ready, 1)
                elif k == "mlT":
                    h = s[2]
                    dve.wait_ge(*full_of(s))
                    o = MLT[:, h, c0:TOK]
                    link(dve.scalar_tensor_tensor(o, bank_of(s)[0:ML_D, c0:TOK], c96(24 * l + h),
                                                  UC[:, h, c0:TOK], ALU.mult, ALU.add))
                    tick(dve, free_of(s)[0])
                    dve.scalar_tensor_tensor(o, o, 0.5, ZS[:, h, c0:TOK], ALU.mult, ALU.mult).then_inc(mlt_ready, 1)
                    if h == ML_H - 1:
                        dve.wait_ge(mlt_ready, ML_H * (l + 1))
                        tick(dve, hn_used)
                elif k == "cnorm":
                    t = s[2]
                    m = ssq_cols(s)
                    mm, rr = rstd(s, 0)
                    dve.wait_ge(ssq_ready, ssq_at[s])
                    if t in tq:
                        link(dve.tensor_scalar(mm[:, 0:1], m[:, 0:1], 1.0 / Q_RANK, EPS, ALU.mult, ALU.add))
                    else:
                        link(dve.memset(mm[:, 0:1], 1.0))
                    dve.tensor_scalar(mm[:, 1:2], m[:, 1:2], 1.0 / KV_RANK, EPS, ALU.mult, ALU.add).then_inc(
                        mean_ready, 1)
                    dve.wait_ge(rstd_ready, rstd_at[s])
                    if t in tq:
                        link(dve.tensor_scalar(PRv[:, t, 0:Q_RANK], PRv[:, t, 0:Q_RANK], rr[:, 0:1], None, ALU.mult))
                    dve.tensor_scalar(PRv[:, t, Q_RANK:384], PRv[:, t, Q_RANK:384], rr[:, 1:2], None,
                                      ALU.mult).then_inc(cn_ready, 1)
                elif k == "cT":
                    t = s[2]
                    dve.wait_ge(*full_of(s))
                    for c in range(0 if t in tq else 2, 3):
                        ins = dve.tensor_scalar(CT[:, c, t * P:(t + 1) * P], bank_of(s)[:, c * P:(c + 1) * P],
                                                c2(16 + 3 * l + c), None, ALU.mult)
                    ins.then_inc(free_of(s)[0], 1)
                elif k == "uqk":
                    t = s[2]
                    q, kt = QTM[t % 2], KTM[t % 2]
                    isq = t in tq
                    if t >= 2:
                        for key in qkT_jobs(("qkT", l, t - 2)):
                            dve.wait_ge(*full_of(key))
                    if isq:
                        for i in (0, 1):
                            key = s + ("q", i)
                            dve.wait_ge(*full_of(key))
                            dve.tensor_copy(q[:, 3 * i:3 * i + 3, :],
                                            bank_of(key)[:, 0:288].rearrange("p (h e) -> p h e", h=3)).then_inc(
                                free_of(key)[0], 1)
                    for i in (0, 1):
                        key = s + ("k", i)
                        dve.wait_ge(*full_of(key))
                        kvv = bank_of(key)[:, 0:384].rearrange("p (h e) -> p h e", h=3)
                        dve.tensor_copy(kt[:, 3 * i:3 * i + 3, 0:NOPE_D], kvv[:, :, 0:NOPE_D])
                        dve.tensor_copy(VV[:, t, 3 * i:3 * i + 3, :], kvv[:, :, NOPE_D:]).then_inc(
                            free_of(key)[0], 1)
                    link(dve.tensor_copy(kt[:, :, NOPE_D:], PRv[:, t, 384:416].unsqueeze(1).broadcast_to(
                        [P, MLA_H, ROPE_D])))
                    for i in (0, 1):
                        dve.wait_ge(*free_of(s + ("k", i)))
                        if isq:
                            dve.wait_ge(*free_of(s + ("q", i)))
                    m, r = rstd(s, 0)
                    sq = view(WORK, 2560, MLA_H, QK_D)
                    both = ([(q, m[:, 0:6], bc_qg(l))] if isq else []) + [(kt, m[:, 6:12], bc_kg(l))]
                    if not isq:
                        link(dve.memset(m[:, 0:6], 1.0))
                    for x_, mm, _g in both:
                        link(dve.tensor_tensor(sq, x_, x_, ALU.mult))
                        link(dve.tensor_reduce(mm, sq, AX.X, ALU.add))
                    dve.tensor_scalar(m, m, 1.0 / QK_D, EPS, ALU.mult, ALU.add).then_inc(mean_ready, 1)
                    dve.wait_ge(rstd_ready, rstd_at[s])
                    for x_, _m, g_ in both:
                        rr = r[:, 0:6] if x_ is q else r[:, 6:12]
                        link(dve.tensor_tensor(x_, x_, bcast(rr, QK_D), ALU.mult))
                        ins = dve.tensor_tensor(x_, x_, g_.unsqueeze(1).broadcast_to([P, MLA_H, QK_D]), ALU.mult)
                        if t < 2 and x_ is kt:
                            ins.then_inc(qk_ready, 1)
                            continue
                        link(ins)
                        if t < 2:
                            continue
                        cos = ROv[:, t - 2, 0, :].unsqueeze(1).broadcast_to([P, MLA_H, ROPE_D])
                        sin = ROv[:, t - 2, 1, :].rearrange("p (a b c) -> p a b c", a=2, b=2)
                        xr = x_[:, :, NOPE_D:]
                        x4 = xr.rearrange("p h (a b c) -> p h a b c", a=2, b=2)
                        t4 = view(WORK, 3200, MLA_H, ROPE_D)
                        t5 = t4.rearrange("p h (a b c) -> p h a b c", a=2, b=2)
                        for b_ in (0, 1):
                            sb_ = sin[:, :, b_, :].unsqueeze(1).broadcast_to([P, MLA_H, 2, 8])
                            link(dve.tensor_tensor(t5[:, :, :, b_, :], x4[:, :, :, 1 - b_, :], sb_, ALU.mult))
                        link(dve.tensor_tensor(xr, xr, cos, ALU.mult))
                        ins = dve.tensor_tensor(xr, xr, t4, ALU.add)
                        if x_ is kt:
                            ins.then_inc(qk_ready, 1)
                        else:
                            link(ins)
                elif k == "qkT":
                    for key in qkT_jobs(s):
                        if key[3] == "q":
                            dve.wait_ge(*full_of(key))
                            hh = 3 * key[4]
                            dve.tensor_copy(QT[:, hh:hh + 3, s[2] * P:(s[2] + 1) * P],
                                            bank_of(key)[0:QK_D, 0:384].rearrange("p (h t) -> p h t",
                                                                                  h=3)).then_inc(free_of(key)[0], 1)
                elif k == "nan":
                    t = s[2]
                    isq = t in tq
                    dve.wait_ge(*free_of(("pP", l, "B", t)))
                    dve.wait_ge(*free_of(("pP", l, "C", t)))
                    h0 = 0 if isq else NA_H
                    x_ = PRv[:, t, PNQ + h0 * NA_D:PNV].rearrange("p (h e) -> p h e", e=NA_D)
                    nh = 2 * NA_H - h0
                    sq = view(WORK, 2560, nh, NA_D)
                    m, r = rstd(s, 0)
                    if not isq:
                        link(dve.memset(m[:, 0:4], 1.0))
                    link(dve.tensor_tensor(sq, x_, x_, ALU.mult))
                    link(dve.tensor_reduce(m[:, h0:8], sq, AX.X, ALU.add))
                    dve.tensor_scalar(m, m, 1.0 / NA_D, EPS, ALU.mult, ALU.add).then_inc(mean_ready, 1)
                    dve.wait_ge(rstd_ready, rstd_at[s])
                    link(dve.tensor_tensor(x_, x_, bcast(r[:, h0:8], NA_D), ALU.mult))
                    if isq:
                        xq = x_[:, 0:NA_H, :]
                        link(dve.tensor_tensor(xq, xq, bc_nq(l).unsqueeze(1).broadcast_to([P, NA_H, NA_D]),
                                               ALU.mult))
                    xk = x_[:, nh - NA_H:nh, :]
                    dve.tensor_tensor(xk, xk, bc_nk(l).unsqueeze(1).broadcast_to([P, NA_H, NA_D]),
                                      ALU.mult).then_inc(na_ready, 1)
                elif k == "nT":
                    t = s[2]
                    dve.wait_ge(*full_of(s))
                    bk = bank_of(s)[:, :].rearrange("p (a t) -> p a t", a=4)
                    if t in tq:
                        dve.tensor_copy(NQT[:, :, t * P:(t + 1) * P], bk[:, 0:2, :])
                    dve.tensor_copy(NKT[:, :, t * P:(t + 1) * P], bk[:, 2:4, :]).then_inc(free_of(s)[0], 1)
                elif k == "S":
                    _, b, _, t, h, _ = s
                    u = UNIT_AT[s[1:]]
                    nk = keys_of(s)
                    bk = bank_of(s)
                    dve.wait_ge(*full_of(s))
                    if b == 1 and t >= 2:
                        dve.wait_ge(bias_masked, 2 * (l + 1))
                        link(dve.tensor_tensor(bk[:, L:TOK], bk[:, L:TOK], BIAS[:, t - 2, h, :], ALU.add))
                    if u >= 2:
                        dve.wait_ge(*free_of(("S",) + UNITS[u - 2]))
                    dve.tensor_reduce(neg_max(u), bk[:, 0:nk], AX.X, ALU.max, negate=True).then_inc(nmax_ready, 1)
                elif k == "PV":
                    u = UNIT_AT[s[1:]]
                    key = ("ET",) + s[1:]
                    nkt = keys_of(s) // P
                    dve.wait_ge(*full_of(key))
                    if u >= 2:
                        dve.wait_ge(pv_done, pv_at[("PV",) + UNITS[u - 2]])
                    dve.tensor_copy(PT[u % 2][:, 0:nkt, :].rearrange("p a b -> p (a b)"),
                                    bank_of(key)[:, 0:nkt * P]).then_inc(free_of(key)[0], 1)
                elif k == "OT":
                    _, b, _, t, h, _ = s
                    u = UNIT_AT[s[1:]]
                    nh = h + 1
                    acc = bank[6 + acc_at[s] % 2]
                    dve.wait_ge(pv_done, pv_at[("PV",) + s[1:]])
                    rs = ST[:, 160:160 + nh]
                    link(dve.reciprocal(rs, exp_sums(u - h, nh)))
                    if OT_n[s] > 1:
                        dve.wait_ge(*full_of(OT_key[OT_n[s] - 1]))
                    dve.tensor_tensor(OM[:, 0:nh * 64].rearrange("p (h e) -> p h e", h=nh),
                                      acc[:, 0:nh * 64].rearrange("p (h e) -> p h e", h=nh), bcast(rs, 64),
                                      ALU.mult).then_inc(om_ready, 1)
                    dve.wait_ge(om_ready, OT_n[s])
                    tick(dve, acc_free)
                    dve.wait_ge(*full_of(s))
                    dst = (MLAT, NAT)[b]
                    nc_ = (3, 2)[b]
                    dve.tensor_copy(dst[:, :, t * P:(t + 1) * P],
                                    bank_of(s)[:, 0:nc_ * P].rearrange("p (a t) -> p a t", a=nc_)).then_inc(
                        free_of(s)[0], 1)
                elif k == "wo":
                    t = s[2]
                    st = t // 2
                    for n in (0, 1):
                        key = s + (n,)
                        dve.wait_ge(*full_of(key))
                        dve.wait_ge(*free_of(("gbc", l, 1, st, n)))
                        dve.tensor_tensor(YT, bank_of(key)[:, :], GB[:, st, 512 * n:512 * n + 512],
                                          ALU.mult).then_inc(free_of(key)[0], 1)
                        dve.wait_ge(*free_of(key))
                        xx = Xv[:, t, 512 * n:512 * n + 512]
                        ins = dve.tensor_tensor(xx, xx, YT, ALU.add)
                        if n:
                            ins.then_inc(resid_ready, 1)
                            dve.wait_ge(resid_ready, resid_at[s])
                        else:
                            link(ins)
                elif k == "router":
                    nt = len(tq)
                    dve.wait_ge(*free_of(s))
                    aff = RT[:, 0:16 * nt]
                    sel = RT[:, 64:64 + 16 * nt]
                    link(dve.tensor_scalar(aff, aff, 0.5, 0.5, ALU.mult, ALU.add))
                    a3 = aff.rearrange("p (t e) -> p t e", e=16)
                    s3 = sel.rearrange("p (t e) -> p t e", e=16)
                    link(dve.tensor_tensor(s3, a3, bc_rb.unsqueeze(1).broadcast_to([P, nt, 16]), ALU.add))
                    s4 = sel.rearrange("p (g e) -> p g e", e=4)
                    ng = 4 * nt
                    pr = RT[:, 128:128 + 6 * ng].rearrange("p (g e) -> p g e", e=6)
                    link(dve.tensor_tensor(pr[:, :, 0:3], s4[:, :, 0:3], s4[:, :, 1:4], ALU.add))
                    link(dve.tensor_tensor(pr[:, :, 3:5], s4[:, :, 0:2], s4[:, :, 2:4], ALU.add))
                    link(dve.tensor_tensor(pr[:, :, 5:6], s4[:, :, 0:1], s4[:, :, 3:4], ALU.add))
                    gs = RT[:, 224:224 + ng]
                    link(dve.tensor_reduce(gs, pr, AX.X, ALU.max))
                    g3 = gs.rearrange("p (t g) -> p t g", g=4)
                    mx = RT[:, 240:240 + nt]

                    def first_max(v3, m_, out3, wts, width):
                        link(dve.tensor_reduce(m_, v3, AX.X, ALU.max))
                        link(dve.tensor_tensor(out3, v3, bcast(m_, width), ALU.is_equal))
                        link(dve.tensor_tensor(out3, out3, wts, ALU.mult))
                        link(dve.tensor_reduce(m_, out3, AX.X, ALU.max))
                        link(dve.tensor_tensor(out3, out3, bcast(m_, width), ALU.is_equal))

                    wt16 = RANK.unsqueeze(1).broadcast_to([P, nt, 16])
                    wt4 = RANK[:, 12:16].unsqueeze(1).broadcast_to([P, nt, 4])
                    ing = RT[:, 244:244 + ng].rearrange("p (t g) -> p t g", g=4)
                    first_max(g3, mx, ing, wt4, 4)
                    off = RT[:, 260:260 + ng]
                    link(dve.tensor_scalar(off, RT[:, 244:244 + ng], -1.0, BIG, ALU.add, ALU.mult))
                    link(dve.tensor_tensor(s4, s4, bcast(off, 4), ALU.add))
                    oh = RT[:, 128:128 + 16 * nt].rearrange("p (t e) -> p t e", e=16)
                    first_max(s3, mx, oh, wt16, 16)
                    gt = RT[:, 280:280 + 16 * nt].rearrange("p (t e) -> p t e", e=16)
                    link(dve.tensor_copy(gt, oh))
                    link(dve.tensor_scalar(oh, oh, -4.0 * BIG, None, ALU.mult))
                    link(dve.tensor_tensor(s3, s3, oh, ALU.add))
                    first_max(s3, mx, oh, wt16, 16)
                    link(dve.tensor_tensor(gt, gt, oh, ALU.add))
                    link(dve.tensor_tensor(gt, gt, a3, ALU.mult))
                    link(dve.tensor_reduce(mx, gt, AX.X, ALU.add))
                    link(dve.reciprocal(mx, mx))
                    link(dve.tensor_scalar(mx, mx, 0.5, None, ALU.mult))
                    dve.tensor_tensor(GATEv[:, tq[0]:tq[0] + nt, :], gt, bcast(mx, 16), ALU.mult).then_inc(
                        gate_ready, 1)
                    dve.wait_ge(gate_ready, l + 1)
                elif k == "ab":
                    _, _, e, t = s
                    n = ab_n[s]
                    dve.wait_ge(moe_tanh, n)
                    if n > 2:
                        dve.wait_ge(*full_of(y_key[n - 2] + ("T",)))
                    bk = bank_of(s)
                    link(dve.scalar_tensor_tensor(HID[n % 2], TH[n % 2], 1.0, bk[:, 0:FF], ALU.add, ALU.mult))
                    dve.scalar_tensor_tensor(HID[n % 2], HID[n % 2], GATEv[:, t, e:e + 1], bk[:, FF:2 * FF],
                                             ALU.mult, ALU.mult).then_inc(hid_ready, 1)
                    dve.wait_ge(hid_ready, n)
                    tick(dve, free_of(s)[0])
                elif k == "y":
                    _, _, e, t = s
                    for nn in (0, 1):
                        key = s + (nn,)
                        dve.wait_ge(*full_of(key))
                        if e:
                            dve.wait_ge(*free_of(("y", l, e - 1, t, nn)))
                        o = ACC[:, t, 512 * nn:512 * nn + 512]
                        if e == 0:
                            ins = dve.tensor_copy(o, bank_of(key)[:, :])
                        else:
                            ins = dve.tensor_tensor(o, o, bank_of(key)[:, :], ALU.add)
                        ins.then_inc(free_of(key)[0], 1)
                elif k == "moe_out":
                    t = s[2]
                    st = t // 2
                    if t == tq[0]:
                        for nn in (0, 1):
                            dve.wait_ge(*free_of(("y", l, N_E - 1, tq[-1], nn)))
                            for st_ in sorted({t_ // 2 for t_ in tq}):
                                dve.wait_ge(*free_of(("gbc2", l, st_, nn)))
                    link(dve.tensor_tensor(ACC[:, t, :], ACC[:, t, :], GB[:, st, :], ALU.mult))
                    ins = dve.tensor_tensor(Xv[:, t, :], Xv[:, t, :], ACC[:, t, :], ALU.add)
                    ins.then_inc(resid_ready if l < DEPTH - 1 else out_ready, 1)


INPUTS = ["x", "c", "ctx", "c_ctx", "w_mod", "b_mod", "norm1_g", "norm2_g", "w_in", "w_out", "mla_qnorm_g",
          "mla_w_uq", "mla_kvnorm_g", "mla_w_ukv", "mla_q_g", "mla_k_g", "ml_conv_w", "ml_conv_b", "ml_w_q",
          "ml_w_k", "ml_w_v", "ml_gate_b", "ml_norm_g", "ml_skip", "na_q_g", "na_k_g", "na_rpb", "router_w",
          "router_b", "moe_w1", "moe_w3", "moe_w2"]


def shape_constants():
    t = np.arange(L)
    inv = 10000.0 ** (-np.arange(ROPE_D // 4, dtype=np.float32) / (ROPE_D // 4))
    ar = (t // GRID).astype(np.float32)[:, None] * inv
    ac = (t % GRID).astype(np.float32)[:, None] * inv
    cos = np.cos(np.concatenate([ar, ar, ac, ac], axis=-1))
    sin = np.sin(np.concatenate([-ar, ar, -ac, ac], axis=-1))
    table = np.zeros((P, 2, 2, ROPE_D), np.float32)
    for i in (0, 1):
        table[:, i, 0], table[:, i, 1] = cos[i * P:(i + 1) * P], sin[i * P:(i + 1) * P]
    rank = np.tile(np.arange(16, 0, -1, dtype=np.float32), (P, 1))
    return np.ascontiguousarray(np.concatenate([table.reshape(P, -1), rank], axis=1).astype(np.float32))


def kernel(**inputs):
    import numpy as _np
    import concourse.bacc as _bacc
    from concourse import mybir as _mybir
    from concourse.bass_utils import run_bass_kernel_spmd as _run

    nc = _bacc.Bacc("TRN2", target_bir_lowering=False, num_devices=1)
    arrays, aps = {}, {}
    data = {name: _np.ascontiguousarray(inputs[name]) for name in INPUTS}
    data["rope"] = shape_constants()
    for name, v in data.items():
        arrays[f"in_{name}"] = v
        aps[name] = nc.dram_tensor(f"in_{name}", v.shape, _mybir.dt.from_np(v.dtype), kind="ExternalInput").ap()
    aps["out"] = nc.dram_tensor("out_x", (1, L, D), F32, kind="ExternalOutput").ap()
    build(nc, aps)
    r = _run(nc, [arrays], core_ids=[0])
    return r.results[0]["out_x"]
```

```python
from contextlib import ExitStack

import numpy as np

import concourse.bass as bass
from concourse import mybir

F32 = mybir.dt.float32
U32 = mybir.dt.uint32
ALU = mybir.AluOpType
ACT = mybir.ActivationFunctionType
AX = mybir.AxisListType

P = 128
D = 1024
KD = D // P
DEPTH = 2
L = 256
T = 4
TOK = T * P
EPS = 1e-6
Q_RANK, KV_RANK, ROPE_D, NOPE_D, V_D = 256, 128, 32, 64, 64
QK_D = NOPE_D + ROPE_D
MLA_H = 6
ML_H, ML_D = 4, 96
ML_W = ML_H * ML_D
NA_H, NA_D = 4, 64
NA_W = NA_H * NA_D
GRID = 64
WIN_R, WIN_C = 8, 16
ROWS = L // GRID
N_E, N_G, FF = 16, 4, 256
OFF_Q = 0
OFF_U = Q_RANK + KV_RANK + ROPE_D
OFF_Z = OFF_U + ML_W
OFF_G = OFF_Z + ML_W
OFF_NQ = OFF_G + 4 * ML_H
OFF_NK = OFF_NQ + NA_W
N_IN = OFF_NK + 2 * NA_W
CAP = P
NOWHERE = 65536.0
NEG = -1e30
BIG = 1e30

PA, PG, PNQ, PNK, PNV = 0, OFF_U, OFF_U + 16, OFF_U + 16 + NA_W, OFF_U + 16 + 2 * NA_W
PW = OFF_U + 16 + 3 * NA_W
CHUNK = {"A": (OFF_Q, OFF_U, PA), "B": (OFF_G, 16 + NA_W, PG), "C": (OFF_NK, 2 * NA_W, PNK)}


def tiles_q(l):
    return [0, 1, 2, 3] if l < DEPTH - 1 else [2, 3]


def allowed(d, t, j):
    if t // 2 != j // 2:
        return t >= 2
    return j <= t if d == 0 else j >= t


def runs(l, d, j, diagonal):
    ts = [t for t in tiles_q(l) if allowed(d, t, j) and (diagonal or t != j)]
    out = []
    for t in ts:
        if out and out[-1][1] == t:
            out[-1][1] = t + 1
        else:
            out.append([t, t + 1])
    return out


def layer_of(s):
    return s[2] if s[0] in ("S", "PV", "OT") else s[1]


def p_cols(s):
    _, l, w, t = s
    c, n = CHUNK[w][2], CHUNK[w][1]
    if t not in tiles_q(l):
        if w == "A":
            return Q_RANK, n - Q_RANK
        if w == "B":
            return PG, 16
    return c, n


def keys_of(s):
    return TOK if s[3] >= 2 else L


def qkT_jobs(s):
    return [s + (w, i) for w in ("q", "k") if w == "k" or s[2] in tiles_q(s[1]) for i in (0, 1)]


PACK_DMAS = DEPTH * 9 + 2
PARAM_DMAS = DEPTH * 5 + 3
MODS = 12
MOD_FIRST = 4


def weight_pieces():
    out = []
    out += [("mod", 0, i) for i in range(MOD_FIRST)]
    for l in range(DEPTH):
        out += [("w_u", l), ("w_B", l), ("w_A", l), ("w_C", l), ("w_z", l)]
        out += late_mods(l)
        out += [("wo_mla", l), ("wo_ml", l), ("wo_na", l)]
        out += [("w13", l, e) for e in range(N_E)]
    return out


def late_mods(l):
    if l:
        return []
    return [("mod", 0, i) for i in range(MOD_FIRST, MODS)] + [("mod", m, i) for m in range(1, DEPTH)
                                                              for i in range(MODS)]


def spread(steps, fill):
    out, done = [], 0
    n = len(steps) - 8
    for i, st in enumerate(steps):
        out.append(st)
        if st[0] in ("mst", "mgrid") or st[0] == "mpv" and st[3] == 0:
            continue
        while done < len(fill) and (done + 1) * n <= (i + 1) * len(fill):
            out += fill[done]
            done += 1
    assert done == len(fill)
    return out


def unit_steps(l, b):
    units = [u for u in UNITS if u[0] == b and u[1] == l]
    s = []
    for i, u in enumerate(units):
        s += [("S",) + u]
        if i >= 1:
            s += [("PV",) + units[i - 1]]
            if units[i - 1][4]:
                s += [("OT",) + units[i - 1]]
    return s + [("PV",) + units[-1], ("OT",) + units[-1]]


def merge(x, y):
    n, out, j = len(x), [], 0
    for i, st in enumerate(x):
        out.append(st)
        while j < len(y) and j * n < (i + 1) * len(y):
            out.append(y[j])
            j += 1
    return out + y[j:]


def make_schedule():
    s = []
    for l in range(DEPTH):
        tq = tiles_q(l)
        sq = sorted({t // 2 for t in tq})
        if l == 0:
            s += [(k, l, i) for i in range(MOD_FIRST) for k in ("mod", "modT")] + [("modfin", l, 1)]
        s += [("norm", l, 1, t) for t in range(T)]
        s += [("hT", l, 1, st, kp) for st in (0, 1) for kp in range(4)]
        s += [("pu", l, h) for h in range(ML_H)]
        s += [("pP", l, "B", t) for t in range(T)] + [("gates", l)]
        s += [("pP", l, "A", 0)] + [("gT", l, t) for t in range(T)] + [("pP", l, "A", 1), ("rows", l)]
        s += [("pP", l, "A", 2), ("cnorm", l, 0), ("pP", l, "A", 3), ("cnorm", l, 1), ("pP", l, "C", 0)]
        s += [("conv", l, 0), ("pP", l, "C", 1), ("cnorm", l, 2), ("cnorm", l, 3), ("conv", l, 1)]
        s += [("pP", l, "C", 2), ("nan", l, 0), ("nan", l, 1), ("conv", l, 2)]
        s += [("pP", l, "C", 3), ("nan", l, 2), ("conv", l, 3), ("cols", l)]
        s += [("mv", l, t) for t in range(T)] + [("pz", l, 0), ("nan", l, 3), ("pz", l, 1)]
        s += [("mqk", l, 0), ("nT", l, 0), ("pz", l, 2), ("mqk", l, 1), ("nT", l, 1), ("pz", l, 3)]
        s += [("mqk", l, 2), ("nT", l, 2), ("mqk", l, 3), ("nT", l, 3)]
        start = len(s)
        for h in range(ML_H):
            s += [("mst", l, h)]
            s += [("mgrid", l, h, d) for d in (0, 1)]
            s += [("mpv", l, h, d) for d in (0, 1)]
        s += [("mln", l)] + [("mlT", l, h) for h in range(ML_H)]
        prep = []
        for t in range(T):
            prep += [("cT", l, t), ("uqk", l, t)]
            if t:
                prep += [("uqn", l, t - 1), ("qkT", l, t - 1)]
        prep += [("uqn", l, T - 1), ("qkT", l, T - 1)]
        s += merge(prep, unit_steps(l, 1)) + unit_steps(l, 0)
        late = late_mods(l)
        fill = [[p] + ([("modT",) + late[i - 1][1:]] if i else []) for i, p in enumerate(late)]
        if fill:
            fill[-1].append(("modT",) + late[-1][1:])
        s[start:] = spread(s[start:], fill)
        if l == 0:
            s += [("modfin", 0, 2)] + [("modfin", m, w) for m in range(1, DEPTH) for w in (1, 2)]
        s += [("gbc", l, 1, st) for st in sq]
        s += [("wo", l, t) for t in tq]
        s += [("norm", l, 2, t) for t in tq]
        s += [("hT", l, 2, st, kp) for st in sq for kp in range(4)]
        s += [("router", l)] + [("h2T", l, t, n) for t in tq for n in (0, 1)] + [("gbc2", l), ("pfx", l)]
        s += [("xg", l, e) for e in (0, 1, 2)] + [("xT", l, 0), ("ab", l, 0), ("xT", l, 1)]
        for e in range(N_E):
            s += [("ab", l, e + 1)] if e + 1 < N_E else []
            s += [("y", l, e)]
            s += [("xg", l, e + 3)] if e + 3 < N_E else []
            s += [("ys", l, e)]
            s += [("xT", l, e + 2)] if e + 2 < N_E else []
        s += [("comb", l, t) for t in tq] + [("dense", l)]
        s += [("moe_out", l, t) for t in tq]
    return s


UNITS = [(b, l, t, h, h == nh - 1) for l in range(DEPTH) for b, nh in ((1, NA_H), (0, MLA_H))
         for t in tiles_q(l) for h in range(nh)]
UNIT_AT = {u: i for i, u in enumerate(UNITS)}


def build(nc, a):
    pieces = weight_pieces()
    piece_at = {p: i for i, p in enumerate(pieces)}
    SLOTS = 3
    schedule = make_schedule()

    RING = 6
    jobs = []
    last_job_of_piece = {}

    def add(key, piece=None):
        jobs.append(key)
        if piece is not None:
            last_job_of_piece[piece] = key

    for st in schedule:
        k, l = st[0], layer_of(st)
        if k == "mod":
            add(st, st)
        elif k == "modT":
            add(st)
        elif k == "hT":
            add(st)
        elif k == "pu":
            add(st, ("w_u", l))
        elif k == "pz":
            add(st, ("w_z", l))
        elif k == "pP":
            add(st, ("w_" + st[2], l))
        elif k in ("gT", "cols"):
            add(st)
        elif k == "mv":
            add(st)
        elif k == "mqk":
            add(st + ("q",))
            add(st + ("k",))
        elif k == "mst":
            for j in range(T):
                add(st + (j,))
        elif k == "mgrid":
            add(st)
        elif k == "mlT":
            add(st)
        elif k == "cT":
            add(st)
        elif k == "uqk":
            if st[2] in tiles_q(l):
                add(st + ("q", 0))
                add(st + ("q", 1))
            add(st + ("k", 0))
            add(st + ("k", 1))
        elif k == "qkT":
            if st[2] in tiles_q(l):
                add(st + ("q", 0))
                add(st + ("q", 1))
            add(st + ("k", 0))
            add(st + ("k", 1))
        elif k == "nT":
            add(st)
        elif k in ("S", "PV"):
            if k == "S":
                add(st)
            else:
                add(("ET",) + st[1:])
        elif k == "OT":
            add(st)
        elif k == "gbc":
            add(st + (0,))
            add(st + (1,))
        elif k == "wo":
            for n in (0, 1):
                add(st + (n,))
                for p in ("wo_mla", "wo_ml", "wo_na"):
                    last_job_of_piece[(p, l)] = st + (n,)
        elif k in ("router", "h2T", "pfx"):
            add(st)
        elif k == "xT":
            add(st + (0,))
            add(st + (1,))
        elif k == "gbc2":
            for s_ in sorted({t // 2 for t in tiles_q(l)}):
                add(st + (s_, 0))
                add(st + (s_, 1))
        elif k == "ab":
            add(st, ("w13", l, st[2]))
        elif k == "y":
            add(st + ("T",))
            add(st + (0,))
            add(st + (1,), ("w2", l, st[2]))
    job_at = {k: i for i, k in enumerate(jobs)}
    assert len(job_at) == len(jobs)
    acc_jobs = [st for st in schedule if st[0] == "mpv" or st[0] == "OT"]
    acc_at = {k: i for i, k in enumerate(acc_jobs)}
    pv_steps = [st for st in schedule if st[0] in ("mpv", "PV")]
    pv_at = {k: i + 1 for i, k in enumerate(pv_steps)}

    ctx = ExitStack()
    with ctx:
        def sb(name, cols, parts=P):
            return ctx.enter_context(nc.sbuf_tensor(name, [parts, cols], F32))

        def sem(name):
            return ctx.enter_context(nc.semaphore(name))

        bank = [ctx.enter_context(nc.psum_tensor(f"bank{i}", [P, 512], F32)) for i in range(8)]

        def view(reg, off, *shape, parts=P):
            n = int(np.prod(shape))
            ap = reg[0:parts, off:off + n]
            if len(shape) == 2:
                return ap.rearrange("p (a b) -> p a b", a=shape[0])
            if len(shape) == 3:
                return ap.rearrange("p (a b c) -> p a b c", a=shape[0], b=shape[1])
            return ap

        X = sb("X", T * D)
        Xv = view(X, 0, T, D)
        WORK = sb("WORK", 4096)
        XS = view(WORK, 0, T, D)
        H = sb("H", 4608)
        HT = view(H, 0, KD, TOK)
        MLAT = view(H, 0, 3, TOK)
        HS = view(H, 0, T, ML_W)
        MLT = view(H, 1536, ML_H, TOK, parts=ML_D)
        NAT = view(H, 3584, 2, TOK)
        PR = sb("PROJ", T * PW)
        PRv = view(PR, 0, T, PW)
        M = sb("BRANCH", 9984)
        UT = view(M, 0, ML_H, TOK, parts=ML_D)
        MQ = UT
        ZS = view(M, 2048, ML_H, TOK, parts=ML_D)
        UC = view(M, 4096, ML_H, TOK, parts=ML_D)
        MK = view(M, 6144, ML_H, TOK, parts=ML_D)
        MV = view(M, 8192, T, ML_H, 97)
        CT = view(M, 0, 3, TOK)
        QTM = [view(M, 1536 + 576 * i, MLA_H, QK_D) for i in (0, 1)]
        KTM = [view(M, 2688 + 576 * i, MLA_H, QK_D) for i in (0, 1)]
        QT = view(M, 3840, MLA_H, TOK, parts=QK_D)
        KT = view(M, 6912, MLA_H, TOK, parts=QK_D)
        VV = PRv[:, :, 0:MLA_H * V_D].rearrange("p t (h e) -> p t h e", h=MLA_H)
        XG = [view(M, 1024 * i, D) for i in (0, 1, 2)]
        OH = [view(M, 3072 + 64 * k, T * N_E) for k in (0, 1)]
        INCL = view(M, 3200, P)
        PICK = view(M, 3328, T * N_E)
        PROD = view(M, 3392, T * N_E)
        ASSIGN = view(M, 3456, T * N_E)
        TABS = view(M, 3520, N_E, 4)
        SLOTF = view(M, 3584, 2 * T)
        ACC = view(M, 0, T, D)
        GB = view(M, 4096, 2, D)
        HID = [view(M, 6144 + 256 * i, FF) for i in (0, 1)]
        HIDT = [view(M, 6656 + 256 * i, 2, P) for i in (0, 1)]
        TH = [view(M, 7168 + 256 * i, FF) for i in (0, 1)]
        YT = view(M, 7680, 512)
        YO = [view(M, 7680 + 1024 * i, D) for i in (0, 1)]
        N_R = sb("NA", 4096)
        XGT = [view(N_R, 1024 * i, KD, P) for i in (0, 1)]
        NQT = view(N_R, 0, 2, TOK)
        NKT = view(N_R, 1024, 2, TOK)
        BIAS = view(N_R, 2048, 2, NA_H, L)
        RINGW = sb("RINGW", SLOTS * 4096)
        W2R = sb("W2R", 2 * 2048)
        MROW = [W2R[0:2, 3072 + 512 * i:3584 + 512 * i] for i in (0, 1)]
        NEGMU = sb("NEGMU", 2 * TOK, ML_H)
        NEGMUv = view(NEGMU, 0, 2, TOK, parts=ML_H)
        ROW = view(WORK, 0, 4, TOK, parts=ML_H)
        GEM = view(WORK, 2048, 4, TOK, parts=ML_H)
        GRIDB = [view(WORK, 2048 * i, T, TOK) for i in (0, 1)]
        E = [view(WORK, 512 * i, TOK) for i in (0, 1)]
        PT = [view(WORK, 1024 + 512 * i, 4, P) for i in (0, 1)]
        OM = view(WORK, 2048, MLA_H * V_D)
        SQN = view(M, 6144, 512)
        SQC = view(M, 6656, 384)
        SQU = [view(WORK, 2432 + 576 * i, MLA_H, QK_D) for i in (0, 1)]
        SWAP = [view(WORK, 3584 + 192 * i, MLA_H, ROPE_D) for i in (0, 1)]
        IDENT = sb("IDENT", P)
        PACK = M[:, 9984 - 3 * P:9984]
        COLS = sb("COLS", 3 * P)
        MODC = sb("MODC", DEPTH * 96)
        MODv = [view(MODC, 96 * l, 48, 2) for l in range(DEPTH)]
        AMOD = sb("AMOD", DEPTH * 32)
        AMv = [view(AMOD, 32 * l, 2, KD, 2) for l in range(DEPTH)]
        CS = sb("CS", 16)
        CSv = CS[:, :].rearrange("p (j k) -> p k j", j=2)
        TRI = sb("TRI", 2 * P)
        ROPE = sb("ROPE", 2 * 2 * ROPE_D + 16 + 8 * T)
        RANK = ROPE[:, 2 * 2 * ROPE_D:2 * 2 * ROPE_D + 16]
        ENT = view(ROPE, 2 * 2 * ROPE_D + 16, T, 2, 4)
        ROv = view(ROPE, 0, 2, 2, ROPE_D)
        BC = sb("BC", 2 * 352 + 16)
        GEMC = sb("GEMC", 4 * T * ML_H)
        GC = view(GEMC, 0, 4, T, ML_H)
        ST = sb("ST", 256)
        PAD = sb("PAD", 128, 56)
        RWT = sb("RWT", KD * N_E)
        RW = view(RWT, 0, KD, N_E)
        GATE = sb("GATE", T * N_E)
        GATEv = view(GATE, 0, T, N_E)
        RT = sb("RT", 448)
        IDX = ctx.enter_context(nc.sbuf_tensor("IDX", [P, 2 * T + 2 * N_E + 1], U32))
        SLOTU = IDX[:, 0:2 * T]
        TOKU = IDX[:, 2 * T:2 * T + N_E]
        PAIRU = IDX[:, 2 * T + N_E:2 * T + 2 * N_E]
        OVER = IDX[:, 2 * T + 2 * N_E:2 * T + 2 * N_E + 1]
        assert nc.sbuf_bytes_remaining >= 0

        c2 = lambda r: COLS[:, P + r:P + r + 1]
        c96 = lambda r, n=1: COLS[0:ML_D, 2 * P + r:2 * P + r + n]
        bc_qg = lambda l: BC[:, 352 * l:352 * l + 96]
        bc_kg = lambda l: BC[:, 352 * l + 96:352 * l + 192]
        bc_nq = lambda l: BC[:, 352 * l + 192:352 * l + 256]
        bc_nk = lambda l: BC[:, 352 * l + 256:352 * l + 320]
        bc_gb = lambda l: BC[:, 352 * l + 320:352 * l + 336]
        bc_rb = BC[:, 704:720]

        SHIFT = 2 * GRID + 1
        BROW = GRID * SHIFT
        scratch = nc.dram_tensor("bias_rows", [2 * NA_H * 7, BROW], F32, kind="Internal").ap()

        h2_rows = nc.dram_tensor("h2_rows", [TOK, D], F32, kind="Internal").ap()
        slots = [nc.dram_tensor(f"slots_{l}", [CAP * N_E, 4], F32, kind="Internal").ap() for l in range(DEPTH)]
        pairs = nc.dram_tensor("pairs", [2 * TOK, D], F32, kind="Internal").ap()

        full = [sem(f"bank_full_{i}") for i in range(RING)]
        free = [sem(f"bank_free_{i}") for i in range(RING)]
        slot_loaded = [sem(f"slot_loaded_{i}") for i in range(SLOTS)]
        w2_loaded = [sem(f"w2_loaded_{i}") for i in range(2)]
        pack_loaded = sem("pack_loaded")
        params_loaded = sem("params_loaded")
        small_loaded = sem("small_loaded")
        x_loaded = sem("x_loaded")
        pad_loaded = sem("pad_loaded")
        rows_stored = sem("rows_stored")
        bias_loaded = [sem(f"bias_loaded_{l}") for l in range(DEPTH)]
        bias_masked = sem("bias_masked")
        const_ready = sem("const_ready")
        pack_zero = sem("pack_zero")
        cols_full = sem("cols_full")
        cols_ready = sem("cols_ready")
        csilu_ready = sem("csilu_ready")
        mod_ready = sem("mod_ready")
        ssq_ready = sem("ssq_ready")
        mean_ready = sem("mean_ready")
        rstd_ready = sem("rstd_ready")
        xs_ready = sem("xs_ready")
        lf_ready = sem("lf_ready")
        lfa_ready = sem("lfa_ready")
        gates_ready = sem("gates_ready")
        rows_ready = sem("rows_ready")
        mv_ready = sem("mv_ready")
        conv_acc = sem("conv_acc")
        conv_tanh = sem("conv_tanh")
        uc_ready = sem("uc_ready")
        diag_ready = sem("diag_ready")
        grid_exp = sem("grid_exp")
        grid_ready = sem("grid_ready")
        pv_done = sem("pv_done")
        acc_free = sem("acc_free")
        hn_ready = sem("hn_ready")
        zs_tanh = sem("zs_tanh")
        cn_ready = sem("cn_ready")
        usq_ready = sem("usq_ready")
        qk_ready = sem("qk_ready")
        na_ready = sem("na_ready")
        nmax_ready = sem("nmax_ready")
        exp_ready = sem("exp_ready")
        om_ready = sem("om_ready")
        resid_ready = sem("resid_ready")
        assign_ready = sem("assign_ready")
        moe_tanh = sem("moe_tanh")
        hid_ready = sem("hid_ready")
        out_ready = sem("out_ready")
        out_stored = sem("out_stored")
        em_in = sem("em_in")
        em_ready = sem("em_ready")
        gc_ready = sem("gc_ready")
        hn_used = sem("hn_used")
        mlt_ready = sem("mlt_ready")
        slots_blank = sem("slots_blank")
        h2_stored = sem("h2_stored")
        xg_blank = sem("xg_blank")
        pairs_blank = sem("pairs_blank")
        route_ready = sem("route_ready")
        slots_stored = sem("slots_stored")
        slots_loaded = sem("slots_loaded")
        index_ready = sem("index_ready")
        xg_loaded = [sem(f"xg_loaded_{i}") for i in range(3)]
        ys_stored = [sem(f"ys_stored_{i}") for i in range(2)]
        pair_loaded = [sem(f"pair_loaded_{i}") for i in range(T)]
        dn = [{w: sem(f"dense_{w}_{l}") for w in ("loaded", "ab", "tanh", "half", "hid", "T", "ht", "y", "acc",
                                                 "zero", "gate")} for l in range(DEPTH)]
        dve_step = sem("dve_step")
        act_step = sem("act_step")
        pool_step = sem("pool_step")

        block = ctx.enter_context(nc.Block())

        def bank_of(key):
            return bank[job_at[key] % RING]

        def full_of(key):
            n = job_at[key]
            return full[n % RING], n // RING + 1

        def free_of(key):
            n = job_at[key]
            return free[n % RING], n // RING + 1

        def slot(p):
            i = piece_at[p]
            return RINGW[:, 4096 * (i % SLOTS):4096 * (i % SLOTS + 1)]

        def loaded(p):
            i = piece_at[p]
            return slot_loaded[i % SLOTS], 16 * loads_upto[i]

        parts_of = {"w13": 2}
        loads_upto = []
        seen = [0] * SLOTS
        for i, p in enumerate(pieces):
            seen[i % SLOTS] += parts_of.get(p[0], 1)
            loads_upto.append(seen[i % SLOTS])

        def tick(eng, s):
            eng.sem_inc(s, 1)

        rstd_keys = []
        for s in schedule:
            if s[0] in ("norm", "mln", "cnorm"):
                rstd_keys.append(s)
            elif s[0] in ("uqk", "nan"):
                rstd_keys.append(s)
        rstd_at = {k: i + 1 for i, k in enumerate(rstd_keys)}
        ssq_keys = [s for s in schedule if s[0] in ("norm", "cnorm")]
        ssq_at = {k: i + 1 for i, k in enumerate(ssq_keys)}

        def order(kind):
            return {s: i + 1 for i, s in enumerate(x for x in schedule if x[0] == kind)}

        norm_n, mv_n, conv_n, mqk_n = order("norm"), order("mv"), order("conv"), order("mqk")
        grid_n, mlT_n, cn_n, uqk_n = order("mgrid"), order("mlT"), order("cnorm"), order("uqk")
        nan_n, wo_n, ab_n, y_n, pz_n = order("nan"), order("wo"), order("ab"), order("y"), order("pz")
        S_n, OT_n = order("S"), order("OT")
        mod_n, modfin_n = order("mod"), order("modfin")
        mod_key = {n: s for s, n in mod_n.items()}
        grid_key = {n: s for s, n in grid_n.items()}
        OT_key = {n: s for s, n in OT_n.items()}
        expert_n = lambda l, e: l * N_E + e
        expert_key = lambda n: (n // N_E, n % N_E)

        resid_at, c = {}, 0
        for s in schedule:
            if s[0] == "wo" or (s[0] == "moe_out" and s[1] < DEPTH - 1):
                c += 1
                resid_at[s] = c

        def resid_for(s):
            return resid_at[("wo", s[1], s[3])] if s[2] == 2 else resid_at[("moe_out", s[1] - 1, s[3])]

        def mpv_before(s):
            g = grid_key[grid_n[s] - 2]
            return pv_at[("mpv",) + g[1:]]

        def diagonal(s):
            t0 = tiles_q(s[1])[0]
            o = 2048 * (grid_n[s] % 2) + t0 * (TOK + P)
            b = WORK[:, o:o + P]
            return bass.AP(tensor=b.tensor, offset=b.offset,
                           ap=[list(b.ap[0]), [TOK + P, len(tiles_q(s[1]))], [1, P]])

        def conv_tmp(s):
            return WORK[0:ML_D, 512 * (s[2] % 2):512 * (s[2] % 2) + TOK]

        def ssq_cols(s):
            o = 176 + 2 * (ssq_at[s] % 4)
            return ST[:, o:o + 2]

        def neg_max(u):
            return ST[:, 192 + u % 4:193 + u % 4]

        def exp_sums(u, n):
            b, l, t, h, _ = UNITS[u]
            o = 200 + 8 * (OT_n[("OT", b, l, t, (MLA_H, NA_H)[b] - 1, True)] % 4) + h
            return ST[:, o:o + n]

        def stat(n, w=16):
            return ST[:, 16 * (n % 4):16 * (n % 4) + w], ST[:, 64 + 16 * (n % 4):64 + 16 * (n % 4) + w]

        POOL_HALF = RT[:, 432:448]

        def rstd_width(s):
            if s[0] == "norm":
                return 1
            if s[0] == "mln":
                return 4 * len(tiles_q(s[1]))
            if s[0] == "cnorm":
                return 2
            return 12 if s[0] == "uqk" else 8

        SMALL_PARTS = 5

        def small_views(l):
            s = W2R
            wq = s[0:ML_D, 0:384].rearrange("p (h e) -> p h e", h=ML_H)
            wk = s[0:ML_D, 384:768].rearrange("p (h e) -> p h e", h=ML_H)
            wv = s[0:ML_D, 768:1152].rearrange("p (h e) -> p h e", h=ML_H)
            uq = s[:, 1152:2304].rearrange("p (k n) -> p k n", k=2)
            ukv = s[:, 2304:3072]
            return wq, wk, wv, uq, ukv

        @block.sync
        def _(sp):
            sp.dma_start(Xv[:, 0:2, :], a["ctx"].rearrange("b (t p) d -> p (b t) d", p=P)).then_inc(x_loaded, 16)
            sp.dma_start(Xv[:, 2:4, :], a["x"].rearrange("b (t p) d -> p (b t) d", p=P)).then_inc(x_loaded, 16)
            w2_keys = [(l, e) for l in range(DEPTH) for e in range(N_E)]

            def dense_weights(l):
                nt = len(tiles_q(l))
                sp.wait_ge(route_ready, l + 1)
                over = sp.value_load(OVER[0:1, :])
                with sp.If(over > 0):
                    sp.wait_ge(*full_of(("y", l, N_E - 1, 1)))
                    with sp.Fori(0, N_E) as e:
                        sp.wait_ge(dn[l]["acc"], e * nt + 1)
                        w13 = RINGW[:, 0:4096].rearrange("p (k n) -> p k n", k=KD)
                        w2 = RINGW[:, 4096:6144].rearrange("p (k n) -> p k n", k=2)
                        sp.dma_start(w13[:, :, 0:FF], a["moe_w1"][l][e].rearrange("(k p) f -> p k f", p=P)).then_inc(
                            dn[l]["loaded"], 16)
                        sp.dma_start(w13[:, :, FF:2 * FF],
                                     a["moe_w3"][l][e].rearrange("(k p) f -> p k f", p=P)).then_inc(
                            dn[l]["loaded"], 16)
                        sp.dma_start(w2, a["moe_w2"][l][e].rearrange("(k p) n -> p k n", p=P)).then_inc(
                            dn[l]["loaded"], 16)
                    sp.wait_ge(dn[l]["acc"], N_E * nt + 1)

            for i, p in enumerate(pieces):
                if p[0] == "w_u" and p[1]:
                    dense_weights(p[1] - 1)
                if p[0] == "w_z":
                    if p[1]:
                        for e in (N_E - 2, N_E - 1):
                            sp.wait_ge(*full_of(last_job_of_piece[("w2", p[1] - 1, e)]))
                    wq, wk, wv, uq, ukv = small_views(p[1])
                    for w, name in ((wq, "ml_w_q"), (wk, "ml_w_k"), (wv, "ml_w_v")):
                        sp.dma_start(w, a[name][p[1]].rearrange("h d e -> d h e")).then_inc(small_loaded, 16)
                    sp.dma_start(uq, a["mla_w_uq"][p[1]].rearrange("(k p) n -> p k n", p=P)).then_inc(
                        small_loaded, 16)
                    sp.dma_start(ukv, a["mla_w_ukv"][p[1]]).then_inc(small_loaded, 16)
                if i >= SLOTS:
                    s, v = full_of(last_job_of_piece[pieces[i - SLOTS]])
                    sp.wait_ge(s, v)
                dst, k, l = slot(p), p[0], p[1]
                done = slot_loaded[i % SLOTS]
                w_in = a["w_in"][l].rearrange("(k p) n -> p k n", p=P)
                if k == "mod":
                    c = 512 * p[2]
                    sp.dma_start(dst.rearrange("p (k n) -> p k n", k=KD),
                                 a["w_mod"][l].rearrange("(k p) n -> p k n", p=P)[:, :, c:c + 512]).then_inc(done, 16)
                elif k in ("w_u", "w_z", "w_A", "w_B", "w_C"):
                    c, n = {"w_u": (OFF_U, ML_W), "w_z": (OFF_Z, ML_W)}.get(k) or CHUNK[k[-1]][:2]
                    sp.dma_start(dst[:, 0:KD * n].rearrange("p (k n) -> p k n", k=KD),
                                 w_in[:, :, c:c + n]).then_inc(done, 16)
                elif k == "wo_mla":
                    sp.dma_start(dst[:, 0:3 * D].rearrange("p (k n) -> p k n", k=3),
                                 a["w_out"][l][0:384, :].rearrange("(k p) n -> p k n", p=P)).then_inc(done, 16)
                elif k == "wo_ml":
                    sp.dma_start(dst[0:ML_D, :].rearrange("p (k n) -> p k n", k=ML_H),
                                 a["w_out"][l][384:768, :].rearrange("(k p) n -> p k n", p=ML_D)).then_inc(done, 16)
                elif k == "wo_na":
                    sp.dma_start(dst[:, 0:2 * D].rearrange("p (k n) -> p k n", k=2),
                                 a["w_out"][l][768:1024, :].rearrange("(k p) n -> p k n", p=P)).then_inc(done, 16)
                else:
                    e = p[2]
                    w13 = dst.rearrange("p (k n) -> p k n", k=KD)
                    sp.dma_start(w13[:, :, 0:FF], a["moe_w1"][l, e].rearrange("(k p) f -> p k f", p=P)).then_inc(
                        done, 16)
                    sp.dma_start(w13[:, :, FF:2 * FF], a["moe_w3"][l, e].rearrange("(k p) f -> p k f", p=P)).then_inc(
                        done, 16)
                    n = w2_keys.index((l, e))
                    if e >= 2:
                        sp.wait_ge(*full_of(last_job_of_piece[("w2",) + w2_keys[n - 2]]))
                    elif e == 0:
                        sp.wait_ge(*full_of(("uqk", l, T - 1, "k", 1)))
                        for m in late_mods(l)[-2:]:
                            sp.wait_ge(*full_of(("modT",) + m[1:]))
                    sp.dma_start(W2R[:, 2048 * (n % 2):2048 * (n % 2 + 1)].rearrange("p (k n) -> p k n", k=2),
                                 a["moe_w2"][l, e].rearrange("(k p) n -> p k n", p=P)).then_inc(w2_loaded[n % 2], 16)
            dense_weights(DEPTH - 1)
            for i in range(2):
                sp.wait_ge(out_ready, i + 1)
                sp.dma_start(a["out"][0, i * P:(i + 1) * P, :], Xv[:, 2 + i, :]).then_inc(out_stored, 16)
            sp.wait_ge(out_stored, 32)

        def w2_of(l, e):
            n = l * N_E + e
            return (W2R[:, 2048 * (n % 2):2048 * (n % 2 + 1)].rearrange("p (k n) -> p k n", k=2),
                    w2_loaded[n % 2], 16 * (n // 2 + 1))

        @block.gpsimd
        def _(pool):
            step = [0]

            def link(ins):
                step[0] += 1
                ins.then_inc(pool_step, 1)
                pool.wait_ge(pool_step, step[0])

            link(pool.memset(IDENT[:, :], 0.0))
            link(pool.affine_select(out=IDENT[:, :], in_=IDENT[:, :], compare_op=ALU.not_equal, fill=1.0, base=0,
                                    pattern=[[-1, P]], channel_multiplier=1))
            link(pool.memset(TRI[:, :], 0.0))
            link(pool.affine_select(out=TRI[:, 0:P], in_=TRI[:, 0:P], compare_op=ALU.is_ge, fill=NEG, base=0,
                                    pattern=[[1, P]], channel_multiplier=-1))
            link(pool.affine_select(out=TRI[:, P:2 * P], in_=TRI[:, P:2 * P], compare_op=ALU.is_ge, fill=NEG,
                                    base=0, pattern=[[-1, P]], channel_multiplier=1))
            link(pool.memset(POOL_HALF, -0.5))
            link(pool.memset(PAD[:, :], 0.0))
            pool.memset(PACK[:, :], 0.0).then_inc(const_ready, 1)
            pool.wait_ge(const_ready, 1)
            for l in range(DEPTH):
                for dst, name in ((bc_qg(l), "mla_q_g"), (bc_kg(l), "mla_k_g"), (bc_nq(l), "na_q_g"),
                                  (bc_nk(l), "na_k_g"), (bc_gb(l), "ml_gate_b")):
                    pool.dma_start(dst, a[name][l].partition_broadcast(P)).then_inc(params_loaded, 16)
            pool.dma_start(bc_rb, a["router_b"].partition_broadcast(P)).then_inc(params_loaded, 16)
            pool.dma_start(RW, a["router_w"].rearrange("(k p) n -> p k n", p=P)).then_inc(params_loaded, 16)
            pool.dma_start(ROPE[:, :], a["rope"]).then_inc(params_loaded, 16)
            blank = view(M, 0, N_E, 4)
            link(pool.memset(blank, NOWHERE))
            link(pool.memset(blank[:, :, 1:2], 0.0))
            for l in range(DEPTH):
                pool.dma_start(slots[l].rearrange("(p e) c -> p e c", e=N_E), blank).then_inc(slots_blank, 16)
            lo = GRID - 1 - (WIN_C - 1)
            for l in range(DEPTH):
                for h in range(NA_H):
                    pool.dma_start(PAD[28 * l + 7 * h:28 * l + 7 * h + 7, lo:lo + 2 * WIN_C - 1],
                                   a["na_rpb"][l, h, WIN_R - ROWS:WIN_R + ROWS - 1, :]).then_inc(pad_loaded, 16)
            pool.wait_ge(pad_loaded, 16 * DEPTH * NA_H)
            pool.dma_start(scratch.rearrange("r (c i) -> r c i", i=SHIFT)[:, :, 0:2 * GRID - 1],
                           PAD[:, 0:2 * GRID - 1].unsqueeze(1).broadcast_to([2 * NA_H * 7, GRID, 2 * GRID - 1])
                           ).then_inc(rows_stored, 16)
            pool.wait_ge(rows_stored, 16)
            pool.wait_ge(slots_blank, 16 * DEPTH)

            def load_bias(l):
                for r in range(ROWS):
                    for h in range(NA_H):
                        src = bass.AP(tensor=scratch.tensor,
                                      offset=(28 * l + 7 * h + ROWS - 1 - r) * BROW + GRID - 1,
                                      ap=[[2 * GRID, GRID], [BROW, ROWS], [1, GRID]])
                        q0 = (r % 2) * GRID
                        pool.dma_start(BIAS[q0:q0 + GRID, r // 2, h, :].rearrange("p (j c) -> p j c", j=ROWS),
                                       src).then_inc(bias_loaded[l], 16)
                pool.wait_ge(bias_loaded[l], 16 * ROWS * NA_H)
                for q0 in (0, GRID):
                    b = N_R[q0:q0 + GRID, 2048:4096].rearrange("p (m c) -> p m c", c=GRID)
                    lowc = GRID - WIN_C
                    link(pool.affine_select(out=b[:, :, 0:lowc], in_=b[:, :, 0:lowc], compare_op=ALU.is_ge, fill=NEG,
                                            base=WIN_C // 2, pattern=[[0, 32], [1, lowc]], channel_multiplier=-1))
                    ins = pool.affine_select(out=b[:, :, WIN_C:], in_=b[:, :, WIN_C:], compare_op=ALU.is_ge,
                                             fill=NEG, base=WIN_C // 2 - 1 - WIN_C,
                                             pattern=[[0, 32], [-1, lowc]], channel_multiplier=1)
                    ins.then_inc(bias_masked, 1)
                    pool.wait_ge(bias_masked, 2 * l + (1 if q0 == 0 else 2))

            for s in schedule:
                if s in rstd_at:
                    m, r = stat(rstd_at[s])
                    w = rstd_width(s)
                    pool.wait_ge(mean_ready, rstd_at[s])
                    pool.tensor_tensor(r[:, 0:w], m[:, 0:w], POOL_HALF[:, 0:w], ALU.pow).then_inc(rstd_ready, 1)
                k, l = s[0], layer_of(s)
                if k == "gates":
                    if l:
                        pool.wait_ge(nmax_ready, max(UNIT_AT[u] for u in UNITS if u[1] == l - 1) + 1)
                    load_bias(l)
                elif k == "router":
                    pool.wait_ge(resid_ready, resid_at[("wo", l, T - 1)])
                    pool.memset(M[:, 0:3072], 0.0).then_inc(xg_blank, 1)
                    pool.wait_ge(xg_blank, l + 1)
                    if l == 0:
                        pool.dma_start(pairs.rearrange("(j p) d -> p j d", p=P),
                                       XG[2].unsqueeze(1).broadcast_to([P, 2 * T, D])).then_inc(pairs_blank, 16)
                elif k == "pfx":
                    pool.wait_ge(route_ready, l + 1)
                    nt = len(tiles_q(l))
                    for i, t in enumerate(tiles_q(l)):
                        for c in (0, 1):
                            pool.indirect_dma_start(
                                slots[l], bass.IndirectOffsetOnAxis(ap=SLOTU[:, 2 * i + c:2 * i + c + 1], axis=0),
                                ENT[:, t, c, :], None, bounds_check=CAP * N_E - 1, oob_is_err=False).then_inc(
                                slots_stored, 16)
                    pool.wait_ge(slots_stored, 32 * sum(len(tiles_q(m)) for m in range(l + 1)))
                    pool.dma_start(TABS, slots[l].rearrange("(p e) c -> p e c", e=N_E)).then_inc(slots_loaded, 16)
                elif k == "xg":
                    e = s[2]
                    n = expert_n(l, e)
                    if e == 0:
                        pool.wait_ge(index_ready, l + 1)
                        pool.wait_ge(h2_stored, 16 * sum(len(tiles_q(m)) for m in range(l + 1)))
                    if e == 2:
                        pool.wait_ge(pairs_blank, 16)
                    if e >= 3:
                        pool.wait_ge(*full_of(("xT", l, e - 3, 1)))
                    pool.indirect_dma_start(XG[n % 3], None, h2_rows,
                                            bass.IndirectOffsetOnAxis(ap=TOKU[:, e:e + 1], axis=0),
                                            bounds_check=TOK - 1, oob_is_err=False).then_inc(xg_loaded[n % 3], 16)
                elif k == "ys":
                    e = s[2]
                    n = expert_n(l, e)
                    pool.wait_ge(*free_of(("y", l, e, 0)))
                    pool.wait_ge(*free_of(("y", l, e, 1)))
                    pool.indirect_dma_start(pairs, bass.IndirectOffsetOnAxis(ap=PAIRU[:, e:e + 1], axis=0),
                                            YO[n % 2], None, bounds_check=2 * TOK - 1, oob_is_err=False).then_inc(
                        ys_stored[n % 2], 16)

        @block.scalar
        def _(act):
            step = [0]

            def link(ins):
                step[0] += 1
                ins.then_inc(act_step, 1)
                act.wait_ge(act_step, step[0])

            act.wait_ge(const_ready, 1)

            def pack(r0, r1, c, n, src):
                act.dma_start(PACK[r0:r1, c:c + n], src).then_inc(pack_loaded, 16)

            pack(0, 8, P, P, a["c_ctx"].rearrange("(r p) -> r p", p=P))
            pack(8, 16, P, P, a["c"][0].rearrange("(r p) -> r p", p=P))
            for l in range(DEPTH):
                r = 64 * l
                pack(r, r + 48, 0, P, a["b_mod"][l].rearrange("(r p) -> r p", p=P))
                pack(r + 48, r + 56, 0, P, a["norm1_g"][l].rearrange("(r p) -> r p", p=P))
                pack(r + 56, r + 64, 0, P, a["norm2_g"][l].rearrange("(r p) -> r p", p=P))
                pack(16 + 3 * l, 18 + 3 * l, P, P, a["mla_qnorm_g"][l].rearrange("(r p) -> r p", p=P))
                pack(18 + 3 * l, 19 + 3 * l, P, P, a["mla_kvnorm_g"][l:l + 1, :])
                q = 24 * l
                for o, name in ((0, "ml_norm_g"), (4, "ml_skip"), (8, "ml_conv_b")):
                    pack(q + o, q + o + 4, 2 * P, ML_D, a[name][l].rearrange("(r p) -> r p", p=ML_D))
                pack(q + 12, q + 24, 2 * P, ML_D, a["ml_conv_w"][l].rearrange("k (r p) -> (k r) p", p=ML_D))
            act.wait_ge(cols_ready, 1)
            act.activation(RT[:, 0:16], COLS[:, P:P + 16], ACT.Tanh, scale=0.5).then_inc(csilu_ready, 1)
            for s in schedule:
                k, l = s[0], layer_of(s)
                if k == "mod":
                    n = mod_n[s]
                    act.wait_ge(*full_of(s))
                    if n > 2:
                        act.wait_ge(*full_of(("modT",) + mod_key[n - 2][1:]))
                    act.activation(MROW[n % 2], bank_of(s)[0:2, :], ACT.Copy).then_inc(free_of(s)[0], 1)
                elif k == "norm":
                    t = s[3]
                    if (l, s[2]) == (0, 1):
                        act.wait_ge(x_loaded, 32)
                    else:
                        act.wait_ge(resid_ready, resid_for(s))
                    if ssq_at[s] > 4:
                        act.wait_ge(mean_ready, rstd_at[ssq_keys[ssq_at[s] - 5]])
                    m = ssq_cols(s)
                    act.activation(XS[:, t, :], Xv[:, t, :], ACT.Square, accum_out=m[:, 0:1]).then_inc(ssq_ready, 1)
                elif k == "hT" and s[4] % 2:
                    _, _, w, st, kp = s
                    act.wait_ge(*full_of(s))
                    act.wait_ge(mod_ready, modfin_n[("modfin", l, w)])
                    for i in (0, 1):
                        kk = 2 * kp + i
                        ins = act.activation(HT[:, kk, st * L:(st + 1) * L], bank_of(s)[:, i * L:(i + 1) * L],
                                             ACT.Identity, scale=AMv[l][:, w - 1, kk, st:st + 1],
                                             bias=MODv[l][:, 24 * (w - 1) + kk, st:st + 1])
                    ins.then_inc(free_of(s)[0], 1)
                elif k == "pu" and s[2] % 2:
                    act.wait_ge(*full_of(s))
                    act.activation(UT[:, s[2], :], bank_of(s)[0:ML_D, :], ACT.Copy).then_inc(free_of(s)[0], 1)
                elif k == "pP" and s[3] % 2:
                    act.wait_ge(*full_of(s))
                    c, n = p_cols(s)
                    act.activation(PRv[:, s[3], c:c + n], bank_of(s)[:, 0:n], ACT.Copy).then_inc(free_of(s)[0], 1)
                elif k == "pz":
                    act.wait_ge(*full_of(s))
                    c0 = 0 if l < DEPTH - 1 else L
                    act.activation(ZS[:, s[2], c0:TOK], bank_of(s)[0:ML_D, c0:TOK], ACT.Tanh, scale=0.5).then_inc(
                        zs_tanh, 1)
                elif k == "rows":
                    act.wait_ge(lfa_ready, l + 1)
                    fa = GEM[:, 0:2, :]
                    link(act.activation(fa, fa, ACT.Exp, scale=-1.0))
                    act.activation(fa, fa, ACT.Ln, bias=1.0).then_inc(lf_ready, 1)
                    act.wait_ge(em_in, l + 1)
                    act.activation(GEM[:, 2:4, :], GEM[:, 2:4, :], ACT.Exp, scale=-1.0).then_inc(em_ready, 1)
                elif k == "mv" and s[2] % 2:
                    act.wait_ge(*full_of(s))
                    act.activation(MV[:, s[2], :, 0:ML_D],
                                   bank_of(s)[:, 0:ML_W].rearrange("p (h e) -> p h e", h=ML_H),
                                   ACT.Copy).then_inc(free_of(s)[0], 1)
                elif k == "conv":
                    act.wait_ge(conv_acc, conv_n[s])
                    act.activation(conv_tmp(s), UC[:, s[2], :], ACT.Tanh).then_inc(conv_tanh, 1)
                elif k == "mqk":
                    key = s + ("k",)
                    act.wait_ge(*full_of(key))
                    if s[2] == 0:
                        act.wait_ge(na_ready, T * (l + 1))
                    act.activation(MK[:, s[2], :], bank_of(key)[0:ML_D, :], ACT.Copy,
                                   scale=ML_D ** -0.5).then_inc(free_of(key)[0], 1)
                elif k == "mgrid":
                    _, _, h, d = s
                    g = GRIDB[grid_n[s] % 2]
                    mu = bank_of(s)
                    act.wait_ge(*full_of(s))
                    if grid_n[s] > 2:
                        act.wait_ge(pv_done, mpv_before(s))
                    act.wait_ge(diag_ready, grid_n[s])
                    act.wait_ge(gc_ready, l + 1)
                    for j in range(T):
                        for t0, t1 in runs(l, d, j, False):
                            act.activation(g[:, j, t0 * P:t1 * P], mu[:, t0 * P:t1 * P], ACT.Exp,
                                           bias=GC[:, d, j, h:h + 1])
                    act.activation(diagonal(s), diagonal(s), ACT.Exp).then_inc(grid_exp, 1)
                elif k == "cnorm":
                    t = s[2]
                    m = ssq_cols(s)
                    act.wait_ge(*free_of(("pP", l, "A", t)))
                    if s[2] == 0 and l:
                        act.wait_ge(resid_ready, resid_at[("moe_out", l - 1, T - 1)])
                    act.wait_ge(mean_ready, rstd_at[ssq_keys[ssq_at[s] - 5]])
                    act.wait_ge(ssq_ready, ssq_at[s] - 1)
                    if t in tiles_q(l):
                        link(act.activation(SQC[:, 0:Q_RANK], PRv[:, t, 0:Q_RANK], ACT.Square,
                                            accum_out=m[:, 0:1]))
                    act.activation(SQC[:, Q_RANK:384], PRv[:, t, Q_RANK:384], ACT.Square,
                                   accum_out=m[:, 1:2]).then_inc(ssq_ready, 1)
                elif k == "uqk":
                    t = s[2]
                    isq = t in tiles_q(l)
                    if t >= 2:
                        for key in qkT_jobs(("qkT", l, t - 2)):
                            act.wait_ge(*full_of(key))
                    if isq:
                        for i in (0, 1):
                            key = s + ("q", i)
                            act.wait_ge(*full_of(key))
                            act.activation(QTM[t % 2][:, 3 * i:3 * i + 3, :],
                                           bank_of(key)[:, 0:288].rearrange("p (h e) -> p h e", h=3),
                                           ACT.Copy).then_inc(free_of(key)[0], 1)
                    kt = KTM[t % 2]
                    link(act.activation(kt[:, :, NOPE_D:], PRv[:, t, 384:416].unsqueeze(1).broadcast_to(
                        [P, MLA_H, ROPE_D]), ACT.Copy))
                    key = s + ("k", 1)
                    act.wait_ge(*full_of(key))
                    kvv = bank_of(key)[:, 0:384].rearrange("p (h e) -> p h e", h=3)
                    act.activation(kt[:, 3:6, 0:NOPE_D], kvv[:, :, 0:NOPE_D], ACT.Copy)
                    act.activation(VV[:, t, 3:6, :], kvv[:, :, NOPE_D:], ACT.Copy).then_inc(free_of(key)[0], 1)
                    act.wait_ge(mean_ready, rstd_at[s] - 1)
                    if isq:
                        for i in (0, 1):
                            act.wait_ge(*free_of(s + ("q", i)))
                        act.activation(SQU[0], QTM[t % 2], ACT.Square)
                    for i in (0, 1):
                        act.wait_ge(*free_of(s + ("k", i)))
                    act.activation(SQU[1], kt, ACT.Square).then_inc(usq_ready, 1)
                elif k == "nT":
                    t = s[2]
                    act.wait_ge(*full_of(s))
                    bk = bank_of(s)[:, :].rearrange("p (a t) -> p a t", a=4)
                    if t in tiles_q(l):
                        act.activation(NQT[:, :, t * P:(t + 1) * P], bk[:, 0:2, :], ACT.Copy)
                    act.activation(NKT[:, :, t * P:(t + 1) * P], bk[:, 2:4, :], ACT.Copy).then_inc(free_of(s)[0], 1)
                elif k == "qkT":
                    for key in qkT_jobs(s):
                        if key[3] == "k":
                            act.wait_ge(*full_of(key))
                            hh = 3 * key[4]
                            act.activation(KT[:, hh:hh + 3, s[2] * P:(s[2] + 1) * P],
                                           bank_of(key)[0:QK_D, 0:384].rearrange("p (h t) -> p h t", h=3),
                                           ACT.Copy).then_inc(free_of(key)[0], 1)
                elif k == "S":
                    u = UNIT_AT[s[1:]]
                    nk = keys_of(s)
                    act.wait_ge(nmax_ready, u + 1)
                    if u >= 2:
                        act.wait_ge(*full_of(("ET",) + UNITS[u - 2]))
                    act.activation(E[u % 2][:, 0:nk], bank_of(s)[:, 0:nk], ACT.Exp, bias=neg_max(u),
                                   accum_out=exp_sums(u, 1)).then_inc(free_of(s)[0], 1)
                elif k == "router":
                    act.wait_ge(*full_of(s))
                    nt = len(tiles_q(l))
                    act.activation(RT[:, 0:16 * nt], bank_of(s)[:, 0:16 * nt], ACT.Tanh, scale=0.5).then_inc(
                        free_of(s)[0], 1)
                elif k == "gbc":
                    for i in (0, 1):
                        act.wait_ge(*full_of(s + (i,)))
                        act.activation(GB[:, s[3], 512 * i:512 * i + 512], bank_of(s + (i,))[:, :],
                                       ACT.Copy).then_inc(free_of(s + (i,))[0], 1)
                elif k == "gbc2":
                    act.wait_ge(resid_ready, resid_at[("wo", l, tiles_q(l)[-1])])
                    for st in sorted({t // 2 for t in tiles_q(l)}):
                        for i in (0, 1):
                            key = s + (st, i)
                            act.wait_ge(*full_of(key))
                            act.activation(GB[:, st, 512 * i:512 * i + 512], bank_of(key)[:, :],
                                           ACT.Copy).then_inc(free_of(key)[0], 1)
                elif k == "h2T":
                    _, _, t, n = s
                    act.wait_ge(*full_of(s))
                    act.activation(XS[:, t, 512 * n:512 * n + 512], bank_of(s)[:, :], ACT.Copy).then_inc(
                        free_of(s)[0], 1)
                    if n:
                        for i in (0, 1):
                            act.wait_ge(*free_of(("h2T", l, t, i)))
                        act.dma_start(h2_rows[t * P:(t + 1) * P, :], XS[:, t, :]).then_inc(h2_stored, 16)
                elif k == "xT":
                    n = expert_n(l, s[2])
                    act.wait_ge(*full_of(s + (1,)))
                    if n >= 2:
                        act.wait_ge(*full_of(("ab",) + expert_key(n - 2)))
                    act.activation(XGT[n % 2][:, 4:8, :].rearrange("p k t -> p (k t)"), bank_of(s + (1,))[:, :],
                                   ACT.Copy).then_inc(free_of(s + (1,))[0], 1)
                elif k == "ab":
                    act.wait_ge(*full_of(s))
                    n = ab_n[s]
                    if n > 2:
                        act.wait_ge(hid_ready, n - 2)
                    act.activation(TH[n % 2], bank_of(s)[:, 0:FF], ACT.Tanh, scale=0.5).then_inc(moe_tanh, 1)
                elif k == "y":
                    key = s + ("T",)
                    e = s[2]
                    n = y_n[s]
                    act.wait_ge(*full_of(key))
                    if n > 2:
                        act.wait_ge(*full_of(("y",) + expert_key(n - 3) + (1,)))
                    act.activation(HIDT[n % 2].rearrange("p k t -> p (k t)"), bank_of(key)[:, 0:FF],
                                   ACT.Copy).then_inc(free_of(key)[0], 1)
                    key = s + (1,)
                    n = expert_n(l, e)
                    act.wait_ge(*full_of(key))
                    if n >= 2:
                        act.wait_ge(ys_stored[n % 2], 16 * (n // 2))
                    act.activation(YO[n % 2][:, 512:1024], bank_of(key)[:, :], ACT.Copy).then_inc(
                        free_of(key)[0], 1)
                elif k == "comb":
                    t = s[2]
                    n = expert_n(l, N_E)
                    act.wait_ge(ys_stored[0], 16 * ((n + 1) // 2))
                    act.wait_ge(ys_stored[1], 16 * (n // 2))
                    act.dma_start(ACC[:, t, :], pairs[t * P:(t + 1) * P, :]).then_inc(pair_loaded[t], 16)
                    act.dma_start(XS[:, t, :], pairs[TOK + t * P:TOK + (t + 1) * P, :]).then_inc(pair_loaded[t], 16)
                elif k == "dense":
                    nt = len(tiles_q(l))
                    over = act.value_load(OVER[0:1, :])
                    with act.If(over > 0):
                        with act.Fori(0, N_E) as e:
                            for i in range(nt):
                                act.wait_ge(dn[l]["ab"], e * nt + (i + 1))
                                act.activation(TH[0], bank[0][:, 0:FF], ACT.Tanh, scale=0.5).then_inc(
                                    dn[l]["tanh"], 1)

        @block.tensor
        def _(pe):
            def open_bank(key):
                n = job_at[key]
                if n >= RING:
                    pe.wait_ge(free[n % RING], n // RING)

            def flip(out, in_):
                k = in_.shape[0]
                return pe.transpose(out, in_, IDENT[0:k, 0:k])

            def open_acc(key):
                n = acc_at[key]
                if n >= 2:
                    pe.wait_ge(acc_free, n - 1)
                return bank[6 + n % 2]

            pe.wait_ge(pack_loaded, 16 * PACK_DMAS)
            pe.wait_ge(const_ready, 1)
            for i in range(3):
                ins = flip(bank[6][:, i * P:(i + 1) * P], PACK[:, i * P:(i + 1) * P])
            ins.then_inc(cols_full, 1)
            pe.wait_ge(csilu_ready, 2)
            for s in schedule:
                k, l = s[0], layer_of(s)
                tq = tiles_q(l)
                c0 = 0 if l < DEPTH - 1 else L
                if k == "mod":
                    open_bank(s)
                    pe.wait_ge(*loaded(s))
                    w = slot(s).rearrange("p (k n) -> p k n", k=KD)
                    for kk in range(KD):
                        ins = pe.matmul(bank_of(s)[0:2, :], CSv[:, kk, :], w[:, kk, :], start=kk == 0,
                                        stop=kk == KD - 1)
                    ins.then_inc(full_of(s)[0], 1)
                elif k == "modT":
                    key = ("mod",) + s[1:]
                    open_bank(s)
                    pe.wait_ge(*free_of(key))
                    for c in range(4):
                        ins = flip(bank_of(s)[:, 2 * c:2 * c + 2], MROW[mod_n[key] % 2][:, c * P:(c + 1) * P])
                    ins.then_inc(full_of(s)[0], 1)
                elif k == "hT":
                    _, _, w, st, kp = s
                    open_bank(s)
                    pe.wait_ge(xs_ready, norm_n[("norm", l, w, 2 * st + 1)])
                    for i in (0, 1):
                        for tt in (0, 1):
                            kk = 2 * kp + i
                            ins = flip(bank_of(s)[:, i * L + tt * P:i * L + (tt + 1) * P],
                                       XS[:, 2 * st + tt, kk * P:(kk + 1) * P])
                    ins.then_inc(full_of(s)[0], 1)
                elif k in ("pu", "pz"):
                    open_bank(s)
                    piece = ("w_" + k[1], l)
                    pe.wait_ge(*loaded(piece))
                    if k == "pu" and s[2] == 0:
                        for st in (0, 1):
                            for kp in range(4):
                                pe.wait_ge(*free_of(("hT", l, 1, st, kp)))
                    w = slot(piece)[:, 0:KD * ML_W].rearrange("p (k n) -> p k n", k=KD)
                    b0 = 0 if k == "pu" else c0
                    for kk in range(KD):
                        ins = pe.matmul(bank_of(s)[0:ML_D, b0:TOK], w[:, kk, s[2] * ML_D:(s[2] + 1) * ML_D],
                                        HT[:, kk, b0:TOK], start=kk == 0, stop=kk == KD - 1)
                    ins.then_inc(full_of(s)[0], 1)
                elif k == "pP":
                    _, _, w, t = s
                    open_bank(s)
                    pe.wait_ge(*loaded(("w_" + w, l)))
                    n = CHUNK[w][1]
                    wv = slot(("w_" + w, l))[:, 0:KD * n].rearrange("p (k n) -> p k n", k=KD)
                    c, nn = p_cols(s)
                    off = c - CHUNK[w][2]
                    for kk in range(KD):
                        ins = pe.matmul(bank_of(s)[:, 0:nn], HT[:, kk, t * P:(t + 1) * P], wv[:, kk, off:off + nn],
                                        start=kk == 0, stop=kk == KD - 1)
                    ins.then_inc(full_of(s)[0], 1)
                elif k == "gT":
                    t = s[2]
                    open_bank(s)
                    pe.wait_ge(gates_ready, l + 1)
                    for q in range(4):
                        ins = flip(bank_of(s)[0:ML_H, q * P:(q + 1) * P], PRv[:, t, PG + 4 * q:PG + 4 * q + 4])
                    ins.then_inc(full_of(s)[0], 1)
                elif k == "cols":
                    open_bank(s)
                    pe.wait_ge(rows_ready, l + 1)
                    for q in range(4):
                        for t in range(T):
                            o = (q * T + t) * ML_H
                            ins = flip(bank_of(s)[:, o:o + ML_H], GEM[:, q, t * P:(t + 1) * P])
                    ins.then_inc(full_of(s)[0], 1)
                elif k == "mv":
                    t = s[2]
                    open_bank(s)
                    pe.wait_ge(small_loaded, 16 * SMALL_PARTS * (l + 1))
                    if t == 0:
                        for h in range(ML_H):
                            pe.wait_ge(*free_of(("pu", l, h)))
                    wv = small_views(l)[2]
                    for h in range(ML_H):
                        ins = pe.matmul(bank_of(s)[:, h * ML_D:(h + 1) * ML_D], UT[:, h, t * P:(t + 1) * P],
                                        wv[:, h, :], start=True, stop=True)
                    ins.then_inc(full_of(s)[0], 1)
                elif k == "mqk":
                    h = s[2]
                    wq, wk = small_views(l)[0:2]
                    pe.wait_ge(uc_ready, conv_n[("conv", l, h)])
                    open_bank(s + ("q",))
                    pe.matmul(bank_of(s + ("q",))[0:ML_D, c0:TOK], wq[:, h, :], UC[:, h, c0:TOK], start=True,
                              stop=True).then_inc(full_of(s + ("q",))[0], 1)
                    open_bank(s + ("k",))
                    pe.matmul(bank_of(s + ("k",))[0:ML_D, :], wk[:, h, :], UC[:, h, :], start=True,
                              stop=True).then_inc(full_of(s + ("k",))[0], 1)
                elif k == "mst":
                    h = s[2]
                    pe.wait_ge(*free_of(("mqk", l, h, "q")))
                    pe.wait_ge(*free_of(("mqk", l, h, "k")))
                    for j in range(T):
                        q0 = c0 if j < 2 else L
                        open_bank(s + (j,))
                        pe.matmul(bank_of(s + (j,))[:, q0:TOK], MK[:, h, j * P:(j + 1) * P], MQ[:, h, q0:TOK],
                                  start=True, stop=True).then_inc(full_of(s + (j,))[0], 1)
                elif k == "mgrid":
                    open_bank(s)
                    pe.wait_ge(rows_ready, l + 1)
                    pe.matmul(bank_of(s)[:, c0:TOK], IDENT[0:ML_H, s[2]:s[2] + 1].broadcast_to([ML_H, P]), NEGMUv[:, s[3], c0:TOK], start=True,
                              stop=True).then_inc(full_of(s)[0], 1)
                elif k == "mpv":
                    _, _, h, d = s
                    acc = open_acc(s)
                    pe.wait_ge(grid_ready, grid_n[("mgrid", l, h, d)])
                    if h == 0 and d == 0:
                        for t in range(T):
                            pe.wait_ge(*free_of(("mv", l, t)))
                        pe.wait_ge(mv_ready, l + 1)
                    g = GRIDB[grid_n[("mgrid", l, h, d)] % 2]
                    for t in tq:
                        js = [j for j in range(T) if allowed(d, t, j)]
                        for j in js:
                            ins = pe.matmul(acc[:, t * 97:t * 97 + 97], g[:, j, t * P:(t + 1) * P],
                                            MV[:, j, h, :], start=j == js[0], stop=j == js[-1])
                    ins.then_inc(pv_done, 1)
                elif k == "mlT":
                    h = s[2]
                    open_bank(s)
                    pe.wait_ge(hn_ready, l + 1)
                    for t in tq:
                        ins = flip(bank_of(s)[0:ML_D, t * P:(t + 1) * P], HS[:, t, h * ML_D:(h + 1) * ML_D])
                    ins.then_inc(full_of(s)[0], 1)
                elif k == "cT":
                    t = s[2]
                    open_bank(s)
                    pe.wait_ge(cn_ready, cn_n[("cnorm", l, t)])
                    for c in range(0 if t in tq else 2, 3):
                        ins = flip(bank_of(s)[:, c * P:(c + 1) * P], PRv[:, t, c * P:(c + 1) * P])
                    ins.then_inc(full_of(s)[0], 1)
                elif k == "uqk":
                    t = s[2]
                    uq, ukv = small_views(l)[3:5]
                    pe.wait_ge(*free_of(("cT", l, t)))
                    if t in tq:
                        for i in (0, 1):
                            key = s + ("q", i)
                            open_bank(key)
                            for kk in (0, 1):
                                ins = pe.matmul(bank_of(key)[:, 0:288], CT[:, kk, t * P:(t + 1) * P],
                                                uq[:, kk, 288 * i:288 * i + 288], start=kk == 0, stop=kk == 1)
                            ins.then_inc(full_of(key)[0], 1)
                    for i in (0, 1):
                        key = s + ("k", i)
                        open_bank(key)
                        pe.matmul(bank_of(key)[:, 0:384], CT[:, 2, t * P:(t + 1) * P],
                                  ukv[:, 384 * i:384 * i + 384], start=True, stop=True).then_inc(full_of(key)[0], 1)
                elif k == "qkT":
                    t = s[2]
                    pe.wait_ge(qk_ready, uqk_n[("uqk", l, t)])
                    for key in qkT_jobs(s):
                        src = (QTM if key[3] == "q" else KTM)[t % 2]
                        open_bank(key)
                        for i in range(3):
                            ins = flip(bank_of(key)[0:QK_D, i * P:(i + 1) * P], src[:, 3 * key[4] + i, :])
                        ins.then_inc(full_of(key)[0], 1)
                elif k == "nT":
                    t = s[2]
                    open_bank(s)
                    pe.wait_ge(na_ready, nan_n[("nan", l, t)])
                    for i in range(0 if t in tq else 2, 4):
                        ins = flip(bank_of(s)[:, i * P:(i + 1) * P], PRv[:, t, PNQ + i * P:PNQ + (i + 1) * P])
                    ins.then_inc(full_of(s)[0], 1)
                elif k == "S":
                    _, b, _, t, h, _ = s
                    open_bank(s)
                    nk = keys_of(s)
                    if h == 0 and t == tq[0]:
                        for tt in range(T):
                            if b == 0:
                                for key in qkT_jobs(("qkT", l, tt)):
                                    pe.wait_ge(*free_of(key))
                            else:
                                pe.wait_ge(*free_of(("nT", l, tt)))
                    if b == 0:
                        q, kk = QT[:, h, t * P:(t + 1) * P], KT[:, h, 0:nk]
                    else:
                        r = (h % 2) * NA_D
                        q = NQT[r:r + NA_D, h // 2, t * P:(t + 1) * P]
                        kk = NKT[r:r + NA_D, h // 2, 0:nk]
                    pe.matmul(bank_of(s)[:, 0:nk], q, kk, start=True, stop=True).then_inc(full_of(s)[0], 1)
                elif k == "PV":
                    u = UNIT_AT[s[1:]]
                    _, b, _, t, h, lasth = s
                    nkt = keys_of(s) // P
                    key = ("ET",) + s[1:]
                    open_bank(key)
                    pe.wait_ge(*free_of(("S",) + s[1:]))
                    for i in range(nkt):
                        ins = flip(bank_of(key)[:, i * P:(i + 1) * P], E[u % 2][:, i * P:(i + 1) * P])
                    ins.then_inc(full_of(key)[0], 1)
                    akey = ("OT", b, l, t, (MLA_H, NA_H)[b] - 1, True)
                    acc = bank[6 + acc_at[akey] % 2]
                    if h == 0:
                        open_acc(akey)
                    pe.wait_ge(*free_of(key))
                    for i in range(nkt):
                        v = VV[:, i, h, :] if b == 0 else PRv[:, i, PNV + h * NA_D:PNV + (h + 1) * NA_D]
                        ins = pe.matmul(acc[:, h * 64:h * 64 + 64], PT[u % 2][:, i, :], v, start=i == 0,
                                        stop=i == nkt - 1)
                    ins.then_inc(pv_done, 1)
                elif k == "OT":
                    _, b, _, t, h, _ = s
                    open_bank(s)
                    pe.wait_ge(om_ready, OT_n[s])
                    for i in range((3, 2)[b]):
                        ins = flip(bank_of(s)[:, i * P:(i + 1) * P], OM[:, i * P:(i + 1) * P])
                    ins.then_inc(full_of(s)[0], 1)
                elif k == "gbc" or k == "gbc2":
                    keys = [s + (i,) for i in (0, 1)] if k == "gbc" else [
                        s + (st, i) for st in sorted({t // 2 for t in tq}) for i in (0, 1)]
                    v = 16 if k == "gbc" else 40
                    for i in (v // 4, v // 4 + 1):
                        pe.wait_ge(*free_of(("modT", l, i)))
                    for key in keys:
                        st = key[3] if k == "gbc" else key[2]
                        i = key[-1]
                        open_bank(key)
                        for c in range(4):
                            col = MODv[l][:, v + 4 * i + c, st:st + 1].broadcast_to([P, P])
                            ins = pe.matmul(bank_of(key)[:, c * P:(c + 1) * P], col, IDENT[:, :], start=True,
                                            stop=True, is_transpose=True)
                        ins.then_inc(full_of(key)[0], 1)
                elif k == "wo":
                    t = s[2]
                    if t == tq[0]:
                        for p in ("wo_mla", "wo_ml", "wo_na"):
                            pe.wait_ge(*loaded((p, l)))
                        pe.wait_ge(mlt_ready, ML_H * (l + 1))
                        for u in schedule:
                            if u[0] == "OT" and u[2] == l:
                                pe.wait_ge(*free_of(u))
                    wm = slot(("wo_mla", l))[:, 0:3 * D].rearrange("p (k n) -> p k n", k=3)
                    wl = slot(("wo_ml", l))[0:ML_D, :].rearrange("p (k n) -> p k n", k=ML_H)
                    wn = slot(("wo_na", l))[:, 0:2 * D].rearrange("p (k n) -> p k n", k=2)
                    terms = [(MLAT, wm, i) for i in range(3)] + [(MLT, wl, i) for i in range(4)] + [
                        (NAT, wn, i) for i in range(2)]
                    for n in (0, 1):
                        open_bank(s + (n,))
                        for i, (m, w, c) in enumerate(terms):
                            ins = pe.matmul(bank_of(s + (n,))[:, :], m[:, c, t * P:(t + 1) * P],
                                            w[:, c, 512 * n:512 * n + 512], start=i == 0, stop=i == len(terms) - 1)
                        ins.then_inc(full_of(s + (n,))[0], 1)
                elif k == "router":
                    open_bank(s)
                    for st in sorted({t // 2 for t in tq}):
                        for kp in range(4):
                            pe.wait_ge(*free_of(("hT", l, 2, st, kp)))
                    for i, t in enumerate(tq):
                        for kk in range(KD):
                            ins = pe.matmul(bank_of(s)[:, 16 * i:16 * i + 16], HT[:, kk, t * P:(t + 1) * P],
                                            RW[:, kk, :], start=kk == 0, stop=kk == KD - 1)
                    ins.then_inc(full_of(s)[0], 1)
                elif k == "h2T":
                    _, _, t, n = s
                    open_bank(s)
                    for c in range(4):
                        ins = flip(bank_of(s)[:, c * P:(c + 1) * P], HT[:, 4 * n + c, t * P:(t + 1) * P])
                    ins.then_inc(full_of(s)[0], 1)
                elif k == "pfx":
                    open_bank(s)
                    pe.wait_ge(assign_ready, l + 1)
                    nt = len(tq)
                    ones = RANK[:, 15:16].broadcast_to([P, P])
                    for i in range(nt):
                        out = bank_of(s)[:, 16 * i:16 * i + 16]
                        for j in range(i):
                            pe.matmul(out, ones, ASSIGN[:, 16 * j:16 * j + 16], start=j == 0, stop=False)
                        pe.matmul(out, INCL, ASSIGN[:, 16 * i:16 * i + 16], start=i == 0, stop=True)
                    for j in range(nt):
                        ins = pe.matmul(bank_of(s)[:, 64:80], ones, ASSIGN[:, 16 * j:16 * j + 16], start=j == 0,
                                        stop=j == nt - 1)
                    ins.then_inc(full_of(s)[0], 1)
                elif k == "xT":
                    n = expert_n(l, s[2])
                    pe.wait_ge(xg_loaded[n % 3], 16 * (n // 3 + 1))
                    for i in (0, 1):
                        open_bank(s + (i,))
                        for c in range(4):
                            o = (4 * i + c) * P
                            ins = flip(bank_of(s + (i,))[:, c * P:(c + 1) * P], XG[n % 3][:, o:o + P])
                        ins.then_inc(full_of(s + (i,))[0], 1)
                elif k == "ab":
                    e = s[2]
                    n = expert_n(l, e)
                    open_bank(s)
                    pe.wait_ge(*loaded(("w13", l, e)))
                    pe.wait_ge(*free_of(("xT", l, e, 0)))
                    pe.wait_ge(*free_of(("xT", l, e, 1)))
                    w = slot(("w13", l, e)).rearrange("p (k n) -> p k n", k=KD)
                    for kk in range(KD):
                        ins = pe.matmul(bank_of(s)[:, :], XGT[n % 2][:, kk, :], w[:, kk, :], start=kk == 0,
                                        stop=kk == KD - 1)
                    ins.then_inc(full_of(s)[0], 1)
                elif k == "y":
                    e = s[2]
                    n = y_n[s]
                    key = s + ("T",)
                    open_bank(key)
                    pe.wait_ge(hid_ready, n)
                    for i in (0, 1):
                        ins = flip(bank_of(key)[:, i * P:(i + 1) * P], HID[n % 2][:, i * P:(i + 1) * P])
                    ins.then_inc(full_of(key)[0], 1)
                    w2, sm, v = w2_of(l, e)
                    pe.wait_ge(sm, v)
                    pe.wait_ge(*free_of(key))
                    for nn in (0, 1):
                        open_bank(s + (nn,))
                        for i in (0, 1):
                            ins = pe.matmul(bank_of(s + (nn,))[:, :], HIDT[n % 2][:, i, :],
                                            w2[:, i, 512 * nn:512 * nn + 512], start=i == 0, stop=i == 1)
                        ins.then_inc(full_of(s + (nn,))[0], 1)
                elif k == "dense":
                    nt = len(tq)
                    d = dn[l]
                    over = pe.value_load(OVER[0:1, :])
                    with pe.If(over > 0):
                        last = job_at[("y", l, N_E - 1, 1)]
                        for j in range(RING):
                            pe.wait_ge(*free_of(jobs[last - j]))
                        w13 = RINGW[:, 0:4096].rearrange("p (k n) -> p k n", k=KD)
                        w2 = RINGW[:, 4096:6144].rearrange("p (k n) -> p k n", k=2)
                        with pe.Fori(0, N_E) as e:
                            pe.wait_ge(d["loaded"], e * 48 + 48)
                            for i, t in enumerate(tq):
                                pe.wait_ge(d["hid"], e * nt + (i + 1))
                                for kk in range(KD):
                                    ins = pe.matmul(bank[0][:, :], HT[:, kk, t * P:(t + 1) * P], w13[:, kk, :],
                                                    start=kk == 0, stop=kk == KD - 1)
                                ins.then_inc(d["ab"], 1)
                                pe.wait_ge(d["hid"], e * nt + (i + 2))
                                for c in (0, 1):
                                    ins = flip(bank[1][:, c * P:(c + 1) * P], HID[0][:, c * P:(c + 1) * P])
                                ins.then_inc(d["T"], 1)
                                pe.wait_ge(d["ht"], e * nt + (i + 1))
                                pe.wait_ge(d["acc"], e * nt + (i + 1))
                                for nn in (0, 1):
                                    for c in (0, 1):
                                        ins = pe.matmul(bank[2 + nn][:, :], HIDT[0][:, c, :],
                                                        w2[:, c, 512 * nn:512 * nn + 512], start=c == 0, stop=c == 1)
                                ins.then_inc(d["y"], 1)
                        pe.wait_ge(d["acc"], N_E * nt + 1)

        @block.vector
        def _(dve):
            step = [0]

            def link(ins):
                step[0] += 1
                ins.then_inc(dve_step, 1)
                dve.wait_ge(dve_step, step[0])

            dve.wait_ge(cols_full, 1)
            dve.tensor_copy(COLS[:, :], bank[6][:, 0:3 * P]).then_inc(cols_ready, 1)
            dve.wait_ge(cols_ready, 1)
            dve.wait_ge(params_loaded, 16 * PARAM_DMAS)
            for l in range(DEPTH):
                q = 2 * P + 24 * l
                link(dve.tensor_scalar(COLS[0:ML_D, q + 8:q + 24], COLS[0:ML_D, q + 8:q + 24], 0.5, None, ALU.mult))
                link(dve.tensor_scalar(bc_qg(l), bc_qg(l), QK_D ** -0.5, None, ALU.mult))
                link(dve.tensor_scalar(bc_nq(l), bc_nq(l), NA_D ** -0.5, None, ALU.mult))
            dve.wait_ge(csilu_ready, 1)
            link(dve.scalar_tensor_tensor(CS[:, :], RT[:, 0:16], 1.0, COLS[:, P:P + 16], ALU.add, ALU.mult))
            dve.tensor_scalar(CS[:, :], CS[:, :], 0.5, None, ALU.mult).then_inc(csilu_ready, 1)

            def rstd(s, n):
                w = rstd_width(s)
                m, r = stat(rstd_at[s])
                return m[:, 0:w], r[:, 0:w]

            def bcast(ap, n):
                return ap.unsqueeze(2).broadcast_to([ap.shape[0], ap.shape[1], n])

            for s in schedule:
                k, l = s[0], layer_of(s)
                tq = tiles_q(l)
                c0 = 0 if l < DEPTH - 1 else L
                if k == "modT":
                    i = s[2]
                    dve.wait_ge(*full_of(s))
                    link_to = dve.tensor_tensor(MODv[l][:, 4 * i:4 * i + 4, :],
                                                bank_of(s)[:, 0:8].rearrange("p (c j) -> p c j", j=2),
                                                bcast(COLS[:, 64 * l + 4 * i:64 * l + 4 * i + 4], 2), ALU.add)
                    link_to.then_inc(free_of(s)[0], 1)
                elif k == "modfin":
                    w = s[2] - 1
                    for i in range(6 * w, 6 * w + 4):
                        dve.wait_ge(*free_of(("modT", l, i)))
                    link(dve.scalar_tensor_tensor(AMv[l][:, w, :, 0], MODv[l][:, 24 * w + 8:24 * w + 16, 0], 1.0,
                                                  COLS[:, 64 * l + 48 + 8 * w:64 * l + 56 + 8 * w], ALU.add,
                                                  ALU.mult))
                    dve.scalar_tensor_tensor(AMv[l][:, w, :, 1], MODv[l][:, 24 * w + 8:24 * w + 16, 1], 1.0,
                                             COLS[:, 64 * l + 48 + 8 * w:64 * l + 56 + 8 * w], ALU.add,
                                             ALU.mult).then_inc(mod_ready, 1)
                elif k == "norm":
                    t, w = s[3], s[2]
                    dve.wait_ge(ssq_ready, ssq_at[s])
                    m = ssq_cols(s)
                    mm, rr = rstd(s, D)
                    dve.tensor_scalar(mm, m[:, 0:1], 1.0 / D, EPS, ALU.mult, ALU.add).then_inc(mean_ready, 1)
                    dve.wait_ge(rstd_ready, rstd_at[s])
                    dve.tensor_scalar(XS[:, t, :], Xv[:, t, :], rr, None, ALU.mult).then_inc(xs_ready, 1)
                elif k == "hT" and s[4] % 2 == 0:
                    _, _, w, st, kp = s
                    dve.wait_ge(*full_of(s))
                    dve.wait_ge(mod_ready, modfin_n[("modfin", l, w)])
                    for i in (0, 1):
                        kk = 2 * kp + i
                        ins = dve.tensor_scalar(HT[:, kk, st * L:(st + 1) * L], bank_of(s)[:, i * L:(i + 1) * L],
                                                AMv[l][:, w - 1, kk, st:st + 1], MODv[l][:, 24 * (w - 1) + kk, st:st + 1],
                                                ALU.mult, ALU.add)
                    ins.then_inc(free_of(s)[0], 1)
                elif k == "pu" and s[2] % 2 == 0:
                    dve.wait_ge(*full_of(s))
                    dve.tensor_copy(UT[:, s[2], :], bank_of(s)[0:ML_D, :]).then_inc(free_of(s)[0], 1)
                elif k == "pP" and s[3] % 2 == 0:
                    dve.wait_ge(*full_of(s))
                    c, n = p_cols(s)
                    dve.tensor_copy(PRv[:, s[3], c:c + n], bank_of(s)[:, 0:n]).then_inc(free_of(s)[0], 1)
                elif k == "pz":
                    dve.wait_ge(zs_tanh, pz_n[s])
                    dve.scalar_tensor_tensor(ZS[:, s[2], c0:TOK], ZS[:, s[2], c0:TOK], 1.0,
                                             bank_of(s)[0:ML_D, c0:TOK], ALU.add, ALU.mult).then_inc(
                        free_of(s)[0], 1)
                elif k == "gates":
                    for t in range(T):
                        dve.wait_ge(*free_of(("pP", l, "B", t)))
                    g = PRv[:, :, PG:PG + 16]
                    dve.tensor_tensor(g, g, bc_gb(l).unsqueeze(1).broadcast_to([P, T, 16]), ALU.add).then_inc(
                        gates_ready, 1)
                elif k == "gT":
                    t = s[2]
                    dve.wait_ge(*full_of(s))
                    bk = bank_of(s)[0:ML_H, :].rearrange("p (q t) -> p q t", q=4)
                    r0 = (t // 2) * L + (1 - t % 2) * P
                    dve.tensor_copy(ROW[:, 0:2, t * P:(t + 1) * P], bk[:, 0:2, :])
                    dve.tensor_copy(ROW[:, 2:4, r0:r0 + P], bk[:, 2:4, ::-1]).then_inc(free_of(s)[0], 1)
                elif k == "rows":
                    for t in range(T):
                        dve.wait_ge(*free_of(("gT", l, t)))
                    f = ROW[:, 1::2, :]
                    dve.scalar_tensor_tensor(GEM[:, 0:2, :], f, -1.0, f, ALU.mult, ALU.max).then_inc(lfa_ready, 1)
                    link(dve.memset(GEM[:, 2:3, :], 1.0))
                    dve.wait_ge(lf_ready, l + 1)
                    link(dve.scalar_tensor_tensor(f, f, 0.0, GEM[:, 0:2, :], ALU.min, ALU.subtract))
                    for d in (0, 1):
                        link(dve.tensor_tensor_scan(GEM[:, d, :], GEM[:, 2, :], ROW[:, 2 * d + 1, :], 0.0, ALU.mult,
                                                    ALU.add))
                    for d in (0, 1):
                        link(dve.tensor_tensor(ROW[:, 2 * d, :], ROW[:, 2 * d, :], GEM[:, d, :], ALU.subtract))
                        link(dve.tensor_tensor_scan(ROW[:, 2 * d + 1, :], ROW[:, 2 * d, :], ROW[:, 2 * d, :], 0.0,
                                                    ALU.max, ALU.max))
                    def nat(ap, d):
                        return ap if d == 0 else ap.rearrange("p (s t) -> p s t", s=2)[:, :, ::-1]

                    def plain(ap, d):
                        return ap if d == 0 else ap.rearrange("p (s t) -> p s t", s=2)
                    for d in (0, 1):
                        link(dve.tensor_tensor(plain(GEM[:, 2 + d, :], d), nat(GEM[:, d, :], d),
                                               nat(ROW[:, 2 * d + 1, :], d), ALU.add))
                    for d in (0, 1):
                        link(dve.tensor_copy(plain(GEM[:, d, :], d), nat(ROW[:, 2 * d, :], d)))
                        ins = dve.tensor_scalar(plain(NEGMUv[:, d, :], d), nat(ROW[:, 2 * d + 1, :], d), -1.0, None,
                                                ALU.mult)
                        if d == 0:
                            link(ins)
                    ins.then_inc(em_in, 1)
                    dve.wait_ge(em_ready, l + 1)
                    dve.wait_ge(em_in, l + 1)
                    dve.memset(MV[:, :, :, 96:97].rearrange("p t h o -> p (t h) o"), 1.0).then_inc(mv_ready, 1)
                    dve.wait_ge(mv_ready, l + 1)
                    tick(dve, rows_ready)
                elif k == "cols":
                    dve.wait_ge(*full_of(s))
                    dve.tensor_copy(GEMC[:, :], bank_of(s)[:, 0:64]).then_inc(gc_ready, 1)
                    dve.wait_ge(gc_ready, l + 1)
                    tick(dve, free_of(s)[0])
                elif k == "mv" and s[2] % 2 == 0:
                    dve.wait_ge(*full_of(s))
                    dve.tensor_copy(MV[:, s[2], :, 0:ML_D],
                                    bank_of(s)[:, 0:ML_W].rearrange("p (h e) -> p h e", h=ML_H)).then_inc(
                        free_of(s)[0], 1)
                elif k == "conv":
                    h = s[2]
                    dve.wait_ge(*free_of(("pu", l, h)))
                    q = 24 * l
                    b, w0, w1, w2 = (c96(q + 8 + h), c96(q + 12 + h), c96(q + 16 + h), c96(q + 20 + h))
                    u2 = UT[:, h, :].rearrange("p (s t) -> p s t", s=2)
                    o2 = UC[:, h, :].rearrange("p (s t) -> p s t", s=2)
                    link(dve.tensor_scalar(UC[:, h, :], UT[:, h, :], w1, b, ALU.mult, ALU.add))
                    link(dve.scalar_tensor_tensor(o2[:, :, 1:L], u2[:, :, 0:L - 1], w0, o2[:, :, 1:L], ALU.mult,
                                                  ALU.add))
                    dve.scalar_tensor_tensor(o2[:, :, 0:L - 1], u2[:, :, 1:L], w2, o2[:, :, 0:L - 1], ALU.mult,
                                             ALU.add).then_inc(conv_acc, 1)
                    dve.wait_ge(conv_tanh, conv_n[s])
                    dve.wait_ge(conv_acc, conv_n[s])
                    dve.scalar_tensor_tensor(UC[:, h, :], conv_tmp(s), 1.0, UC[:, h, :], ALU.add,
                                             ALU.mult).then_inc(uc_ready, 1)
                elif k == "mqk":
                    h = s[2]
                    key = s + ("q",)
                    dve.wait_ge(*full_of(key))
                    dve.tensor_copy(MQ[:, h, c0:TOK], bank_of(key)[0:ML_D, c0:TOK]).then_inc(free_of(key)[0], 1)
                    dve.wait_ge(*full_of(s + ("k",)))
                    link(dve.tensor_scalar(UC[:, h, :], UC[:, h, :], c96(24 * l + 4 + h), None, ALU.mult))
                elif k == "mgrid":
                    _, _, h, d = s
                    n = grid_n[s]
                    g = GRIDB[n % 2]
                    mu = bank_of(s)
                    dve.wait_ge(*full_of(s))
                    dve.wait_ge(gc_ready, l + 1)
                    if n > 2:
                        dve.wait_ge(pv_done, mpv_before(s))
                    for t in tq:
                        ins = dve.scalar_tensor_tensor(g[:, t, t * P:(t + 1) * P], mu[:, t * P:(t + 1) * P],
                                                       GC[:, d, t, h:h + 1], TRI[:, d * P:(d + 1) * P], ALU.add,
                                                       ALU.add)
                    ins.then_inc(diag_ready, 1)
                    dve.wait_ge(grid_exp, n)
                    todo = [(j, t0, t1) for j in range(T) for t0, t1 in runs(l, d, j, True)]
                    for j, t0, t1 in todo:
                        if d == 0:
                            dve.wait_ge(*full_of(("mst", l, h, j)))
                        ins = dve.tensor_tensor(g[:, j, t0 * P:t1 * P], g[:, j, t0 * P:t1 * P],
                                                bank_of(("mst", l, h, j))[:, t0 * P:t1 * P], ALU.mult)
                    ins.then_inc(grid_ready, 1)
                    dve.wait_ge(grid_ready, n)
                    tick(dve, free_of(s)[0])
                    if d == 1:
                        for j in range(T):
                            tick(dve, free_of(("mst", l, h, j))[0])
                elif k == "mpv":
                    _, _, h, d = s
                    acc = bank[6 + acc_at[s] % 2]
                    nt = len(tq)
                    av = acc[:, tq[0] * 97:(tq[0] + nt) * 97].rearrange("p (t e) -> p t e", e=97)
                    dve.wait_ge(pv_done, pv_at[s])
                    den = ST[:, 128:128 + nt]
                    link(dve.scalar_tensor_tensor(den, av[:, :, 96], -1.0, GC[:, 2 + d, tq[0]:tq[0] + nt, h],
                                                  ALU.mult, ALU.max))
                    link(dve.tensor_tensor(den, den, av[:, :, 96], ALU.max))
                    link(dve.reciprocal(den, den))
                    hs = HS[:, tq[0]:tq[0] + nt, h * ML_D:(h + 1) * ML_D]
                    if d == 0:
                        dve.tensor_tensor(hs, av[:, :, 0:ML_D], bcast(den, ML_D), ALU.mult).then_inc(acc_free, 1)
                        dve.wait_ge(acc_free, acc_at[s] + 1)
                    else:
                        tmp = RT[:, 0:384].rearrange("p (t e) -> p t e", t=4)[:, 0:nt, :]
                        dve.tensor_tensor(tmp, av[:, :, 0:ML_D], bcast(den, ML_D), ALU.mult).then_inc(acc_free, 1)
                        dve.wait_ge(acc_free, acc_at[s] + 1)
                        link(dve.tensor_tensor(hs, hs, tmp, ALU.add))
                elif k == "mln":
                    nt = len(tq)
                    hs = HS[:, tq[0]:tq[0] + nt, :].rearrange("p t (h e) -> p (t h) e", e=ML_D)
                    nn = nt * ML_H
                    sq = view(WORK, 2560, nn, ML_D)
                    mu = ST[:, 128:128 + nn]
                    link(dve.tensor_reduce(mu, hs, AX.X, ALU.add))
                    link(dve.tensor_scalar(mu, mu, 1.0 / ML_D, None, ALU.mult))
                    link(dve.tensor_tensor(hs, hs, bcast(mu, ML_D), ALU.subtract))
                    dve.wait_ge(pv_done, pv_at[("mpv", l, ML_H - 1, 1)])
                    link(dve.tensor_tensor(sq, hs, hs, ALU.mult))
                    link(dve.tensor_reduce(mu, sq, AX.X, ALU.add))
                    m, r = rstd(s, ML_D)
                    dve.tensor_scalar(m, mu, 1.0 / ML_D, EPS, ALU.mult, ALU.add).then_inc(mean_ready, 1)
                    dve.wait_ge(rstd_ready, rstd_at[s])
                    dve.tensor_tensor(hs, hs, bcast(r, ML_D), ALU.mult).then_inc(hn_ready, 1)
                elif k == "mlT":
                    h = s[2]
                    dve.wait_ge(*full_of(s))
                    o = MLT[:, h, c0:TOK]
                    link(dve.scalar_tensor_tensor(o, bank_of(s)[0:ML_D, c0:TOK], c96(24 * l + h),
                                                  UC[:, h, c0:TOK], ALU.mult, ALU.add))
                    tick(dve, free_of(s)[0])
                    dve.scalar_tensor_tensor(o, o, 0.5, ZS[:, h, c0:TOK], ALU.mult, ALU.mult).then_inc(mlt_ready, 1)
                    if h == ML_H - 1:
                        dve.wait_ge(mlt_ready, ML_H * (l + 1))
                        tick(dve, hn_used)
                elif k == "cnorm":
                    t = s[2]
                    m = ssq_cols(s)
                    mm, rr = rstd(s, 0)
                    dve.wait_ge(ssq_ready, ssq_at[s])
                    if t in tq:
                        link(dve.tensor_scalar(mm[:, 0:1], m[:, 0:1], 1.0 / Q_RANK, EPS, ALU.mult, ALU.add))
                    else:
                        link(dve.memset(mm[:, 0:1], 1.0))
                    dve.tensor_scalar(mm[:, 1:2], m[:, 1:2], 1.0 / KV_RANK, EPS, ALU.mult, ALU.add).then_inc(
                        mean_ready, 1)
                    dve.wait_ge(rstd_ready, rstd_at[s])
                    if t in tq:
                        link(dve.tensor_scalar(PRv[:, t, 0:Q_RANK], PRv[:, t, 0:Q_RANK], rr[:, 0:1], None, ALU.mult))
                    dve.tensor_scalar(PRv[:, t, Q_RANK:384], PRv[:, t, Q_RANK:384], rr[:, 1:2], None,
                                      ALU.mult).then_inc(cn_ready, 1)
                elif k == "cT":
                    t = s[2]
                    dve.wait_ge(*full_of(s))
                    for c in range(0 if t in tq else 2, 3):
                        ins = dve.tensor_scalar(CT[:, c, t * P:(t + 1) * P], bank_of(s)[:, c * P:(c + 1) * P],
                                                c2(16 + 3 * l + c), None, ALU.mult)
                    ins.then_inc(free_of(s)[0], 1)
                elif k == "uqk":
                    t = s[2]
                    kt = KTM[t % 2]
                    isq = t in tq
                    if t >= 2:
                        for key in qkT_jobs(("qkT", l, t - 2)):
                            dve.wait_ge(*full_of(key))
                    key = s + ("k", 0)
                    dve.wait_ge(*full_of(key))
                    kvv = bank_of(key)[:, 0:384].rearrange("p (h e) -> p h e", h=3)
                    dve.tensor_copy(kt[:, 0:3, 0:NOPE_D], kvv[:, :, 0:NOPE_D])
                    dve.tensor_copy(VV[:, t, 0:3, :], kvv[:, :, NOPE_D:]).then_inc(free_of(key)[0], 1)
                    m, r = rstd(s, 0)
                    if not isq:
                        dve.memset(m[:, 0:6], 1.0)
                    dve.wait_ge(usq_ready, uqk_n[s])
                    if isq:
                        dve.tensor_reduce(m[:, 0:6], SQU[0], AX.X, ALU.add)
                    link(dve.tensor_reduce(m[:, 6:12], SQU[1], AX.X, ALU.add))
                    dve.tensor_scalar(m, m, 1.0 / QK_D, EPS, ALU.mult, ALU.add).then_inc(mean_ready, 1)
                elif k == "uqn":
                    t = s[2]
                    q, kt = QTM[t % 2], KTM[t % 2]
                    m, r = rstd(("uqk", l, t), 0)
                    dve.wait_ge(rstd_ready, rstd_at[("uqk", l, t)])
                    both = ([(q, r[:, 0:6], bc_qg(l), SWAP[0])] if t in tq else []) + [
                        (kt, r[:, 6:12], bc_kg(l), SWAP[1])]

                    def each(op):
                        for x in both[:-1]:
                            op(*x)
                        link(op(*both[-1]))

                    each(lambda x_, rr, g_, sw: dve.tensor_tensor(x_, x_, bcast(rr, QK_D), ALU.mult))
                    gain = lambda x_, rr, g_, sw: dve.tensor_tensor(
                        x_, x_, g_.unsqueeze(1).broadcast_to([P, MLA_H, QK_D]), ALU.mult)
                    if t < 2:
                        for x in both:
                            ins = gain(*x)
                    else:
                        each(gain)
                        cos = ROv[:, t - 2, 0, :].unsqueeze(1).broadcast_to([P, MLA_H, ROPE_D])
                        sin = ROv[:, t - 2, 1, :].rearrange("p (a b c) -> p a b c", a=2, b=2)

                        def swapped(x_, rr, g_, sw):
                            x4 = x_[:, :, NOPE_D:].rearrange("p h (a b c) -> p h a b c", a=2, b=2)
                            s5 = sw.rearrange("p h (a b c) -> p h a b c", a=2, b=2)
                            for b_ in (0, 1):
                                sb_ = sin[:, :, b_, :].unsqueeze(1).broadcast_to([P, MLA_H, 2, 8])
                                o = dve.tensor_tensor(s5[:, :, :, b_, :], x4[:, :, :, 1 - b_, :], sb_, ALU.mult)
                            return o

                        each(swapped)
                        each(lambda x_, rr, g_, sw: dve.tensor_tensor(x_[:, :, NOPE_D:], x_[:, :, NOPE_D:], cos,
                                                                      ALU.mult))
                        for x_, rr, g_, sw in both:
                            ins = dve.tensor_tensor(x_[:, :, NOPE_D:], x_[:, :, NOPE_D:], sw, ALU.add)
                    ins.then_inc(qk_ready, 1)
                elif k == "qkT":
                    for key in qkT_jobs(s):
                        if key[3] == "q":
                            dve.wait_ge(*full_of(key))
                            hh = 3 * key[4]
                            dve.tensor_copy(QT[:, hh:hh + 3, s[2] * P:(s[2] + 1) * P],
                                            bank_of(key)[0:QK_D, 0:384].rearrange("p (h t) -> p h t",
                                                                                  h=3)).then_inc(free_of(key)[0], 1)
                elif k == "nan":
                    t = s[2]
                    isq = t in tq
                    dve.wait_ge(*free_of(("pP", l, "B", t)))
                    dve.wait_ge(*free_of(("pP", l, "C", t)))
                    h0 = 0 if isq else NA_H
                    x_ = PRv[:, t, PNQ + h0 * NA_D:PNV].rearrange("p (h e) -> p h e", e=NA_D)
                    nh = 2 * NA_H - h0
                    sq = SQN[:, 0:nh * NA_D].rearrange("p (h e) -> p h e", e=NA_D)
                    m, r = rstd(s, 0)
                    if not isq:
                        link(dve.memset(m[:, 0:4], 1.0))
                    link(dve.tensor_tensor(sq, x_, x_, ALU.mult))
                    link(dve.tensor_reduce(m[:, h0:8], sq, AX.X, ALU.add))
                    dve.tensor_scalar(m, m, 1.0 / NA_D, EPS, ALU.mult, ALU.add).then_inc(mean_ready, 1)
                    dve.wait_ge(rstd_ready, rstd_at[s])
                    link(dve.tensor_tensor(x_, x_, bcast(r[:, h0:8], NA_D), ALU.mult))
                    if isq:
                        xq = x_[:, 0:NA_H, :]
                        link(dve.tensor_tensor(xq, xq, bc_nq(l).unsqueeze(1).broadcast_to([P, NA_H, NA_D]),
                                               ALU.mult))
                    xk = x_[:, nh - NA_H:nh, :]
                    dve.tensor_tensor(xk, xk, bc_nk(l).unsqueeze(1).broadcast_to([P, NA_H, NA_D]),
                                      ALU.mult).then_inc(na_ready, 1)
                elif k == "S":
                    _, b, _, t, h, _ = s
                    u = UNIT_AT[s[1:]]
                    nk = keys_of(s)
                    bk = bank_of(s)
                    dve.wait_ge(*full_of(s))
                    if b == 1 and t >= 2:
                        dve.wait_ge(bias_masked, 2 * (l + 1))
                        link(dve.tensor_tensor(bk[:, L:TOK], bk[:, L:TOK], BIAS[:, t - 2, h, :], ALU.add))
                    if u >= 2:
                        dve.wait_ge(*free_of(("S",) + UNITS[u - 2]))
                    dve.tensor_reduce(neg_max(u), bk[:, 0:nk], AX.X, ALU.max, negate=True).then_inc(nmax_ready, 1)
                elif k == "PV":
                    u = UNIT_AT[s[1:]]
                    key = ("ET",) + s[1:]
                    nkt = keys_of(s) // P
                    dve.wait_ge(*full_of(key))
                    if u >= 2:
                        dve.wait_ge(pv_done, pv_at[("PV",) + UNITS[u - 2]])
                    dve.tensor_copy(PT[u % 2][:, 0:nkt, :].rearrange("p a b -> p (a b)"),
                                    bank_of(key)[:, 0:nkt * P]).then_inc(free_of(key)[0], 1)
                elif k == "OT":
                    _, b, _, t, h, _ = s
                    u = UNIT_AT[s[1:]]
                    nh = h + 1
                    acc = bank[6 + acc_at[s] % 2]
                    dve.wait_ge(pv_done, pv_at[("PV",) + s[1:]])
                    rs = ST[:, 160:160 + nh]
                    link(dve.reciprocal(rs, exp_sums(u - h, nh)))
                    if OT_n[s] > 1:
                        dve.wait_ge(*full_of(OT_key[OT_n[s] - 1]))
                    dve.tensor_tensor(OM[:, 0:nh * 64].rearrange("p (h e) -> p h e", h=nh),
                                      acc[:, 0:nh * 64].rearrange("p (h e) -> p h e", h=nh), bcast(rs, 64),
                                      ALU.mult).then_inc(om_ready, 1)
                    dve.wait_ge(om_ready, OT_n[s])
                    tick(dve, acc_free)
                    dve.wait_ge(*full_of(s))
                    dst = (MLAT, NAT)[b]
                    nc_ = (3, 2)[b]
                    dve.tensor_copy(dst[:, :, t * P:(t + 1) * P],
                                    bank_of(s)[:, 0:nc_ * P].rearrange("p (a t) -> p a t", a=nc_)).then_inc(
                        free_of(s)[0], 1)
                elif k == "wo":
                    t = s[2]
                    st = t // 2
                    for n in (0, 1):
                        key = s + (n,)
                        dve.wait_ge(*full_of(key))
                        dve.wait_ge(*free_of(("gbc", l, 1, st, n)))
                        dve.tensor_tensor(YT, bank_of(key)[:, :], GB[:, st, 512 * n:512 * n + 512],
                                          ALU.mult).then_inc(free_of(key)[0], 1)
                        dve.wait_ge(*free_of(key))
                        xx = Xv[:, t, 512 * n:512 * n + 512]
                        ins = dve.tensor_tensor(xx, xx, YT, ALU.add)
                        if n:
                            ins.then_inc(resid_ready, 1)
                            dve.wait_ge(resid_ready, resid_at[s])
                        else:
                            link(ins)
                elif k == "router":
                    nt = len(tq)
                    dve.wait_ge(*free_of(s))
                    aff = RT[:, 0:16 * nt]
                    sel = RT[:, 64:64 + 16 * nt]
                    link(dve.tensor_scalar(aff, aff, 0.5, 0.5, ALU.mult, ALU.add))
                    a3 = aff.rearrange("p (t e) -> p t e", e=16)
                    s3 = sel.rearrange("p (t e) -> p t e", e=16)
                    link(dve.tensor_tensor(s3, a3, bc_rb.unsqueeze(1).broadcast_to([P, nt, 16]), ALU.add))
                    s4 = sel.rearrange("p (g e) -> p g e", e=4)
                    ng = 4 * nt
                    pr = RT[:, 128:128 + 6 * ng].rearrange("p (g e) -> p g e", e=6)
                    link(dve.tensor_tensor(pr[:, :, 0:3], s4[:, :, 0:3], s4[:, :, 1:4], ALU.add))
                    link(dve.tensor_tensor(pr[:, :, 3:5], s4[:, :, 0:2], s4[:, :, 2:4], ALU.add))
                    link(dve.tensor_tensor(pr[:, :, 5:6], s4[:, :, 0:1], s4[:, :, 3:4], ALU.add))
                    gs = RT[:, 224:224 + ng]
                    link(dve.tensor_reduce(gs, pr, AX.X, ALU.max))
                    g3 = gs.rearrange("p (t g) -> p t g", g=4)
                    mx = RT[:, 240:240 + nt]

                    def first_max(v3, m_, out3, wts, width):
                        link(dve.tensor_reduce(m_, v3, AX.X, ALU.max))
                        link(dve.tensor_tensor(out3, v3, bcast(m_, width), ALU.is_equal))
                        link(dve.tensor_tensor(out3, out3, wts, ALU.mult))
                        link(dve.tensor_reduce(m_, out3, AX.X, ALU.max))
                        link(dve.tensor_tensor(out3, out3, bcast(m_, width), ALU.is_equal))

                    wt16 = RANK.unsqueeze(1).broadcast_to([P, nt, 16])
                    wt4 = RANK[:, 12:16].unsqueeze(1).broadcast_to([P, nt, 4])
                    ing = RT[:, 244:244 + ng].rearrange("p (t g) -> p t g", g=4)
                    first_max(g3, mx, ing, wt4, 4)
                    off = RT[:, 260:260 + ng]
                    link(dve.tensor_scalar(off, RT[:, 244:244 + ng], -1.0, BIG, ALU.add, ALU.mult))
                    link(dve.tensor_tensor(s4, s4, bcast(off, 4), ALU.add))
                    def te(ap):
                        return ap[:, 0:16 * nt].rearrange("p (t e) -> p t e", e=16)

                    dve.wait_ge(xg_blank, l + 1)
                    oh0, oh1, gt, prod, pick = te(OH[0]), te(OH[1]), te(RT[:, 280:]), te(PROD), te(PICK)
                    first_max(s3, mx, oh0, wt16, 16)
                    link(dve.scalar_tensor_tensor(s3, oh0, -4.0 * BIG, s3, ALU.mult, ALU.add))
                    first_max(s3, mx, oh1, wt16, 16)
                    link(dve.tensor_scalar(INCL, TRI[:, 0:P], 0.0, None, ALU.is_ge))
                    dve.tensor_tensor(te(ASSIGN), oh0, oh1, ALU.add).then_inc(assign_ready, 1)
                    dve.wait_ge(assign_ready, l + 1)
                    link(dve.tensor_tensor(gt, te(ASSIGN), a3, ALU.mult))
                    link(dve.tensor_reduce(mx, gt, AX.X, ALU.add))
                    link(dve.reciprocal(mx, mx))
                    link(dve.tensor_scalar(mx, mx, 0.5, None, ALU.mult))
                    gv = GATEv[:, tq[0]:tq[0] + nt, :]
                    link(dve.tensor_tensor(gv, gt, bcast(mx, 16), ALU.mult))
                    for c, oh in ((0, oh0), (1, oh1)):
                        link(dve.tensor_tensor(prod, oh, gv, ALU.mult))
                        link(dve.tensor_reduce(ENT[:, tq[0]:tq[0] + nt, c, 1], prod, AX.X, ALU.add))
                    dve.wait_ge(*full_of(("pfx", l)))
                    bk = bank_of(("pfx", l))
                    link(dve.scalar_tensor_tensor(pick, te(bk), float(N_E), wt16, ALU.mult, ALU.subtract))
                    link(dve.tensor_reduce(mx[:, 0:1], bk[:, 64:80], AX.X, ALU.max))
                    tick(dve, free_of(("pfx", l))[0])
                    sf = SLOTF[:, 0:2 * nt].rearrange("p (t c) -> p t c", c=2)
                    for c, oh in ((0, oh0), (1, oh1)):
                        link(dve.tensor_tensor(prod, oh, pick, ALU.mult))
                        link(dve.tensor_reduce(sf[:, :, c], prod, AX.X, ALU.add))
                    link(dve.tensor_scalar(OVER, mx[:, 0:1], float(CAP), None, ALU.is_gt))
                    dve.tensor_copy(SLOTU[:, 0:2 * nt], SLOTF[:, 0:2 * nt]).then_inc(route_ready, 1)
                elif k == "pfx":
                    dve.wait_ge(slots_loaded, 16 * (l + 1))
                    dve.tensor_copy(TOKU, TABS[:, :, 0])
                    dve.tensor_copy(PAIRU, TABS[:, :, 2]).then_inc(index_ready, 1)
                elif k == "xT":
                    n = expert_n(l, s[2])
                    dve.wait_ge(*full_of(s + (0,)))
                    if n >= 2:
                        dve.wait_ge(*full_of(("ab",) + expert_key(n - 2)))
                    dve.tensor_copy(XGT[n % 2][:, 0:4, :].rearrange("p k t -> p (k t)"),
                                    bank_of(s + (0,))[:, :]).then_inc(free_of(s + (0,))[0], 1)
                elif k == "ab":
                    e = s[2]
                    n = ab_n[s]
                    dve.wait_ge(moe_tanh, n)
                    if n > 2:
                        dve.wait_ge(*full_of(("y",) + expert_key(n - 3) + ("T",)))
                    bk = bank_of(s)
                    link(dve.scalar_tensor_tensor(HID[n % 2], TH[n % 2], 1.0, bk[:, 0:FF], ALU.add, ALU.mult))
                    dve.scalar_tensor_tensor(HID[n % 2], HID[n % 2], TABS[:, e, 1:2], bk[:, FF:2 * FF],
                                             ALU.mult, ALU.mult).then_inc(hid_ready, 1)
                    dve.wait_ge(hid_ready, n)
                    tick(dve, free_of(s)[0])
                elif k == "y":
                    key = s + (0,)
                    n = expert_n(l, s[2])
                    dve.wait_ge(*full_of(key))
                    if n >= 2:
                        dve.wait_ge(ys_stored[n % 2], 16 * (n // 2))
                    dve.tensor_copy(YO[n % 2][:, 0:512], bank_of(key)[:, :]).then_inc(free_of(key)[0], 1)
                elif k == "comb":
                    t = s[2]
                    uses = sum(t in tiles_q(m) for m in range(l + 1))
                    dve.wait_ge(pair_loaded[t], 32 * uses)
                    link(dve.tensor_tensor(ACC[:, t, :], ACC[:, t, :], XS[:, t, :], ALU.add))
                elif k == "dense":
                    nt = len(tq)
                    d = dn[l]
                    over = dve.value_load(OVER[0:1, :])
                    with dve.If(over > 0):
                        dve.memset(ACC[:, tq[0]:T, :], 0.0).then_inc(d["zero"], 1)
                        dve.wait_ge(d["zero"], 1)
                        tick(dve, d["hid"])
                        tick(dve, d["acc"])
                        gs = GATEv[:, tq[0]:T, :]
                        tmp = RT[:, 0:16 * nt].rearrange("p (t e) -> p t e", e=16)
                        with dve.Fori(0, N_E) as e:
                            for i, t in enumerate(tq):
                                dve.wait_ge(d["tanh"], e * nt + (i + 1))
                                dve.scalar_tensor_tensor(HID[0], TH[0], 1.0, bank[0][:, 0:FF], ALU.add,
                                                         ALU.mult).then_inc(d["half"], 1)
                                dve.wait_ge(d["half"], e * nt + (i + 1))
                                dve.scalar_tensor_tensor(HID[0], HID[0], GATEv[:, t, 0:1], bank[0][:, FF:2 * FF],
                                                         ALU.mult, ALU.mult).then_inc(d["hid"], 1)
                                dve.wait_ge(d["T"], e * nt + (i + 1))
                                dve.tensor_copy(HIDT[0].rearrange("p k t -> p (k t)"),
                                                bank[1][:, 0:FF]).then_inc(d["ht"], 1)
                                dve.wait_ge(d["y"], e * nt + (i + 1))
                                dve.wait_ge(d["acc"], e * nt + (i + 1))
                                for nn in (0, 1):
                                    o = ACC[:, t, 512 * nn:512 * nn + 512]
                                    ins = dve.tensor_tensor(o, o, bank[2 + nn][:, :], ALU.add)
                                ins.then_inc(d["acc"], 1)
                                dve.wait_ge(d["acc"], e * nt + (i + 2))
                            dve.tensor_copy(tmp[:, :, 0:N_E - 1], gs[:, :, 1:N_E]).then_inc(d["gate"], 1)
                            dve.wait_ge(d["gate"], e * 2 + 1)
                            dve.tensor_copy(gs[:, :, 0:N_E - 1], tmp[:, :, 0:N_E - 1]).then_inc(d["gate"], 1)
                            dve.wait_ge(d["gate"], e * 2 + 2)
                elif k == "moe_out":
                    t = s[2]
                    st = t // 2
                    if t == tq[0]:
                        for nn in (0, 1):
                            for st_ in sorted({t_ // 2 for t_ in tq}):
                                dve.wait_ge(*free_of(("gbc2", l, st_, nn)))
                    link(dve.tensor_tensor(ACC[:, t, :], ACC[:, t, :], GB[:, st, :], ALU.mult))
                    ins = dve.tensor_tensor(Xv[:, t, :], Xv[:, t, :], ACC[:, t, :], ALU.add)
                    ins.then_inc(resid_ready if l < DEPTH - 1 else out_ready, 1)


INPUTS = ["x", "c", "ctx", "c_ctx", "w_mod", "b_mod", "norm1_g", "norm2_g", "w_in", "w_out", "mla_qnorm_g",
          "mla_w_uq", "mla_kvnorm_g", "mla_w_ukv", "mla_q_g", "mla_k_g", "ml_conv_w", "ml_conv_b", "ml_w_q",
          "ml_w_k", "ml_w_v", "ml_gate_b", "ml_norm_g", "ml_skip", "na_q_g", "na_k_g", "na_rpb", "router_w",
          "router_b", "moe_w1", "moe_w3", "moe_w2"]


def shape_constants():
    t = np.arange(L)
    inv = 10000.0 ** (-np.arange(ROPE_D // 4, dtype=np.float32) / (ROPE_D // 4))
    ar = (t // GRID).astype(np.float32)[:, None] * inv
    ac = (t % GRID).astype(np.float32)[:, None] * inv
    cos = np.cos(np.concatenate([ar, ar, ac, ac], axis=-1))
    sin = np.sin(np.concatenate([-ar, ar, -ac, ac], axis=-1))
    table = np.zeros((P, 2, 2, ROPE_D), np.float32)
    for i in (0, 1):
        table[:, i, 0], table[:, i, 1] = cos[i * P:(i + 1) * P], sin[i * P:(i + 1) * P]
    rank = np.tile(np.arange(16, 0, -1, dtype=np.float32), (P, 1))
    ent = np.zeros((P, T, 2, 4), np.float32)
    tok = np.arange(P)[:, None] + P * np.arange(T)[None, :]
    for c in (0, 1):
        ent[:, :, c, 0] = tok
        ent[:, :, c, 2] = TOK * c + tok
    return np.ascontiguousarray(np.concatenate([table.reshape(P, -1), rank, ent.reshape(P, -1)],
                                               axis=1).astype(np.float32))


def kernel(**inputs):
    import numpy as _np
    import concourse.bacc as _bacc
    from concourse import mybir as _mybir
    from concourse.bass_utils import run_bass_kernel_spmd as _run

    nc = _bacc.Bacc("TRN2", target_bir_lowering=False, num_devices=1)
    arrays, aps = {}, {}
    data = {name: _np.ascontiguousarray(inputs[name]) for name in INPUTS}
    data["rope"] = shape_constants()
    for name, v in data.items():
        arrays[f"in_{name}"] = v
        aps[name] = nc.dram_tensor(f"in_{name}", v.shape, _mybir.dt.from_np(v.dtype), kind="ExternalInput").ap()
    aps["out"] = nc.dram_tensor("out_x", (1, L, D), F32, kind="ExternalOutput").ap()
    build(nc, aps)
    r = _run(nc, [arrays], core_ids=[0])
    return r.results[0]["out_x"]
```

```python
from contextlib import ExitStack

import numpy as np

import concourse.bass as bass
from concourse import mybir

F32 = mybir.dt.float32
U32 = mybir.dt.uint32
ALU = mybir.AluOpType
ACT = mybir.ActivationFunctionType
AX = mybir.AxisListType

P = 128
D = 1024
KD = D // P
DEPTH = 2
L = 256
T = 4
TOK = T * P
EPS = 1e-6
Q_RANK, KV_RANK, ROPE_D, NOPE_D, V_D = 256, 128, 32, 64, 64
QK_D = NOPE_D + ROPE_D
MLA_H = 6
ML_H, ML_D = 4, 96
ML_W = ML_H * ML_D
NA_H, NA_D = 4, 64
NA_W = NA_H * NA_D
GRID = 64
WIN_R, WIN_C = 8, 16
ROWS = L // GRID
N_E, N_G, FF = 16, 4, 256
OFF_Q = 0
OFF_U = Q_RANK + KV_RANK + ROPE_D
OFF_Z = OFF_U + ML_W
OFF_G = OFF_Z + ML_W
OFF_NQ = OFF_G + 4 * ML_H
OFF_NK = OFF_NQ + NA_W
N_IN = OFF_NK + 2 * NA_W
CAP = P
NOWHERE = 65536.0
NEG = -1e30
BIG = 1e30

PA, PG, PNQ, PNK, PNV = 0, OFF_U, OFF_U + 16, OFF_U + 16 + NA_W, OFF_U + 16 + 2 * NA_W
PW = OFF_U + 16 + 3 * NA_W
CHUNK = {"A": (OFF_Q, OFF_U, PA), "B": (OFF_G, 16 + NA_W, PG), "C": (OFF_NK, 2 * NA_W, PNK)}


def tiles_q(l):
    return [0, 1, 2, 3] if l < DEPTH - 1 else [2, 3]


def allowed(d, t, j):
    if t // 2 != j // 2:
        return t >= 2
    return j <= t if d == 0 else j >= t


def runs(l, d, j, diagonal):
    ts = [t for t in tiles_q(l) if allowed(d, t, j) and (diagonal or t != j)]
    out = []
    for t in ts:
        if out and out[-1][1] == t:
            out[-1][1] = t + 1
        else:
            out.append([t, t + 1])
    return out


def layer_of(s):
    return s[2] if s[0] in ("S", "ET", "PV", "OM", "OT") else s[1]


def p_cols(s):
    _, l, w, t = s
    c, n = CHUNK[w][2], CHUNK[w][1]
    if t not in tiles_q(l):
        if w == "A":
            return Q_RANK, n - Q_RANK
        if w == "B":
            return PG, 16
    return c, n


def keys_of(s):
    return TOK if s[3] >= 2 else L


def qkT_jobs(s):
    return [s + (w, i) for w in ("q", "k") if w == "k" or s[2] in tiles_q(s[1]) for i in (0, 1)]


PACK_DMAS = DEPTH * 9
PARAM_DMAS = DEPTH * 5 + 3
MODS = 12
MOD_FIRST = 4
MLN_MODS = (2, 2)
ROUTE_MODS = (3, 2)
TAIL_MODS = 3


def weight_pieces():
    out = []
    out += [("mod", 0, i) for i in range(MOD_FIRST)]
    for l in range(DEPTH):
        out += [("w_u", l), ("w_B", l), ("w_A", l), ("w_C", l), ("w_z", l)]
        out += late_mods(l)
        out += [("wo_mla", l), ("wo_ml", l), ("wo_na", l)]
        out += route_mods(l)
        out += [("w13", l, e) for e in range(N_E)]
        out += tail_mods(l)
    return out


def late_mods(l):
    n = ROUTE_MODS[l] + (TAIL_MODS if l < DEPTH - 1 else 0)
    return all_late_mods(l)[:-n]


def route_mods(l):
    n = len(late_mods(l))
    return all_late_mods(l)[n:n + ROUTE_MODS[l]]


def tail_mods(l):
    return all_late_mods(l)[len(late_mods(l)) + ROUTE_MODS[l]:]


def all_late_mods(l):
    return [("mod", l, i) for i in range(MOD_FIRST, MODS)] + [("mod", l + 1, i) for i in range(MOD_FIRST)
                                                              if l < DEPTH - 1]


def raw_bank(l, j):
    if l < DEPTH - 1:
        return (j, 0) if j < 2 else (2, (j - 2) * L - L)
    return j // 2, (j % 2) * L - L


def raw_banks(l):
    return raw_bank(l, T - 1)[0] + 1


def spread(steps, fill):
    out, done = [], 0
    for i, st in enumerate(steps):
        out.append(st)
        while done < len(fill) and (done + 1) * len(steps) <= (i + 1) * (len(fill) + 1):
            out += fill[done]
            done += 1
    return out + [x for g in fill[done:] for x in g]


def unit_steps(l, b):
    units = [u for u in UNITS if u[0] == b and u[1] == l]
    s = []
    for i in range(len(units) + 3):
        if i < len(units):
            s += [("S",) + units[i]]
        if 0 <= i - 2 < len(units):
            s += [("ET",) + units[i - 2]]
        if 0 <= i - 3:
            s += [("PV",) + units[i - 3]]
        if 0 <= i - 4 and units[i - 4][4]:
            s += [("OT",) + units[i - 4]]
        if 0 <= i - 3 and units[i - 3][4]:
            s += [("OM",) + units[i - 3]]
    return s + [("OT",) + units[-1]]


def merge(x, y):
    n, out, j = len(x), [], 0
    for i, st in enumerate(x):
        out.append(st)
        while j < len(y) and j * n < (i + 1) * len(y):
            out.append(y[j])
            j += 1
    return out + y[j:]


def make_schedule():
    s = []
    for l in range(DEPTH):
        tq = tiles_q(l)
        sq = sorted({t // 2 for t in tq})
        if l == 0:
            s += [(k, l, i) for i in range(MOD_FIRST - 1) for k in ("mod", "modT")]
        if l == 0:
            s += [("norm", l, 1, t) for t in range(T)]
            s += [("mod", l, MOD_FIRST - 1), ("modT", l, MOD_FIRST - 1), ("modfin", l, 1)]
        s += [("hT", l, 1, st, kp) for st in (0, 1) for kp in range(4)]
        s += [("pu", l, h) for h in range(ML_H)]
        s += [("pP", l, "B", t) for t in range(T)] + [("gates", l)]
        s += [("pP", l, "A", 0)] + [("gT", l, t) for t in range(T)] + [("pP", l, "A", 1), ("rows", l)]
        s += [("pP", l, "A", 2), ("cnorm", l, 0), ("pP", l, "A", 3), ("cnorm", l, 1), ("pP", l, "C", 0)]
        s += [("conv", l, 0), ("pP", l, "C", 1), ("cnorm", l, 2), ("cnorm", l, 3), ("conv", l, 1)]
        s += [("pP", l, "C", 2), ("nan", l, 0), ("nan", l, 1), ("conv", l, 2)]
        s += [("pP", l, "C", 3), ("cols", l), ("nan", l, 2), ("conv", l, 3)]
        s += [("mv", l, t) for t in range(T)] + [("pz", l, 0), ("nan", l, 3), ("pz", l, 1)]
        s += [("mqk", l, 0), ("nT", l, 0), ("pz", l, 2), ("mqk", l, 1), ("nT", l, 1), ("pz", l, 3)]
        s += [("mqk", l, 2), ("nT", l, 2), ("mqk", l, 3), ("nT", l, 3)]
        late = late_mods(l)
        turn = lambda m: ("modT",) + m[1:]
        for h in range(ML_H):
            s += [("mst", l, h), ("mgrid", l, h, 0), ("mgrid", l, h, 1), late[h], ("mpv", l, h, 0), ("mpv", l, h, 1)]
            s += [turn(late[h])]
        late = late[ML_H:]
        n = MLN_MODS[l]
        s += [("mln", l), late[0]]
        for i in range(1, n):
            s += [late[i], turn(late[i - 1])]
        s += [turn(late[n - 1])] + [("mlT", l, h) for h in range(ML_H)]
        prep = []
        for t in range(T + 1):
            now, last = t < T, t > 0
            prep += ([("cT", l, t)] if now else []) + ([("uqn", l, t - 1)] if last else [])
            prep += ([("uqk", l, t)] if now else []) + ([("qkT", l, t - 1)] if last else [])
            prep += [("uqs", l, t)] if now else []
        late = late[n:]
        fill = [[p] + ([turn(late[i - 1])] if i else []) for i, p in enumerate(late)]
        if fill:
            fill.append([turn(late[-1])])
        s += spread(merge(prep, unit_steps(l, 1)), fill) + unit_steps(l, 0)
        s += [("modfin", l, 2)]
        s += [("gbc", l, 1, st) for st in sq]
        for t in tq:
            s += [("wo", l, t, 0)]
            if t == 2 and 0 in sq:
                s += [("hT", l, 2, 0, kp) for kp in range(4)]
            s += [("wo", l, t, 1), ("norm", l, 2, t)]
            if t == 3 and 0 in sq:
                s += [("pfx", l, 0)]
            if t == 2 and 0 in sq:
                s += [("router", l, 0), ("rT", l, 0)]
        s += [("h2T", l, t, n) for t in tq if t < 2 for n in (0, 1)]
        s += [("hT", l, 2, 1, kp) for kp in range(4)] + [("router", l, 1), ("rT", l, 1)]
        s += [("h2T", l, t, n) for t in (2, 3) for n in (0, 1)]
        last = None
        for i, m in enumerate(route_mods(l)):
            if i == len(route_mods(l)) - 2:
                s += [("pfx", l, 1), ("slots", l)]
            s += [m] + ([turn(last)] if last else [])
            last = m
        s += [turn(last), ("gbc2", l)]
        s += [("xg", l, e) for e in (0, 1, 2)] + [("xT", l, 0), ("ab", l, 0), ("xT", l, 1)]
        for e in range(N_E):
            s += [("ab", l, e + 1)] if e + 1 < N_E else []
            s += [("yT", l, e)]
            s += [("xT", l, e + 2)] if e + 2 < N_E else []
            s += [("y", l, e)]
            s += [("xg", l, e + 3)] if e + 3 < N_E else []
            s += [("ys", l, e)]
        s += [("dense", l)]
        tail = tail_mods(l)
        more = [[m] + ([turn(tail[i - 1])] if i else []) for i, m in enumerate(tail)]
        more += [[turn(tail[-1]), ("modfin", l + 1, 1)]] if tail else []
        for i, t in enumerate(tq):
            s += [("comb", l, t)] + (more.pop(0) if more else []) + [("moe_out", l, t)]
            if l < DEPTH - 1 and i:
                s += [("norm", l + 1, 1, tq[i - 1])]
        if l < DEPTH - 1:
            s += [("norm", l + 1, 1, tq[-1])]
        s += [x for g in more for x in g]
    return s


UNITS = [(b, l, t, h, h == nh - 1) for l in range(DEPTH) for b, nh in ((1, NA_H), (0, MLA_H))
         for t in tiles_q(l) for h in range(nh)]
UNIT_AT = {u: i for i, u in enumerate(UNITS)}


def build(nc, a):
    pieces = weight_pieces()
    piece_at = {p: i for i, p in enumerate(pieces)}
    SLOTS = 3
    schedule = make_schedule()

    RING = 6
    jobs = []
    last_job_of_piece = {}

    def add(key, piece=None):
        jobs.append(key)
        if piece is not None:
            last_job_of_piece[piece] = key

    for st in schedule:
        k, l = st[0], layer_of(st)
        if k == "mod":
            add(st, st)
        elif k == "modT":
            add(st)
        elif k == "hT":
            add(st)
        elif k == "pu":
            add(st, ("w_u", l))
        elif k == "pz":
            add(st, ("w_z", l))
        elif k == "pP":
            add(st, ("w_" + st[2], l))
        elif k in ("gT", "cols"):
            add(st)
        elif k == "mv":
            add(st)
        elif k == "mqk":
            add(st + ("q",))
            add(st + ("k",))
        elif k == "mst":
            for j in range(raw_banks(l)):
                add(st + (j,))
        elif k == "mgrid":
            add(st)
        elif k == "mlT":
            add(st)
        elif k == "cT":
            add(st)
        elif k == "uqk":
            if st[2] in tiles_q(l):
                add(st + ("q", 0))
                add(st + ("q", 1))
            add(st + ("k", 0))
            add(st + ("k", 1))
        elif k == "qkT":
            if st[2] in tiles_q(l):
                add(st + ("q", 0))
                add(st + ("q", 1))
            add(st + ("k", 0))
            add(st + ("k", 1))
        elif k == "nT":
            add(st)
        elif k in ("S", "ET"):
            add(st)
        elif k == "OT":
            add(st)
        elif k == "gbc":
            add(st + (0,))
            add(st + (1,))
        elif k == "wo":
            add(st)
            for p in ("wo_mla", "wo_ml", "wo_na"):
                last_job_of_piece[(p, l)] = st
        elif k in ("router", "rT", "h2T", "pfx"):
            add(st)
        elif k == "xT":
            add(st + (0,))
            add(st + (1,))
        elif k == "gbc2":
            for s_ in sorted({t // 2 for t in tiles_q(l)}):
                add(st + (s_, 0))
                add(st + (s_, 1))
        elif k == "ab":
            add(st, ("w13", l, st[2]))
        elif k == "yT":
            add(("y",) + st[1:] + ("T",))
        elif k == "y":
            add(st + (0,))
            add(st + (1,), ("w2", l, st[2]))
    job_at = {k: i for i, k in enumerate(jobs)}
    assert len(job_at) == len(jobs)
    acc_jobs = [st for st in schedule if st[0] == "mpv" or st[0] == "OT"]
    acc_at = {k: i for i, k in enumerate(acc_jobs)}
    pv_steps = [st for st in schedule if st[0] in ("mpv", "PV")]
    pv_at = {k: i + 1 for i, k in enumerate(pv_steps)}

    ctx = ExitStack()
    with ctx:
        def sb(name, cols, parts=P):
            return ctx.enter_context(nc.sbuf_tensor(name, [parts, cols], F32))

        def sem(name):
            return ctx.enter_context(nc.semaphore(name))

        bank = [ctx.enter_context(nc.psum_tensor(f"bank{i}", [P, 512], F32)) for i in range(8)]

        def view(reg, off, *shape, parts=P):
            n = int(np.prod(shape))
            ap = reg[0:parts, off:off + n]
            if len(shape) == 2:
                return ap.rearrange("p (a b) -> p a b", a=shape[0])
            if len(shape) == 3:
                return ap.rearrange("p (a b c) -> p a b c", a=shape[0], b=shape[1])
            return ap

        X = sb("X", T * D)
        Xv = view(X, 0, T, D)
        WORK = sb("WORK", 4096)
        XS = view(WORK, 0, T, D)
        H = sb("H", 4608)
        HT = view(H, 0, KD, TOK)
        MLAT = view(H, 0, 3, TOK)
        HS = view(H, 0, T, ML_W)
        MLT = view(H, 1536, ML_H, TOK, parts=ML_D)
        NAT = view(H, 3584, 2, TOK)
        PR = sb("PROJ", T * PW)
        PRv = view(PR, 0, T, PW)
        M = sb("BRANCH", 9984)
        UT = view(M, 0, ML_H, TOK, parts=ML_D)
        MQ = UT
        ZS = view(M, 2048, ML_H, TOK, parts=ML_D)
        UC = view(M, 4096, ML_H, TOK, parts=ML_D)
        MK = view(M, 6144, ML_H, TOK, parts=ML_D)
        MV = view(M, 8192, T, ML_H, 97)
        CT = view(M, 0, 3, TOK)
        QTM = [view(M, 1536 + 576 * i, MLA_H, QK_D) for i in (0, 1)]
        KTM = [view(M, 2688 + 576 * i, MLA_H, QK_D) for i in (0, 1)]
        QT = view(M, 3840, MLA_H, TOK, parts=QK_D)
        KT = view(M, 6912, MLA_H, TOK, parts=QK_D)
        VV = PRv[:, :, 0:MLA_H * V_D].rearrange("p t (h e) -> p t h e", h=MLA_H)
        XG = [view(M, 1024 * i, D) for i in (0, 1, 2)]
        OH = [view(M, 3072 + 64 * k, T * N_E) for k in (0, 1)]
        INCL = view(M, 3200, P)
        PICK = view(M, 3328, T * N_E)
        PROD = view(M, 3392, T * N_E)
        ASSIGN = view(M, 3456, T * N_E)
        TABS = view(M, 3520, N_E, 4)
        SLOTF = view(M, 3584, 2 * T)
        ACC = view(M, 0, T, D)
        GB = view(M, 4096, 2, D)
        HID = [view(M, 6144 + 256 * i, FF) for i in (0, 1)]
        RROW = view(M, 6144, TOK, parts=N_E)
        HIDT = [view(M, 6656 + 256 * i, 2, P) for i in (0, 1)]
        TH = [view(M, 7168 + 256 * i, FF) for i in (0, 1)]
        YT = view(M, 7680, 512)
        YO = [view(M, 7680 + 1024 * i, D) for i in (0, 1)]
        N_R = sb("NA", 4096)
        XGT = [view(N_R, 1024 * i, KD, P) for i in (0, 1)]
        NQT = view(N_R, 0, 2, TOK)
        NKT = view(N_R, 1024, 2, TOK)
        BIAS = view(N_R, 2048, 2, NA_H, L)
        RINGW = sb("RINGW", SLOTS * 4096)
        W2R = sb("W2R", 2 * 2048)
        MROW = [W2R[0:2, 3072 + 512 * i:3584 + 512 * i] for i in (0, 1)]
        NEGMU = sb("NEGMU", 2 * TOK, ML_H)
        NEGMUv = view(NEGMU, 0, 2, TOK, parts=ML_H)
        ROW = view(WORK, 0, 4, TOK, parts=ML_H)
        GEM = view(WORK, 2048, 4, TOK, parts=ML_H)
        GRIDB = [view(WORK, 2048 * i, T, TOK) for i in (0, 1)]
        E_ = [view(WORK, 512 * i, TOK) for i in (0, 1)] + [view(N_R, 0, TOK), view(H, 0, TOK)]
        PT = [view(WORK, 1024 + 512 * i, 4, P) for i in (0, 1)]
        OM = view(WORK, 2048, MLA_H * V_D)
        SQN = view(M, 6144, 512)
        SQC = view(M, 6656, 384)
        SQU = [view(WORK, 2432 + 576 * i, MLA_H, QK_D) for i in (0, 1)]
        SWAP = [view(WORK, 3584 + 192 * i, MLA_H, ROPE_D) for i in (0, 1)]
        IDENT = sb("IDENT", P)
        PACK = M[:, 9984 - 3 * P:9984]
        COLS = sb("COLS", 3 * P)
        MODC = sb("MODC", DEPTH * 96)
        MODv = [view(MODC, 96 * l, 48, 2) for l in range(DEPTH)]
        AMOD = sb("AMOD", DEPTH * 32)
        AMv = [view(AMOD, 32 * l, 2, KD, 2) for l in range(DEPTH)]
        CS = sb("CS", 16)
        CSv = CS[:, :].rearrange("p (j k) -> p k j", j=2)
        TRI = sb("TRI", 2 * P)
        ROPE = sb("ROPE", 2 * 2 * ROPE_D + 16 + 8 * T)
        RANK = ROPE[:, 2 * 2 * ROPE_D:2 * 2 * ROPE_D + 16]
        ENT = view(ROPE, 2 * 2 * ROPE_D + 16, T, 2, 4)
        ROv = view(ROPE, 0, 2, 2, ROPE_D)
        BC = sb("BC", 2 * 352 + 16)
        GEMC = sb("GEMC", 4 * T * ML_H)
        GC = view(GEMC, 0, 4, T, ML_H)
        ST = sb("ST", 256)
        PAD = sb("PAD", 128, 56)
        RWT = sb("RWT", KD * N_E)
        RW = view(RWT, 0, KD, N_E)
        GATE = sb("GATE", T * N_E)
        GATEv = view(GATE, 0, T, N_E)
        RT = sb("RT", 448)
        IDX = ctx.enter_context(nc.sbuf_tensor("IDX", [P, 2 * T + 2 * N_E + 1], U32))
        SLOTU = IDX[:, 0:2 * T]
        TOKU = IDX[:, 2 * T:2 * T + N_E]
        PAIRU = IDX[:, 2 * T + N_E:2 * T + 2 * N_E]
        OVER = IDX[:, 2 * T + 2 * N_E:2 * T + 2 * N_E + 1]
        assert nc.sbuf_bytes_remaining >= 0

        c2 = lambda r: COLS[:, P + r:P + r + 1]
        c96 = lambda r, n=1: COLS[0:ML_D, 2 * P + r:2 * P + r + n]
        bc_qg = lambda l: BC[:, 352 * l:352 * l + 96]
        bc_kg = lambda l: BC[:, 352 * l + 96:352 * l + 192]
        bc_nq = lambda l: BC[:, 352 * l + 192:352 * l + 256]
        bc_nk = lambda l: BC[:, 352 * l + 256:352 * l + 320]
        bc_gb = lambda l: BC[:, 352 * l + 320:352 * l + 336]
        bc_rb = BC[:, 704:720]

        SHIFT = 2 * GRID + 1
        BROW = GRID * SHIFT
        scratch = nc.dram_tensor("bias_rows", [2 * NA_H * 7, BROW], F32, kind="Internal").ap()

        h2_rows = nc.dram_tensor("h2_rows", [TOK, D], F32, kind="Internal").ap()
        slots = [nc.dram_tensor(f"slots_{l}", [CAP * N_E, 4], F32, kind="Internal").ap() for l in range(DEPTH)]
        pairs = nc.dram_tensor("pairs", [2 * TOK, D], F32, kind="Internal").ap()

        full = [sem(f"bank_full_{i}") for i in range(RING)]
        free = [sem(f"bank_free_{i}") for i in range(RING)]
        slot_loaded = [sem(f"slot_loaded_{i}") for i in range(SLOTS)]
        w2_loaded = [sem(f"w2_loaded_{i}") for i in range(2)]
        pack_loaded = sem("pack_loaded")
        params_loaded = sem("params_loaded")
        small_loaded = sem("small_loaded")
        x_loaded = sem("x_loaded")
        pad_loaded = sem("pad_loaded")
        rows_stored = sem("rows_stored")
        bias_loaded = [sem(f"bias_loaded_{l}") for l in range(DEPTH)]
        bias_masked = sem("bias_masked")
        const_ready = sem("const_ready")
        pack_zero = sem("pack_zero")
        cond_loaded = sem("cond_loaded")
        cond_full = sem("cond_full")
        cols_full = sem("cols_full")
        cols_ready = sem("cols_ready")
        csilu_ready = sem("csilu_ready")
        mod_ready = sem("mod_ready")
        ssq_ready = sem("ssq_ready")
        mean_ready = sem("mean_ready")
        rstd_ready = sem("rstd_ready")
        xs_ready = sem("xs_ready")
        lf_ready = sem("lf_ready")
        lfa_ready = sem("lfa_ready")
        gates_ready = sem("gates_ready")
        rows_ready = sem("rows_ready")
        mv_ready = sem("mv_ready")
        conv_acc = sem("conv_acc")
        conv_tanh = sem("conv_tanh")
        uc_ready = sem("uc_ready")
        diag_ready = sem("diag_ready")
        grid_exp = sem("grid_exp")
        grid_ready = sem("grid_ready")
        pv_done = sem("pv_done")
        acc_free = sem("acc_free")
        hn_ready = sem("hn_ready")
        zs_tanh = sem("zs_tanh")
        cn_ready = sem("cn_ready")
        usq_ready = sem("usq_ready")
        qk_ready = sem("qk_ready")
        na_ready = sem("na_ready")
        nmax_ready = sem("nmax_ready")
        om_ready = sem("om_ready")
        resid_ready = sem("resid_ready")
        assign_ready = sem("assign_ready")
        moe_tanh = sem("moe_tanh")
        hid_ready = sem("hid_ready")
        out_ready = sem("out_ready")
        out_stored = sem("out_stored")
        em_in = sem("em_in")
        em_ready = sem("em_ready")
        gc_ready = sem("gc_ready")
        mlt_ready = sem("mlt_ready")
        slots_blank = sem("slots_blank")
        h2_stored = sem("h2_stored")
        xg_blank = sem("xg_blank")
        pairs_blank = sem("pairs_blank")
        route_ready = sem("route_ready")
        slots_stored = sem("slots_stored")
        slots_loaded = sem("slots_loaded")
        index_ready = sem("index_ready")
        xg_loaded = [sem(f"xg_loaded_{i}") for i in range(3)]
        ys_stored = [sem(f"ys_stored_{i}") for i in range(2)]
        pair_loaded = [sem(f"pair_loaded_{i}") for i in range(T)]
        dn = [{w: sem(f"dense_{w}_{l}") for w in ("loaded", "ab", "tanh", "half", "hid", "T", "ht", "y", "acc",
                                                 "zero", "gate", "stored", "reloaded")} for l in range(DEPTH)]
        dve_step = sem("dve_step")
        act_step = sem("act_step")
        pool_step = sem("pool_step")

        block = ctx.enter_context(nc.Block())

        def bank_of(key):
            return bank[job_at[key] % RING]

        def full_of(key):
            n = job_at[key]
            return full[n % RING], n // RING + 1

        def free_of(key):
            n = job_at[key]
            return free[n % RING], n // RING + 1

        def slot(p):
            i = piece_at[p]
            return RINGW[:, 4096 * (i % SLOTS):4096 * (i % SLOTS + 1)]

        def loaded(p):
            i = piece_at[p]
            return slot_loaded[i % SLOTS], 16 * loads_upto[i]

        parts_of = {"w13": 2}
        loads_upto = []
        seen = [0] * SLOTS
        for i, p in enumerate(pieces):
            seen[i % SLOTS] += parts_of.get(p[0], 1)
            loads_upto.append(seen[i % SLOTS])

        def tick(eng, s):
            eng.sem_inc(s, 1)

        rstd_keys = []
        for s in schedule:
            if s[0] in ("norm", "mln", "cnorm"):
                rstd_keys.append(s)
            elif s[0] in ("uqk", "nan"):
                rstd_keys.append(s)
        rstd_at = {k: i + 1 for i, k in enumerate(rstd_keys)}
        ssq_keys = [s for s in schedule if s[0] in ("norm", "cnorm")]
        ssq_at = {k: i + 1 for i, k in enumerate(ssq_keys)}

        def order(kind):
            return {s: i + 1 for i, s in enumerate(x for x in schedule if x[0] == kind)}

        norm_n, mv_n, conv_n, mqk_n = order("norm"), order("mv"), order("conv"), order("mqk")
        grid_n, mlT_n, cn_n, uqk_n = order("mgrid"), order("mlT"), order("cnorm"), order("uqk")
        nan_n, ab_n, pz_n = order("nan"), order("ab"), order("pz")
        OT_n, pfx_n = order("OT"), order("pfx")
        mod_n, modfin_n = order("mod"), order("modfin")
        mod_key = {n: s for s, n in mod_n.items()}
        grid_key = {n: s for s, n in grid_n.items()}
        OT_key = {n: s for s, n in OT_n.items()}
        expert_n = lambda l, e: l * N_E + e
        expert_key = lambda n: (n // N_E, n % N_E)

        resid_at, c = {}, 0
        for s in schedule:
            if (s[0] == "wo" and s[3]) or (s[0] == "moe_out" and s[1] < DEPTH - 1):
                c += 1
                resid_at[s[:3]] = c

        def resid_for(s):
            return resid_at[("wo", s[1], s[3])] if s[2] == 2 else resid_at[("moe_out", s[1] - 1, s[3])]

        def mpv_before(s):
            g = grid_key[grid_n[s] - 2]
            return pv_at[("mpv",) + g[1:]]

        def diagonal(s):
            t0 = tiles_q(s[1])[0]
            o = 2048 * (grid_n[s] % 2) + t0 * (TOK + P)
            b = WORK[:, o:o + P]
            return bass.AP(tensor=b.tensor, offset=b.offset,
                           ap=[list(b.ap[0]), [TOK + P, len(tiles_q(s[1]))], [1, P]])

        def conv_tmp(s):
            return WORK[0:ML_D, 512 * (s[2] % 2):512 * (s[2] % 2) + TOK]

        def ssq_cols(s):
            o = 176 + 2 * (ssq_at[s] % 4)
            return ST[:, o:o + 2]

        def exps(u):
            return E_[u % 3 + (u % 3 == 2 and UNITS[u][0] == 1)]

        def neg_max(u):
            return ST[:, 192 + u % 4:193 + u % 4]

        def exp_sums(u, n):
            b, l, t, h, _ = UNITS[u]
            o = 200 + 8 * (OT_n[("OT", b, l, t, (MLA_H, NA_H)[b] - 1, True)] % 4) + h
            return ST[:, o:o + n]

        def stat(n, w=16):
            return ST[:, 16 * (n % 4):16 * (n % 4) + w], ST[:, 64 + 16 * (n % 4):64 + 16 * (n % 4) + w]

        POOL_HALF = RT[:, 432:448]
        CIN = RT[0:16, 0:P]

        def rstd_width(s):
            if s[0] == "norm":
                return 1
            if s[0] == "mln":
                return 4 * len(tiles_q(s[1]))
            if s[0] == "cnorm":
                return 2
            return 12 if s[0] == "uqk" else 8

        SMALL_PARTS = 5

        def small_views(l):
            s = W2R
            wq = s[0:ML_D, 0:384].rearrange("p (h e) -> p h e", h=ML_H)
            wk = s[0:ML_D, 384:768].rearrange("p (h e) -> p h e", h=ML_H)
            wv = s[0:ML_D, 768:1152].rearrange("p (h e) -> p h e", h=ML_H)
            uq = s[:, 1152:2304].rearrange("p (k n) -> p k n", k=2)
            ukv = s[:, 2304:3072]
            return wq, wk, wv, uq, ukv

        @block.sync
        def _(sp):
            w2_keys = [(l, e) for l in range(DEPTH) for e in range(N_E)]

            def load_mod(p, done):
                c = 512 * p[2]
                sp.dma_start(slot(p).rearrange("p (k n) -> p k n", k=KD),
                             a["w_mod"][p[1]].rearrange("(k p) n -> p k n", p=P)[:, :, c:c + 512]).then_inc(done, 16)

            def dense_weights(l):
                nt = len(tiles_q(l))
                sp.wait_ge(route_ready, pfx_n[("pfx", l, 1)])
                over = sp.value_load(OVER[0:1, :])
                with sp.If(over > 0):
                    sp.wait_ge(*full_of(("y", l, N_E - 1, 1)))
                    for p in tail_mods(l):
                        sp.wait_ge(*loaded(p))
                    with sp.Fori(0, N_E) as e:
                        sp.wait_ge(dn[l]["acc"], e * nt + 1)
                        w13 = RINGW[:, 0:4096].rearrange("p (k n) -> p k n", k=KD)
                        w2 = RINGW[:, 4096:6144].rearrange("p (k n) -> p k n", k=2)
                        sp.dma_start(w13[:, :, 0:FF], a["moe_w1"][l][e].rearrange("(k p) f -> p k f", p=P)).then_inc(
                            dn[l]["loaded"], 16)
                        sp.dma_start(w13[:, :, FF:2 * FF],
                                     a["moe_w3"][l][e].rearrange("(k p) f -> p k f", p=P)).then_inc(
                            dn[l]["loaded"], 16)
                        sp.dma_start(w2, a["moe_w2"][l][e].rearrange("(k p) n -> p k n", p=P)).then_inc(
                            dn[l]["loaded"], 16)
                    sp.wait_ge(dn[l]["acc"], N_E * nt + 1)
                    n = expert_n(l, N_E)
                    sp.wait_ge(ys_stored[0], 16 * ((n + 1) // 2))
                    sp.wait_ge(ys_stored[1], 16 * (n // 2))
                    for t in tiles_q(l):
                        sp.dma_start(pairs[t * P:(t + 1) * P, :], ACC[:, t, :]).then_inc(dn[l]["stored"], 16)
                        sp.dma_start(pairs[TOK + t * P:TOK + (t + 1) * P, :], XS[:, t, :]).then_inc(
                            dn[l]["stored"], 16)
                    sp.wait_ge(dn[l]["stored"], 32 * nt)
                    for p in tail_mods(l):
                        load_mod(p, dn[l]["reloaded"])
                    if tail_mods(l):
                        sp.wait_ge(dn[l]["reloaded"], 16 * TAIL_MODS)

            for i, p in enumerate(pieces):
                if p[0] == "w_u" and p[1]:
                    dense_weights(p[1] - 1)
                if p[0] == "w_z":
                    if p[1]:
                        for e in (N_E - 2, N_E - 1):
                            sp.wait_ge(*full_of(last_job_of_piece[("w2", p[1] - 1, e)]))
                    wq, wk, wv, uq, ukv = small_views(p[1])
                    for w, name in ((wq, "ml_w_q"), (wk, "ml_w_k"), (wv, "ml_w_v")):
                        sp.dma_start(w, a[name][p[1]].rearrange("h d e -> d h e")).then_inc(small_loaded, 16)
                    sp.dma_start(uq, a["mla_w_uq"][p[1]].rearrange("(k p) n -> p k n", p=P)).then_inc(
                        small_loaded, 16)
                    sp.dma_start(ukv, a["mla_w_ukv"][p[1]]).then_inc(small_loaded, 16)
                if i == 0:
                    sp.wait_ge(cond_loaded, 32)
                elif i == 2:
                    sp.wait_ge(pack_loaded, 16 * PACK_DMAS)
                elif i == 3:
                    sp.dma_start(Xv[:, 0:2, :], a["ctx"].rearrange("b (t p) d -> p (b t) d", p=P)).then_inc(
                        x_loaded, 16)
                    sp.dma_start(Xv[:, 2:4, :], a["x"].rearrange("b (t p) d -> p (b t) d", p=P)).then_inc(
                        x_loaded, 16)
                if i >= SLOTS:
                    s, v = full_of(last_job_of_piece[pieces[i - SLOTS]])
                    sp.wait_ge(s, v)
                dst, k, l = slot(p), p[0], p[1]
                done = slot_loaded[i % SLOTS]
                w_in = a["w_in"][l].rearrange("(k p) n -> p k n", p=P)
                if k == "mod":
                    load_mod(p, done)
                elif k in ("w_u", "w_z", "w_A", "w_B", "w_C"):
                    c, n = {"w_u": (OFF_U, ML_W), "w_z": (OFF_Z, ML_W)}.get(k) or CHUNK[k[-1]][:2]
                    sp.dma_start(dst[:, 0:KD * n].rearrange("p (k n) -> p k n", k=KD),
                                 w_in[:, :, c:c + n]).then_inc(done, 16)
                elif k == "wo_mla":
                    sp.dma_start(dst[:, 0:3 * D].rearrange("p (k n) -> p k n", k=3),
                                 a["w_out"][l][0:384, :].rearrange("(k p) n -> p k n", p=P)).then_inc(done, 16)
                elif k == "wo_ml":
                    sp.dma_start(dst[0:ML_D, :].rearrange("p (k n) -> p k n", k=ML_H),
                                 a["w_out"][l][384:768, :].rearrange("(k p) n -> p k n", p=ML_D)).then_inc(done, 16)
                elif k == "wo_na":
                    sp.dma_start(dst[:, 0:2 * D].rearrange("p (k n) -> p k n", k=2),
                                 a["w_out"][l][768:1024, :].rearrange("(k p) n -> p k n", p=P)).then_inc(done, 16)
                else:
                    e = p[2]
                    w13 = dst.rearrange("p (k n) -> p k n", k=KD)
                    sp.dma_start(w13[:, :, 0:FF], a["moe_w1"][l, e].rearrange("(k p) f -> p k f", p=P)).then_inc(
                        done, 16)
                    sp.dma_start(w13[:, :, FF:2 * FF], a["moe_w3"][l, e].rearrange("(k p) f -> p k f", p=P)).then_inc(
                        done, 16)
                    n = w2_keys.index((l, e))
                    if e >= 2:
                        sp.wait_ge(*full_of(last_job_of_piece[("w2",) + w2_keys[n - 2]]))
                    elif e == 0:
                        sp.wait_ge(*full_of(("uqk", l, T - 1, "k", 1)))
                        for m in route_mods(l):
                            sp.wait_ge(*full_of(("modT",) + m[1:]))
                    sp.dma_start(W2R[:, 2048 * (n % 2):2048 * (n % 2 + 1)].rearrange("p (k n) -> p k n", k=2),
                                 a["moe_w2"][l, e].rearrange("(k p) n -> p k n", p=P)).then_inc(w2_loaded[n % 2], 16)
            dense_weights(DEPTH - 1)
            for i in range(2):
                sp.wait_ge(out_ready, i + 1)
                sp.dma_start(a["out"][0, i * P:(i + 1) * P, :], Xv[:, 2 + i, :]).then_inc(out_stored, 16)
            sp.wait_ge(out_stored, 32)

        def w2_of(l, e):
            n = l * N_E + e
            return (W2R[:, 2048 * (n % 2):2048 * (n % 2 + 1)].rearrange("p (k n) -> p k n", k=2),
                    w2_loaded[n % 2], 16 * (n // 2 + 1))

        @block.gpsimd
        def _(pool):
            step = [0]

            def link(ins):
                step[0] += 1
                ins.then_inc(pool_step, 1)
                pool.wait_ge(pool_step, step[0])

            link(pool.memset(IDENT[:, :], 0.0))
            pool.affine_select(out=IDENT[:, :], in_=IDENT[:, :], compare_op=ALU.not_equal, fill=1.0, base=0,
                               pattern=[[-1, P]], channel_multiplier=1).then_inc(const_ready, 1)
            pool.wait_ge(const_ready, 1)
            link(pool.memset(TRI[:, :], 0.0))
            link(pool.affine_select(out=TRI[:, 0:P], in_=TRI[:, 0:P], compare_op=ALU.is_ge, fill=NEG, base=0,
                                    pattern=[[1, P]], channel_multiplier=-1))
            link(pool.affine_select(out=TRI[:, P:2 * P], in_=TRI[:, P:2 * P], compare_op=ALU.is_ge, fill=NEG,
                                    base=0, pattern=[[-1, P]], channel_multiplier=1))
            link(pool.memset(POOL_HALF, -0.5))
            for l in range(DEPTH):
                for dst, name in ((bc_qg(l), "mla_q_g"), (bc_kg(l), "mla_k_g"), (bc_nq(l), "na_q_g"),
                                  (bc_nk(l), "na_k_g"), (bc_gb(l), "ml_gate_b")):
                    pool.dma_start(dst, a[name][l].partition_broadcast(P)).then_inc(params_loaded, 16)
            pool.dma_start(bc_rb, a["router_b"].partition_broadcast(P)).then_inc(params_loaded, 16)
            pool.dma_start(RW, a["router_w"].rearrange("(k p) n -> p k n", p=P)).then_inc(params_loaded, 16)
            pool.dma_start(ROPE[:, :], a["rope"]).then_inc(params_loaded, 16)
            def prepare_dram():
                link(pool.memset(PAD[:, :], 0.0))
                blank = view(N_R, 0, N_E, 4)
                link(pool.memset(blank, NOWHERE))
                link(pool.memset(blank[:, :, 1:2], 0.0))
                for l in range(DEPTH):
                    pool.dma_start(slots[l].rearrange("(p e) c -> p e c", e=N_E), blank).then_inc(slots_blank, 16)
                lo = GRID - 1 - (WIN_C - 1)
                for l in range(DEPTH):
                    for h in range(NA_H):
                        pool.dma_start(PAD[28 * l + 7 * h:28 * l + 7 * h + 7, lo:lo + 2 * WIN_C - 1],
                                       a["na_rpb"][l, h, WIN_R - ROWS:WIN_R + ROWS - 1, :]).then_inc(pad_loaded, 16)
                pool.wait_ge(pad_loaded, 16 * DEPTH * NA_H)
                pool.dma_start(scratch.rearrange("r (c i) -> r c i", i=SHIFT)[:, :, 0:2 * GRID - 1],
                               PAD[:, 0:2 * GRID - 1].unsqueeze(1).broadcast_to([2 * NA_H * 7, GRID, 2 * GRID - 1])
                               ).then_inc(rows_stored, 16)
                pool.wait_ge(rows_stored, 16)
                pool.wait_ge(slots_blank, 16 * DEPTH)

            def load_bias(l):
                for r in range(ROWS):
                    for h in range(NA_H):
                        src = bass.AP(tensor=scratch.tensor,
                                      offset=(28 * l + 7 * h + ROWS - 1 - r) * BROW + GRID - 1,
                                      ap=[[2 * GRID, GRID], [BROW, ROWS], [1, GRID]])
                        q0 = (r % 2) * GRID
                        pool.dma_start(BIAS[q0:q0 + GRID, r // 2, h, :].rearrange("p (j c) -> p j c", j=ROWS),
                                       src).then_inc(bias_loaded[l], 16)
                pool.wait_ge(bias_loaded[l], 16 * ROWS * NA_H)
                for q0 in (0, GRID):
                    b = N_R[q0:q0 + GRID, 2048:4096].rearrange("p (m c) -> p m c", c=GRID)
                    lowc = GRID - WIN_C
                    link(pool.affine_select(out=b[:, :, 0:lowc], in_=b[:, :, 0:lowc], compare_op=ALU.is_ge, fill=NEG,
                                            base=WIN_C // 2, pattern=[[0, 32], [1, lowc]], channel_multiplier=-1))
                    ins = pool.affine_select(out=b[:, :, WIN_C:], in_=b[:, :, WIN_C:], compare_op=ALU.is_ge,
                                             fill=NEG, base=WIN_C // 2 - 1 - WIN_C,
                                             pattern=[[0, 32], [-1, lowc]], channel_multiplier=1)
                    ins.then_inc(bias_masked, 1)
                    pool.wait_ge(bias_masked, 2 * l + (1 if q0 == 0 else 2))

            for s in schedule:
                if s in rstd_at:
                    m, r = stat(rstd_at[s])
                    w = rstd_width(s)
                    pool.wait_ge(mean_ready, rstd_at[s])
                    pool.tensor_tensor(r[:, 0:w], m[:, 0:w], POOL_HALF[:, 0:w], ALU.pow).then_inc(rstd_ready, 1)
                k, l = s[0], layer_of(s)
                if k == "gates":
                    if l == 0:
                        prepare_dram()
                    if l:
                        pool.wait_ge(nmax_ready, max(UNIT_AT[u] for u in UNITS if u[1] == l - 1) + 1)
                    load_bias(l)
                elif k == "router" and s[2] == min(tiles_q(l)) // 2:
                    pool.wait_ge(nmax_ready, max(UNIT_AT[u] for u in UNITS if u[1] == l) + 1)
                    pool.memset(M[:, 0:3072], 0.0).then_inc(xg_blank, 1)
                    pool.wait_ge(xg_blank, l + 1)
                    if l == 0:
                        pool.dma_start(pairs.rearrange("(j p) d -> p j d", p=P),
                                       XG[2].unsqueeze(1).broadcast_to([P, 2 * T, D])).then_inc(pairs_blank, 16)
                elif k == "pfx":
                    pool.wait_ge(route_ready, pfx_n[s])
                    for t in (2 * s[2], 2 * s[2] + 1):
                        for c in (0, 1):
                            pool.indirect_dma_start(
                                slots[l], bass.IndirectOffsetOnAxis(ap=SLOTU[:, 2 * t + c:2 * t + c + 1], axis=0),
                                ENT[:, t, c, :], None, bounds_check=CAP * N_E - 1, oob_is_err=False).then_inc(
                                slots_stored, 16)
                elif k == "slots":
                    pool.wait_ge(slots_stored, 32 * sum(len(tiles_q(m)) for m in range(l + 1)))
                    pool.dma_start(TABS, slots[l].rearrange("(p e) c -> p e c", e=N_E)).then_inc(slots_loaded, 16)
                elif k == "xg":
                    e = s[2]
                    n = expert_n(l, e)
                    if e == 0:
                        pool.wait_ge(index_ready, l + 1)
                        pool.wait_ge(h2_stored, 16 * sum(len(tiles_q(m)) for m in range(l + 1)))
                    if e == 2:
                        pool.wait_ge(pairs_blank, 16)
                    if e >= 3:
                        pool.wait_ge(*full_of(("xT", l, e - 3, 1)))
                    pool.indirect_dma_start(XG[n % 3], None, h2_rows,
                                            bass.IndirectOffsetOnAxis(ap=TOKU[:, e:e + 1], axis=0),
                                            bounds_check=TOK - 1, oob_is_err=False).then_inc(xg_loaded[n % 3], 16)
                elif k == "ys":
                    e = s[2]
                    n = expert_n(l, e)
                    pool.wait_ge(*free_of(("y", l, e, 0)))
                    pool.wait_ge(*free_of(("y", l, e, 1)))
                    pool.indirect_dma_start(pairs, bass.IndirectOffsetOnAxis(ap=PAIRU[:, e:e + 1], axis=0),
                                            YO[n % 2], None, bounds_check=2 * TOK - 1, oob_is_err=False).then_inc(
                        ys_stored[n % 2], 16)

        @block.scalar
        def _(act):
            step = [0]

            def link(ins):
                step[0] += 1
                ins.then_inc(act_step, 1)
                act.wait_ge(act_step, step[0])

            for r, name in ((0, "c_ctx"), (8, "c")):
                src = a[name] if name == "c_ctx" else a[name][0]
                act.dma_start(CIN[r:r + 8, :], src.rearrange("(r p) -> r p", p=P)).then_inc(cond_loaded, 16)
            act.wait_ge(pack_zero, 1)

            def pack(r0, r1, c, n, src):
                act.dma_start(PACK[r0:r1, c:c + n], src).then_inc(pack_loaded, 16)

            for l in range(DEPTH):
                r = 64 * l
                pack(r, r + 48, 0, P, a["b_mod"][l].rearrange("(r p) -> r p", p=P))
                pack(r + 48, r + 56, 0, P, a["norm1_g"][l].rearrange("(r p) -> r p", p=P))
                pack(r + 56, r + 64, 0, P, a["norm2_g"][l].rearrange("(r p) -> r p", p=P))
                pack(16 + 3 * l, 18 + 3 * l, P, P, a["mla_qnorm_g"][l].rearrange("(r p) -> r p", p=P))
                pack(18 + 3 * l, 19 + 3 * l, P, P, a["mla_kvnorm_g"][l:l + 1, :])
                q = 24 * l
                for o, name in ((0, "ml_norm_g"), (4, "ml_skip"), (8, "ml_conv_b")):
                    pack(q + o, q + o + 4, 2 * P, ML_D, a[name][l].rearrange("(r p) -> r p", p=ML_D))
                pack(q + 12, q + 24, 2 * P, ML_D, a["ml_conv_w"][l].rearrange("k (r p) -> (k r) p", p=ML_D))
            act.wait_ge(cond_full, 1)
            act.activation(RT[:, 128:144], bank[7][:, 0:16], ACT.Tanh, scale=0.5).then_inc(csilu_ready, 1)
            for s in schedule:
                k, l = s[0], layer_of(s)
                if k == "mod":
                    n = mod_n[s]
                    act.wait_ge(*full_of(s))
                    if n > 2:
                        act.wait_ge(*full_of(("modT",) + mod_key[n - 2][1:]))
                    act.activation(MROW[n % 2], bank_of(s)[0:2, :], ACT.Copy).then_inc(free_of(s)[0], 1)
                elif k == "norm":
                    t = s[3]
                    if (l, s[2]) == (0, 1):
                        act.wait_ge(x_loaded, 32)
                    else:
                        act.wait_ge(resid_ready, resid_for(s))
                    if ssq_at[s] > 4:
                        act.wait_ge(mean_ready, rstd_at[ssq_keys[ssq_at[s] - 5]])
                    m = ssq_cols(s)
                    act.activation(XS[:, t, :], Xv[:, t, :], ACT.Square, accum_out=m[:, 0:1]).then_inc(ssq_ready, 1)
                elif k == "hT" and s[4] % 2:
                    _, _, w, st, kp = s
                    act.wait_ge(*full_of(s))
                    act.wait_ge(mod_ready, modfin_n[("modfin", l, w)])
                    for i in (0, 1):
                        kk = 2 * kp + i
                        ins = act.activation(HT[:, kk, st * L:(st + 1) * L], bank_of(s)[:, i * L:(i + 1) * L],
                                             ACT.Identity, scale=AMv[l][:, w - 1, kk, st:st + 1],
                                             bias=MODv[l][:, 24 * (w - 1) + kk, st:st + 1])
                    ins.then_inc(free_of(s)[0], 1)
                elif k == "pu" and s[2] % 2:
                    act.wait_ge(*full_of(s))
                    act.activation(UT[:, s[2], :], bank_of(s)[0:ML_D, :], ACT.Copy).then_inc(free_of(s)[0], 1)
                elif k == "pP" and s[3] % 2:
                    act.wait_ge(*full_of(s))
                    c, n = p_cols(s)
                    act.activation(PRv[:, s[3], c:c + n], bank_of(s)[:, 0:n], ACT.Copy).then_inc(free_of(s)[0], 1)
                elif k == "pz":
                    act.wait_ge(*full_of(s))
                    c0 = 0 if l < DEPTH - 1 else L
                    act.activation(ZS[:, s[2], c0:TOK], bank_of(s)[0:ML_D, c0:TOK], ACT.Tanh, scale=0.5).then_inc(
                        zs_tanh, 1)
                elif k == "rows":
                    act.wait_ge(lfa_ready, l + 1)
                    fa = GEM[:, 0:2, :]
                    link(act.activation(fa, fa, ACT.Exp, scale=-1.0))
                    act.activation(fa, fa, ACT.Ln, bias=1.0).then_inc(lf_ready, 1)
                    act.wait_ge(em_in, l + 1)
                    act.activation(GEM[:, 2:4, :], GEM[:, 2:4, :], ACT.Exp, scale=-1.0).then_inc(em_ready, 1)
                elif k == "mv" and s[2] % 2:
                    act.wait_ge(*full_of(s))
                    act.activation(MV[:, s[2], :, 0:ML_D],
                                   bank_of(s)[:, 0:ML_W].rearrange("p (h e) -> p h e", h=ML_H),
                                   ACT.Copy).then_inc(free_of(s)[0], 1)
                elif k == "conv":
                    act.wait_ge(conv_acc, conv_n[s])
                    act.activation(conv_tmp(s), UC[:, s[2], :], ACT.Tanh).then_inc(conv_tanh, 1)
                elif k == "mqk":
                    key = s + ("k",)
                    act.wait_ge(*full_of(key))
                    if s[2] == 0:
                        act.wait_ge(na_ready, T * (l + 1))
                    act.activation(MK[:, s[2], :], bank_of(key)[0:ML_D, :], ACT.Copy,
                                   scale=ML_D ** -0.5).then_inc(free_of(key)[0], 1)
                elif k == "mgrid":
                    _, _, h, d = s
                    g = GRIDB[grid_n[s] % 2]
                    mu = bank_of(s)
                    act.wait_ge(*full_of(s))
                    if grid_n[s] > 2:
                        act.wait_ge(pv_done, mpv_before(s))
                    act.wait_ge(diag_ready, grid_n[s])
                    act.wait_ge(gc_ready, l + 1)
                    for j in range(T):
                        for t0, t1 in runs(l, d, j, False):
                            act.activation(g[:, j, t0 * P:t1 * P], mu[:, t0 * P:t1 * P], ACT.Exp,
                                           bias=GC[:, d, j, h:h + 1])
                    act.activation(diagonal(s), diagonal(s), ACT.Exp).then_inc(grid_exp, 1)
                elif k == "cnorm":
                    t = s[2]
                    m = ssq_cols(s)
                    act.wait_ge(*free_of(("pP", l, "A", t)))
                    if s[2] == 0 and l:
                        act.wait_ge(resid_ready, resid_at[("moe_out", l - 1, T - 1)])
                    act.wait_ge(mean_ready, rstd_at[ssq_keys[ssq_at[s] - 5]])
                    act.wait_ge(ssq_ready, ssq_at[s] - 1)
                    if t in tiles_q(l):
                        link(act.activation(SQC[:, 0:Q_RANK], PRv[:, t, 0:Q_RANK], ACT.Square,
                                            accum_out=m[:, 0:1]))
                    act.activation(SQC[:, Q_RANK:384], PRv[:, t, Q_RANK:384], ACT.Square,
                                   accum_out=m[:, 1:2]).then_inc(ssq_ready, 1)
                elif k == "uqk":
                    t = s[2]
                    isq = t in tiles_q(l)
                    if t >= 2:
                        for key in qkT_jobs(("qkT", l, t - 2)):
                            act.wait_ge(*full_of(key))
                    if isq:
                        for i in (0, 1):
                            key = s + ("q", i)
                            act.wait_ge(*full_of(key))
                            act.activation(QTM[t % 2][:, 3 * i:3 * i + 3, :],
                                           bank_of(key)[:, 0:288].rearrange("p (h e) -> p h e", h=3),
                                           ACT.Copy).then_inc(free_of(key)[0], 1)
                    kt = KTM[t % 2]
                    link(act.activation(kt[:, :, NOPE_D:], PRv[:, t, 384:416].unsqueeze(1).broadcast_to(
                        [P, MLA_H, ROPE_D]), ACT.Copy))
                    key = s + ("k", 1)
                    act.wait_ge(*full_of(key))
                    kvv = bank_of(key)[:, 0:384].rearrange("p (h e) -> p h e", h=3)
                    act.activation(kt[:, 3:6, 0:NOPE_D], kvv[:, :, 0:NOPE_D], ACT.Copy)
                    act.activation(VV[:, t, 3:6, :], kvv[:, :, NOPE_D:], ACT.Copy).then_inc(free_of(key)[0], 1)
                    act.wait_ge(mean_ready, rstd_at[s] - 1)
                    if isq:
                        for i in (0, 1):
                            act.wait_ge(*free_of(s + ("q", i)))
                        act.activation(SQU[0], QTM[t % 2], ACT.Square)
                    for i in (0, 1):
                        act.wait_ge(*free_of(s + ("k", i)))
                    act.activation(SQU[1], kt, ACT.Square).then_inc(usq_ready, 1)
                elif k == "nT":
                    t = s[2]
                    act.wait_ge(*full_of(s))
                    bk = bank_of(s)[:, :].rearrange("p (a t) -> p a t", a=4)
                    if t in tiles_q(l):
                        act.activation(NQT[:, :, t * P:(t + 1) * P], bk[:, 0:2, :], ACT.Copy)
                    act.activation(NKT[:, :, t * P:(t + 1) * P], bk[:, 2:4, :], ACT.Copy).then_inc(free_of(s)[0], 1)
                elif k == "qkT":
                    for key in qkT_jobs(s):
                        if key[3] == "k":
                            act.wait_ge(*full_of(key))
                            hh = 3 * key[4]
                            act.activation(KT[:, hh:hh + 3, s[2] * P:(s[2] + 1) * P],
                                           bank_of(key)[0:QK_D, 0:384].rearrange("p (h t) -> p h t", h=3),
                                           ACT.Copy).then_inc(free_of(key)[0], 1)
                elif k == "S":
                    u = UNIT_AT[s[1:]]
                    b = s[1]
                    nk = keys_of(s)
                    act.wait_ge(nmax_ready, u + 1)
                    if b == 1:
                        act.wait_ge(pv_done, pv_at[("mpv", l, ML_H - 1, 1)])
                    if u >= 3:
                        act.wait_ge(*full_of(("ET",) + UNITS[u - 3]))
                    if b == 1:
                        act.wait_ge(*full_of(("mlT", l, ML_H - 1)))
                    act.activation(exps(u)[:, 0:nk], bank_of(s)[:, 0:nk], ACT.Exp, bias=neg_max(u),
                                   accum_out=exp_sums(u, 1)).then_inc(free_of(s)[0], 1)
                elif k == "ET" and s[1] == 1:
                    u = UNIT_AT[s[1:]]
                    nkt = keys_of(s) // P
                    act.wait_ge(*full_of(s))
                    act.wait_ge(pv_done, pv_at[("mpv", l, ML_H - 1, 1)])
                    if u >= 2:
                        act.wait_ge(pv_done, pv_at[("PV",) + UNITS[u - 2]])
                    act.activation(PT[u % 2][:, 0:nkt, :].rearrange("p a b -> p (a b)"),
                                   bank_of(s)[:, 0:nkt * P], ACT.Copy).then_inc(free_of(s)[0], 1)
                elif k == "router":
                    act.wait_ge(*full_of(s))
                    act.activation(RROW[:, 0:L], bank_of(s)[0:N_E, 0:L], ACT.Tanh, scale=0.5).then_inc(
                        free_of(s)[0], 1)
                elif k == "gbc":
                    for i in (0, 1):
                        act.wait_ge(*full_of(s + (i,)))
                        act.activation(GB[:, s[3], 512 * i:512 * i + 512], bank_of(s + (i,))[:, :],
                                       ACT.Copy).then_inc(free_of(s + (i,))[0], 1)
                elif k == "gbc2":
                    act.wait_ge(resid_ready, resid_at[("wo", l, tiles_q(l)[-1])])
                    for st in sorted({t // 2 for t in tiles_q(l)}):
                        for i in (0, 1):
                            key = s + (st, i)
                            act.wait_ge(*full_of(key))
                            act.activation(GB[:, st, 512 * i:512 * i + 512], bank_of(key)[:, :],
                                           ACT.Copy).then_inc(free_of(key)[0], 1)
                elif k == "h2T":
                    _, _, t, n = s
                    act.wait_ge(*full_of(s))
                    act.activation(XS[:, t, 512 * n:512 * n + 512], bank_of(s)[:, :], ACT.Copy).then_inc(
                        free_of(s)[0], 1)
                    if n:
                        for i in (0, 1):
                            act.wait_ge(*free_of(("h2T", l, t, i)))
                        act.dma_start(h2_rows[t * P:(t + 1) * P, :], XS[:, t, :]).then_inc(h2_stored, 16)
                elif k == "xT":
                    n = expert_n(l, s[2])
                    act.wait_ge(*full_of(s + (1,)))
                    if n >= 2:
                        act.wait_ge(*full_of(("ab",) + expert_key(n - 2)))
                    act.activation(XGT[n % 2][:, 4:8, :].rearrange("p k t -> p (k t)"), bank_of(s + (1,))[:, :],
                                   ACT.Copy).then_inc(free_of(s + (1,))[0], 1)
                elif k == "ab":
                    act.wait_ge(*full_of(s))
                    n = ab_n[s]
                    if n > 2:
                        act.wait_ge(hid_ready, n - 2)
                    act.activation(TH[n % 2], bank_of(s)[:, 0:FF], ACT.Tanh, scale=0.5).then_inc(moe_tanh, 1)
                elif k == "yT":
                    key = ("y",) + s[1:] + ("T",)
                    n = expert_n(l, s[2]) + 1
                    act.wait_ge(*full_of(key))
                    if n > 2:
                        act.wait_ge(*full_of(("y",) + expert_key(n - 3) + (1,)))
                    act.activation(HIDT[n % 2].rearrange("p k t -> p (k t)"), bank_of(key)[:, 0:FF],
                                   ACT.Copy).then_inc(free_of(key)[0], 1)
                elif k == "y":
                    key = s + (1,)
                    n = expert_n(l, s[2])
                    act.wait_ge(*full_of(key))
                    if n >= 2:
                        act.wait_ge(ys_stored[n % 2], 16 * (n // 2))
                    act.activation(YO[n % 2][:, 512:1024], bank_of(key)[:, :], ACT.Copy).then_inc(
                        free_of(key)[0], 1)
                elif k == "comb":
                    tq = tiles_q(l)
                    if s[2] == tq[0]:
                        n = expert_n(l, N_E)
                        act.wait_ge(ys_stored[0], 16 * ((n + 1) // 2))
                        act.wait_ge(ys_stored[1], 16 * (n // 2))
                        for t in tq:
                            act.dma_start(ACC[:, t, :], pairs[t * P:(t + 1) * P, :]).then_inc(pair_loaded[t], 16)
                            act.dma_start(XS[:, t, :], pairs[TOK + t * P:TOK + (t + 1) * P, :]).then_inc(
                                pair_loaded[t], 16)
                elif k == "dense":
                    nt = len(tiles_q(l))
                    over = act.value_load(OVER[0:1, :])
                    with act.If(over > 0):
                        with act.Fori(0, N_E) as e:
                            for i in range(nt):
                                act.wait_ge(dn[l]["ab"], e * nt + (i + 1))
                                act.activation(TH[0], bank[0][:, 0:FF], ACT.Tanh, scale=0.5).then_inc(
                                    dn[l]["tanh"], 1)
                        act.wait_ge(dn[l]["stored"], 32 * nt)

        @block.tensor
        def _(pe):
            def open_bank(key):
                n = job_at[key]
                if n >= RING:
                    pe.wait_ge(free[n % RING], n // RING)

            def flip(out, in_):
                k = in_.shape[0]
                return pe.transpose(out, in_, IDENT[0:k, 0:k])

            def open_acc(key):
                n = acc_at[key]
                if n >= 2:
                    pe.wait_ge(acc_free, n - 1)
                return bank[6 + n % 2]

            pe.wait_ge(const_ready, 1)
            pe.wait_ge(cond_loaded, 32)
            flip(bank[7][:, 0:16], CIN[0:16, :]).then_inc(cond_full, 1)
            pe.wait_ge(csilu_ready, 2)
            for s in schedule:
                k, l = s[0], layer_of(s)
                tq = tiles_q(l)
                c0 = 0 if l < DEPTH - 1 else L
                if k == "mod":
                    open_bank(s)
                    pe.wait_ge(*loaded(s))
                    w = slot(s).rearrange("p (k n) -> p k n", k=KD)
                    for kk in range(KD):
                        ins = pe.matmul(bank_of(s)[0:2, :], CSv[:, kk, :], w[:, kk, :], start=kk == 0,
                                        stop=kk == KD - 1)
                    ins.then_inc(full_of(s)[0], 1)
                    if s == ("mod", 0, 0):
                        pe.wait_ge(pack_loaded, 16 * PACK_DMAS)
                        for i in range(3):
                            ins = flip(bank[6][:, i * P:(i + 1) * P], PACK[:, i * P:(i + 1) * P])
                        ins.then_inc(cols_full, 1)
                elif k == "modT":
                    key = ("mod",) + s[1:]
                    open_bank(s)
                    pe.wait_ge(*free_of(key))
                    for c in range(4):
                        ins = flip(bank_of(s)[:, 2 * c:2 * c + 2], MROW[mod_n[key] % 2][:, c * P:(c + 1) * P])
                    ins.then_inc(full_of(s)[0], 1)
                elif k == "hT":
                    _, _, w, st, kp = s
                    open_bank(s)
                    pe.wait_ge(xs_ready, norm_n[("norm", l, w, 2 * st + 1)])
                    for i in (0, 1):
                        for tt in (0, 1):
                            kk = 2 * kp + i
                            ins = flip(bank_of(s)[:, i * L + tt * P:i * L + (tt + 1) * P],
                                       XS[:, 2 * st + tt, kk * P:(kk + 1) * P])
                    ins.then_inc(full_of(s)[0], 1)
                elif k in ("pu", "pz"):
                    open_bank(s)
                    piece = ("w_" + k[1], l)
                    pe.wait_ge(*loaded(piece))
                    if k == "pu" and s[2] == 0:
                        for st in (0, 1):
                            for kp in range(4):
                                pe.wait_ge(*free_of(("hT", l, 1, st, kp)))
                    w = slot(piece)[:, 0:KD * ML_W].rearrange("p (k n) -> p k n", k=KD)
                    b0 = 0 if k == "pu" else c0
                    for kk in range(KD):
                        ins = pe.matmul(bank_of(s)[0:ML_D, b0:TOK], w[:, kk, s[2] * ML_D:(s[2] + 1) * ML_D],
                                        HT[:, kk, b0:TOK], start=kk == 0, stop=kk == KD - 1)
                    ins.then_inc(full_of(s)[0], 1)
                elif k == "pP":
                    _, _, w, t = s
                    open_bank(s)
                    pe.wait_ge(*loaded(("w_" + w, l)))
                    n = CHUNK[w][1]
                    wv = slot(("w_" + w, l))[:, 0:KD * n].rearrange("p (k n) -> p k n", k=KD)
                    c, nn = p_cols(s)
                    off = c - CHUNK[w][2]
                    for kk in range(KD):
                        ins = pe.matmul(bank_of(s)[:, 0:nn], HT[:, kk, t * P:(t + 1) * P], wv[:, kk, off:off + nn],
                                        start=kk == 0, stop=kk == KD - 1)
                    ins.then_inc(full_of(s)[0], 1)
                elif k == "gT":
                    t = s[2]
                    open_bank(s)
                    pe.wait_ge(gates_ready, l + 1)
                    for q in range(4):
                        ins = flip(bank_of(s)[0:ML_H, q * P:(q + 1) * P], PRv[:, t, PG + 4 * q:PG + 4 * q + 4])
                    ins.then_inc(full_of(s)[0], 1)
                elif k == "cols":
                    open_bank(s)
                    pe.wait_ge(rows_ready, l + 1)
                    for q in range(4):
                        for t in range(T):
                            o = (q * T + t) * ML_H
                            ins = flip(bank_of(s)[:, o:o + ML_H], GEM[:, q, t * P:(t + 1) * P])
                    ins.then_inc(full_of(s)[0], 1)
                elif k == "mv":
                    t = s[2]
                    open_bank(s)
                    pe.wait_ge(small_loaded, 16 * SMALL_PARTS * (l + 1))
                    if t == 0:
                        for h in range(ML_H):
                            pe.wait_ge(*free_of(("pu", l, h)))
                    wv = small_views(l)[2]
                    for h in range(ML_H):
                        ins = pe.matmul(bank_of(s)[:, h * ML_D:(h + 1) * ML_D], UT[:, h, t * P:(t + 1) * P],
                                        wv[:, h, :], start=True, stop=True)
                    ins.then_inc(full_of(s)[0], 1)
                elif k == "mqk":
                    h = s[2]
                    wq, wk = small_views(l)[0:2]
                    pe.wait_ge(uc_ready, conv_n[("conv", l, h)])
                    open_bank(s + ("q",))
                    pe.matmul(bank_of(s + ("q",))[0:ML_D, c0:TOK], wq[:, h, :], UC[:, h, c0:TOK], start=True,
                              stop=True).then_inc(full_of(s + ("q",))[0], 1)
                    open_bank(s + ("k",))
                    pe.matmul(bank_of(s + ("k",))[0:ML_D, :], wk[:, h, :], UC[:, h, :], start=True,
                              stop=True).then_inc(full_of(s + ("k",))[0], 1)
                elif k == "mst":
                    h = s[2]
                    pe.wait_ge(*free_of(("mqk", l, h, "q")))
                    pe.wait_ge(*free_of(("mqk", l, h, "k")))
                    for j in range(T):
                        q0 = c0 if j < 2 else L
                        i, o = raw_bank(l, j)
                        key = s + (i,)
                        if j == 0 or raw_bank(l, j - 1)[0] != i:
                            open_bank(key)
                        ins = pe.matmul(bank_of(key)[:, q0 + o:TOK + o], MK[:, h, j * P:(j + 1) * P],
                                        MQ[:, h, q0:TOK], start=True, stop=True)
                        if j == T - 1 or raw_bank(l, j + 1)[0] != i:
                            ins.then_inc(full_of(key)[0], 1)
                elif k == "mgrid":
                    open_bank(s)
                    pe.wait_ge(rows_ready, l + 1)
                    pe.matmul(bank_of(s)[:, c0:TOK], IDENT[0:ML_H, s[2]:s[2] + 1].broadcast_to([ML_H, P]),
                              NEGMUv[:, s[3], c0:TOK], start=True,
                              stop=True).then_inc(full_of(s)[0], 1)
                elif k == "mpv":
                    _, _, h, d = s
                    acc = open_acc(s)
                    pe.wait_ge(grid_ready, grid_n[("mgrid", l, h, d)])
                    if h == 0 and d == 0:
                        for t in range(T):
                            pe.wait_ge(*free_of(("mv", l, t)))
                        pe.wait_ge(mv_ready, l + 1)
                    g = GRIDB[grid_n[("mgrid", l, h, d)] % 2]
                    for t in tq:
                        js = [j for j in range(T) if allowed(d, t, j)]
                        for j in js:
                            ins = pe.matmul(acc[:, t * 97:t * 97 + 97], g[:, j, t * P:(t + 1) * P],
                                            MV[:, j, h, :], start=j == js[0], stop=j == js[-1])
                    ins.then_inc(pv_done, 1)
                elif k == "mlT":
                    h = s[2]
                    open_bank(s)
                    pe.wait_ge(hn_ready, l + 1)
                    for t in tq:
                        ins = flip(bank_of(s)[0:ML_D, t * P:(t + 1) * P], HS[:, t, h * ML_D:(h + 1) * ML_D])
                    ins.then_inc(full_of(s)[0], 1)
                elif k == "cT":
                    t = s[2]
                    open_bank(s)
                    pe.wait_ge(cn_ready, cn_n[("cnorm", l, t)])
                    for c in range(0 if t in tq else 2, 3):
                        ins = flip(bank_of(s)[:, c * P:(c + 1) * P], PRv[:, t, c * P:(c + 1) * P])
                    ins.then_inc(full_of(s)[0], 1)
                elif k == "uqk":
                    t = s[2]
                    uq, ukv = small_views(l)[3:5]
                    pe.wait_ge(*free_of(("cT", l, t)))
                    if t in tq:
                        for i in (0, 1):
                            key = s + ("q", i)
                            open_bank(key)
                            for kk in (0, 1):
                                ins = pe.matmul(bank_of(key)[:, 0:288], CT[:, kk, t * P:(t + 1) * P],
                                                uq[:, kk, 288 * i:288 * i + 288], start=kk == 0, stop=kk == 1)
                            ins.then_inc(full_of(key)[0], 1)
                    for i in (0, 1):
                        key = s + ("k", i)
                        open_bank(key)
                        pe.matmul(bank_of(key)[:, 0:384], CT[:, 2, t * P:(t + 1) * P],
                                  ukv[:, 384 * i:384 * i + 384], start=True, stop=True).then_inc(full_of(key)[0], 1)
                elif k == "qkT":
                    t = s[2]
                    pe.wait_ge(qk_ready, uqk_n[("uqk", l, t)])
                    for key in qkT_jobs(s):
                        src = (QTM if key[3] == "q" else KTM)[t % 2]
                        open_bank(key)
                        for i in range(3):
                            ins = flip(bank_of(key)[0:QK_D, i * P:(i + 1) * P], src[:, 3 * key[4] + i, :])
                        ins.then_inc(full_of(key)[0], 1)
                elif k == "nT":
                    t = s[2]
                    open_bank(s)
                    pe.wait_ge(na_ready, nan_n[("nan", l, t)])
                    for i in range(0 if t in tq else 2, 4):
                        ins = flip(bank_of(s)[:, i * P:(i + 1) * P], PRv[:, t, PNQ + i * P:PNQ + (i + 1) * P])
                    ins.then_inc(full_of(s)[0], 1)
                elif k == "S":
                    _, b, _, t, h, _ = s
                    open_bank(s)
                    nk = keys_of(s)
                    if h == 0 and t == tq[0]:
                        for tt in range(T):
                            if b == 0:
                                for key in qkT_jobs(("qkT", l, tt)):
                                    pe.wait_ge(*free_of(key))
                            else:
                                pe.wait_ge(*free_of(("nT", l, tt)))
                    if b == 0:
                        q, kk = QT[:, h, t * P:(t + 1) * P], KT[:, h, 0:nk]
                    else:
                        r = (h % 2) * NA_D
                        q = NQT[r:r + NA_D, h // 2, t * P:(t + 1) * P]
                        kk = NKT[r:r + NA_D, h // 2, 0:nk]
                    pe.matmul(bank_of(s)[:, 0:nk], q, kk, start=True, stop=True).then_inc(full_of(s)[0], 1)
                elif k == "ET":
                    u = UNIT_AT[s[1:]]
                    nkt = keys_of(s) // P
                    key = s
                    open_bank(key)
                    pe.wait_ge(*free_of(("S",) + s[1:]))
                    for i in range(nkt):
                        ins = flip(bank_of(key)[:, i * P:(i + 1) * P], exps(u)[:, i * P:(i + 1) * P])
                    ins.then_inc(full_of(key)[0], 1)
                elif k == "PV":
                    u = UNIT_AT[s[1:]]
                    _, b, _, t, h, lasth = s
                    nkt = keys_of(s) // P
                    key = ("ET",) + s[1:]
                    akey = ("OT", b, l, t, (MLA_H, NA_H)[b] - 1, True)
                    acc = bank[6 + acc_at[akey] % 2]
                    if h == 0:
                        open_acc(akey)
                    pe.wait_ge(*free_of(key))
                    for i in range(nkt):
                        v = VV[:, i, h, :] if b == 0 else PRv[:, i, PNV + h * NA_D:PNV + (h + 1) * NA_D]
                        ins = pe.matmul(acc[:, h * 64:h * 64 + 64], PT[u % 2][:, i, :], v, start=i == 0,
                                        stop=i == nkt - 1)
                    ins.then_inc(pv_done, 1)
                elif k == "OT":
                    _, b, _, t, h, _ = s
                    open_bank(s)
                    pe.wait_ge(om_ready, OT_n[s])
                    for i in range((3, 2)[b]):
                        ins = flip(bank_of(s)[:, i * P:(i + 1) * P], OM[:, i * P:(i + 1) * P])
                    ins.then_inc(full_of(s)[0], 1)
                elif k == "gbc" or k == "gbc2":
                    keys = [s + (i,) for i in (0, 1)] if k == "gbc" else [
                        s + (st, i) for st in sorted({t // 2 for t in tq}) for i in (0, 1)]
                    v = 16 if k == "gbc" else 40
                    for i in (v // 4, v // 4 + 1):
                        pe.wait_ge(*free_of(("modT", l, i)))
                    for key in keys:
                        st = key[3] if k == "gbc" else key[2]
                        i = key[-1]
                        open_bank(key)
                        for c in range(4):
                            col = MODv[l][:, v + 4 * i + c, st:st + 1].broadcast_to([P, P])
                            ins = pe.matmul(bank_of(key)[:, c * P:(c + 1) * P], col, IDENT[:, :], start=True,
                                            stop=True, is_transpose=True)
                        ins.then_inc(full_of(key)[0], 1)
                elif k == "wo":
                    t, n = s[2:]
                    if (t, n) == (tq[0], 0):
                        for p in ("wo_mla", "wo_ml", "wo_na"):
                            pe.wait_ge(*loaded((p, l)))
                        pe.wait_ge(mlt_ready, ML_H * (l + 1))
                        for u in schedule:
                            if u[0] == "OT" and u[2] == l:
                                pe.wait_ge(*free_of(u))
                    wm = slot(("wo_mla", l))[:, 0:3 * D].rearrange("p (k n) -> p k n", k=3)
                    wl = slot(("wo_ml", l))[0:ML_D, :].rearrange("p (k n) -> p k n", k=ML_H)
                    wn = slot(("wo_na", l))[:, 0:2 * D].rearrange("p (k n) -> p k n", k=2)
                    terms = [(MLAT, wm, i) for i in range(3)] + [(MLT, wl, i) for i in range(4)] + [
                        (NAT, wn, i) for i in range(2)]
                    open_bank(s)
                    for i, (m, w, c) in enumerate(terms):
                        ins = pe.matmul(bank_of(s)[:, :], m[:, c, t * P:(t + 1) * P],
                                        w[:, c, 512 * n:512 * n + 512], start=i == 0, stop=i == len(terms) - 1)
                    ins.then_inc(full_of(s)[0], 1)
                elif k == "router":
                    st = s[2]
                    open_bank(s)
                    for kp in range(4):
                        pe.wait_ge(*free_of(("hT", l, 2, st, kp)))
                    for kk in range(KD):
                        ins = pe.matmul(bank_of(s)[0:N_E, 0:L], RW[:, kk, :], HT[:, kk, st * L:(st + 1) * L],
                                        start=kk == 0, stop=kk == KD - 1)
                    ins.then_inc(full_of(s)[0], 1)
                elif k == "rT":
                    open_bank(s)
                    pe.wait_ge(*free_of(("router",) + s[1:]))
                    for i in (0, 1):
                        ins = flip(bank_of(s)[:, 16 * i:16 * i + 16], RROW[:, i * P:(i + 1) * P])
                    ins.then_inc(full_of(s)[0], 1)
                elif k == "h2T":
                    _, _, t, n = s
                    open_bank(s)
                    for c in range(4):
                        ins = flip(bank_of(s)[:, c * P:(c + 1) * P], HT[:, 4 * n + c, t * P:(t + 1) * P])
                    ins.then_inc(full_of(s)[0], 1)
                elif k == "pfx":
                    open_bank(s)
                    pe.wait_ge(assign_ready, pfx_n[s])
                    ones = RANK[:, 15:16].broadcast_to([P, P])
                    tiles = [t for t in tq if t < 2 * s[2] + 2]
                    for i in (0, 1):
                        out = bank_of(s)[:, 16 * i:16 * i + 16]
                        before = [t for t in tiles if t < 2 * s[2] + i]
                        for t in before:
                            pe.matmul(out, ones, ASSIGN[:, 16 * t:16 * t + 16], start=t == before[0], stop=False)
                        t = 2 * s[2] + i
                        pe.matmul(out, INCL, ASSIGN[:, 16 * t:16 * t + 16], start=not before, stop=True)
                    for t in tiles:
                        ins = pe.matmul(bank_of(s)[:, 64:80], ones, ASSIGN[:, 16 * t:16 * t + 16],
                                        start=t == tiles[0], stop=t == tiles[-1])
                    ins.then_inc(full_of(s)[0], 1)
                elif k == "xT":
                    n = expert_n(l, s[2])
                    pe.wait_ge(xg_loaded[n % 3], 16 * (n // 3 + 1))
                    for i in (0, 1):
                        open_bank(s + (i,))
                        for c in range(4):
                            o = (4 * i + c) * P
                            ins = flip(bank_of(s + (i,))[:, c * P:(c + 1) * P], XG[n % 3][:, o:o + P])
                        ins.then_inc(full_of(s + (i,))[0], 1)
                elif k == "ab":
                    e = s[2]
                    n = expert_n(l, e)
                    open_bank(s)
                    pe.wait_ge(*loaded(("w13", l, e)))
                    pe.wait_ge(*free_of(("xT", l, e, 0)))
                    pe.wait_ge(*free_of(("xT", l, e, 1)))
                    w = slot(("w13", l, e)).rearrange("p (k n) -> p k n", k=KD)
                    for kk in range(KD):
                        ins = pe.matmul(bank_of(s)[:, :], XGT[n % 2][:, kk, :], w[:, kk, :], start=kk == 0,
                                        stop=kk == KD - 1)
                    ins.then_inc(full_of(s)[0], 1)
                elif k == "yT":
                    n = expert_n(l, s[2]) + 1
                    key = ("y",) + s[1:] + ("T",)
                    open_bank(key)
                    pe.wait_ge(hid_ready, n)
                    for i in (0, 1):
                        ins = flip(bank_of(key)[:, i * P:(i + 1) * P], HID[n % 2][:, i * P:(i + 1) * P])
                    ins.then_inc(full_of(key)[0], 1)
                elif k == "y":
                    e = s[2]
                    n = expert_n(l, e) + 1
                    key = s + ("T",)
                    w2, sm, v = w2_of(l, e)
                    pe.wait_ge(sm, v)
                    pe.wait_ge(*free_of(key))
                    for nn in (0, 1):
                        open_bank(s + (nn,))
                        for i in (0, 1):
                            ins = pe.matmul(bank_of(s + (nn,))[:, :], HIDT[n % 2][:, i, :],
                                            w2[:, i, 512 * nn:512 * nn + 512], start=i == 0, stop=i == 1)
                        ins.then_inc(full_of(s + (nn,))[0], 1)
                elif k == "dense":
                    nt = len(tq)
                    d = dn[l]
                    over = pe.value_load(OVER[0:1, :])
                    with pe.If(over > 0):
                        last = job_at[("y", l, N_E - 1, 1)]
                        for j in range(RING):
                            pe.wait_ge(*free_of(jobs[last - j]))
                        w13 = RINGW[:, 0:4096].rearrange("p (k n) -> p k n", k=KD)
                        w2 = RINGW[:, 4096:6144].rearrange("p (k n) -> p k n", k=2)
                        with pe.Fori(0, N_E) as e:
                            pe.wait_ge(d["loaded"], e * 48 + 48)
                            for i, t in enumerate(tq):
                                pe.wait_ge(d["hid"], e * nt + (i + 1))
                                for kk in range(KD):
                                    ins = pe.matmul(bank[0][:, :], HT[:, kk, t * P:(t + 1) * P], w13[:, kk, :],
                                                    start=kk == 0, stop=kk == KD - 1)
                                ins.then_inc(d["ab"], 1)
                                pe.wait_ge(d["hid"], e * nt + (i + 2))
                                for c in (0, 1):
                                    ins = flip(bank[1][:, c * P:(c + 1) * P], HID[0][:, c * P:(c + 1) * P])
                                ins.then_inc(d["T"], 1)
                                pe.wait_ge(d["ht"], e * nt + (i + 1))
                                pe.wait_ge(d["acc"], e * nt + (i + 1))
                                for nn in (0, 1):
                                    for c in (0, 1):
                                        ins = pe.matmul(bank[2 + nn][:, :], HIDT[0][:, c, :],
                                                        w2[:, c, 512 * nn:512 * nn + 512], start=c == 0, stop=c == 1)
                                ins.then_inc(d["y"], 1)
                        pe.wait_ge(d["acc"], N_E * nt + 1)
                        if tail_mods(l):
                            pe.wait_ge(d["reloaded"], 16 * TAIL_MODS)

        @block.vector
        def _(dve):
            step = [0]

            def link(ins):
                step[0] += 1
                ins.then_inc(dve_step, 1)
                dve.wait_ge(dve_step, step[0])

            dve.memset(PACK[:, :], 0.0).then_inc(pack_zero, 1)
            dve.wait_ge(csilu_ready, 1)
            link(dve.scalar_tensor_tensor(CS[:, :], RT[:, 128:144], 1.0, bank[7][:, 0:16], ALU.add, ALU.mult))
            dve.tensor_scalar(CS[:, :], CS[:, :], 0.5, None, ALU.mult).then_inc(csilu_ready, 1)
            dve.wait_ge(cols_full, 1)
            dve.tensor_copy(COLS[:, :], bank[6][:, 0:3 * P]).then_inc(cols_ready, 1)
            dve.wait_ge(cols_ready, 1)
            for l in range(DEPTH):
                q = 2 * P + 24 * l
                link(dve.tensor_scalar(COLS[0:ML_D, q + 8:q + 24], COLS[0:ML_D, q + 8:q + 24], 0.5, None, ALU.mult))

            def rstd(s, n):
                w = rstd_width(s)
                m, r = stat(rstd_at[s])
                return m[:, 0:w], r[:, 0:w]

            def of_tiles(ap, t):
                return ap[:, 16 * t:16 * t + 32].rearrange("p (t e) -> p t e", e=16)

            def bcast(ap, n):
                return ap.unsqueeze(2).broadcast_to([ap.shape[0], ap.shape[1], n])

            for s in schedule:
                k, l = s[0], layer_of(s)
                tq = tiles_q(l)
                c0 = 0 if l < DEPTH - 1 else L
                if k == "modT":
                    i = s[2]
                    dve.wait_ge(*full_of(s))
                    link_to = dve.tensor_tensor(MODv[l][:, 4 * i:4 * i + 4, :],
                                                bank_of(s)[:, 0:8].rearrange("p (c j) -> p c j", j=2),
                                                bcast(COLS[:, 64 * l + 4 * i:64 * l + 4 * i + 4], 2), ALU.add)
                    link_to.then_inc(free_of(s)[0], 1)
                elif k == "modfin":
                    w = s[2] - 1
                    for i in range(6 * w, 6 * w + 4):
                        dve.wait_ge(*free_of(("modT", l, i)))
                    link(dve.scalar_tensor_tensor(AMv[l][:, w, :, 0], MODv[l][:, 24 * w + 8:24 * w + 16, 0], 1.0,
                                                  COLS[:, 64 * l + 48 + 8 * w:64 * l + 56 + 8 * w], ALU.add,
                                                  ALU.mult))
                    dve.scalar_tensor_tensor(AMv[l][:, w, :, 1], MODv[l][:, 24 * w + 8:24 * w + 16, 1], 1.0,
                                             COLS[:, 64 * l + 48 + 8 * w:64 * l + 56 + 8 * w], ALU.add,
                                             ALU.mult).then_inc(mod_ready, 1)
                elif k == "norm":
                    t, w = s[3], s[2]
                    dve.wait_ge(ssq_ready, ssq_at[s])
                    m = ssq_cols(s)
                    mm, rr = rstd(s, D)
                    dve.tensor_scalar(mm, m[:, 0:1], 1.0 / D, EPS, ALU.mult, ALU.add).then_inc(mean_ready, 1)
                    dve.wait_ge(rstd_ready, rstd_at[s])
                    dve.tensor_scalar(XS[:, t, :], Xv[:, t, :], rr, None, ALU.mult).then_inc(xs_ready, 1)
                elif k == "hT" and s[4] % 2 == 0:
                    _, _, w, st, kp = s
                    dve.wait_ge(*full_of(s))
                    dve.wait_ge(mod_ready, modfin_n[("modfin", l, w)])
                    for i in (0, 1):
                        kk = 2 * kp + i
                        ins = dve.tensor_scalar(HT[:, kk, st * L:(st + 1) * L], bank_of(s)[:, i * L:(i + 1) * L],
                                                AMv[l][:, w - 1, kk, st:st + 1], MODv[l][:, 24 * (w - 1) + kk, st:st + 1],
                                                ALU.mult, ALU.add)
                    ins.then_inc(free_of(s)[0], 1)
                elif k == "pu" and s[2] % 2 == 0:
                    dve.wait_ge(*full_of(s))
                    dve.tensor_copy(UT[:, s[2], :], bank_of(s)[0:ML_D, :]).then_inc(free_of(s)[0], 1)
                elif k == "pP" and s[3] % 2 == 0:
                    dve.wait_ge(*full_of(s))
                    c, n = p_cols(s)
                    dve.tensor_copy(PRv[:, s[3], c:c + n], bank_of(s)[:, 0:n]).then_inc(free_of(s)[0], 1)
                elif k == "pz":
                    dve.wait_ge(zs_tanh, pz_n[s])
                    dve.scalar_tensor_tensor(ZS[:, s[2], c0:TOK], ZS[:, s[2], c0:TOK], 1.0,
                                             bank_of(s)[0:ML_D, c0:TOK], ALU.add, ALU.mult).then_inc(
                        free_of(s)[0], 1)
                elif k == "gates":
                    if l == 0:
                        dve.wait_ge(params_loaded, 16 * PARAM_DMAS)
                        for m in range(DEPTH):
                            link(dve.tensor_scalar(bc_qg(m), bc_qg(m), QK_D ** -0.5, None, ALU.mult))
                            link(dve.tensor_scalar(bc_nq(m), bc_nq(m), NA_D ** -0.5, None, ALU.mult))
                    for t in range(T):
                        dve.wait_ge(*free_of(("pP", l, "B", t)))
                    g = PRv[:, :, PG:PG + 16]
                    dve.tensor_tensor(g, g, bc_gb(l).unsqueeze(1).broadcast_to([P, T, 16]), ALU.add).then_inc(
                        gates_ready, 1)
                elif k == "gT":
                    t = s[2]
                    dve.wait_ge(*full_of(s))
                    bk = bank_of(s)[0:ML_H, :].rearrange("p (q t) -> p q t", q=4)
                    r0 = (t // 2) * L + (1 - t % 2) * P
                    dve.tensor_copy(ROW[:, 0:2, t * P:(t + 1) * P], bk[:, 0:2, :])
                    dve.tensor_copy(ROW[:, 2:4, r0:r0 + P], bk[:, 2:4, ::-1]).then_inc(free_of(s)[0], 1)
                elif k == "rows":
                    for t in range(T):
                        dve.wait_ge(*free_of(("gT", l, t)))
                    f = ROW[:, 1::2, :]
                    dve.scalar_tensor_tensor(GEM[:, 0:2, :], f, -1.0, f, ALU.mult, ALU.max).then_inc(lfa_ready, 1)
                    link(dve.memset(GEM[:, 2:3, :], 1.0))
                    dve.wait_ge(lf_ready, l + 1)
                    link(dve.scalar_tensor_tensor(f, f, 0.0, GEM[:, 0:2, :], ALU.min, ALU.subtract))
                    for d in (0, 1):
                        link(dve.tensor_tensor_scan(GEM[:, d, :], GEM[:, 2, :], ROW[:, 2 * d + 1, :], 0.0, ALU.mult,
                                                    ALU.add))
                    for d in (0, 1):
                        link(dve.tensor_tensor(ROW[:, 2 * d, :], ROW[:, 2 * d, :], GEM[:, d, :], ALU.subtract))
                        link(dve.tensor_tensor_scan(ROW[:, 2 * d + 1, :], ROW[:, 2 * d, :], ROW[:, 2 * d, :], 0.0,
                                                    ALU.max, ALU.max))
                    def nat(ap, d):
                        return ap if d == 0 else ap.rearrange("p (s t) -> p s t", s=2)[:, :, ::-1]

                    def plain(ap, d):
                        return ap if d == 0 else ap.rearrange("p (s t) -> p s t", s=2)
                    for d in (0, 1):
                        link(dve.tensor_tensor(plain(GEM[:, 2 + d, :], d), nat(GEM[:, d, :], d),
                                               nat(ROW[:, 2 * d + 1, :], d), ALU.add))
                    for d in (0, 1):
                        link(dve.tensor_copy(plain(GEM[:, d, :], d), nat(ROW[:, 2 * d, :], d)))
                        ins = dve.tensor_scalar(plain(NEGMUv[:, d, :], d), nat(ROW[:, 2 * d + 1, :], d), -1.0, None,
                                                ALU.mult)
                        if d == 0:
                            link(ins)
                    ins.then_inc(em_in, 1)
                    dve.wait_ge(em_ready, l + 1)
                    dve.wait_ge(em_in, l + 1)
                    dve.memset(MV[:, :, :, 96:97].rearrange("p t h o -> p (t h) o"), 1.0).then_inc(mv_ready, 1)
                    dve.wait_ge(mv_ready, l + 1)
                    tick(dve, rows_ready)
                elif k == "cols":
                    dve.wait_ge(*full_of(s))
                    dve.tensor_copy(GEMC[:, :], bank_of(s)[:, 0:64]).then_inc(gc_ready, 1)
                    dve.wait_ge(gc_ready, l + 1)
                    tick(dve, free_of(s)[0])
                elif k == "mv" and s[2] % 2 == 0:
                    dve.wait_ge(*full_of(s))
                    dve.tensor_copy(MV[:, s[2], :, 0:ML_D],
                                    bank_of(s)[:, 0:ML_W].rearrange("p (h e) -> p h e", h=ML_H)).then_inc(
                        free_of(s)[0], 1)
                elif k == "conv":
                    h = s[2]
                    dve.wait_ge(*free_of(("pu", l, h)))
                    q = 24 * l
                    b, w0, w1, w2 = (c96(q + 8 + h), c96(q + 12 + h), c96(q + 16 + h), c96(q + 20 + h))
                    u2 = UT[:, h, :].rearrange("p (s t) -> p s t", s=2)
                    o2 = UC[:, h, :].rearrange("p (s t) -> p s t", s=2)
                    link(dve.tensor_scalar(UC[:, h, :], UT[:, h, :], w1, b, ALU.mult, ALU.add))
                    link(dve.scalar_tensor_tensor(o2[:, :, 1:L], u2[:, :, 0:L - 1], w0, o2[:, :, 1:L], ALU.mult,
                                                  ALU.add))
                    dve.scalar_tensor_tensor(o2[:, :, 0:L - 1], u2[:, :, 1:L], w2, o2[:, :, 0:L - 1], ALU.mult,
                                             ALU.add).then_inc(conv_acc, 1)
                    dve.wait_ge(conv_tanh, conv_n[s])
                    dve.wait_ge(conv_acc, conv_n[s])
                    dve.scalar_tensor_tensor(UC[:, h, :], conv_tmp(s), 1.0, UC[:, h, :], ALU.add,
                                             ALU.mult).then_inc(uc_ready, 1)
                elif k == "mqk":
                    h = s[2]
                    key = s + ("q",)
                    dve.wait_ge(*full_of(key))
                    dve.tensor_copy(MQ[:, h, c0:TOK], bank_of(key)[0:ML_D, c0:TOK]).then_inc(free_of(key)[0], 1)
                    dve.wait_ge(*full_of(s + ("k",)))
                    link(dve.tensor_scalar(UC[:, h, :], UC[:, h, :], c96(24 * l + 4 + h), None, ALU.mult))
                elif k == "mgrid":
                    _, _, h, d = s
                    n = grid_n[s]
                    g = GRIDB[n % 2]
                    mu = bank_of(s)
                    dve.wait_ge(*full_of(s))
                    dve.wait_ge(gc_ready, l + 1)
                    if n > 2:
                        dve.wait_ge(pv_done, mpv_before(s))
                    for t in tq:
                        ins = dve.scalar_tensor_tensor(g[:, t, t * P:(t + 1) * P], mu[:, t * P:(t + 1) * P],
                                                       GC[:, d, t, h:h + 1], TRI[:, d * P:(d + 1) * P], ALU.add,
                                                       ALU.add)
                    ins.then_inc(diag_ready, 1)
                    dve.wait_ge(grid_exp, n)
                    todo = [(j, t0, t1) for j in range(T) for t0, t1 in runs(l, d, j, True)]
                    for j, t0, t1 in todo:
                        if d == 0:
                            dve.wait_ge(*full_of(("mst", l, h, raw_bank(l, j)[0])))
                        i, o = raw_bank(l, j)
                        ins = dve.tensor_tensor(g[:, j, t0 * P:t1 * P], g[:, j, t0 * P:t1 * P],
                                                bank_of(("mst", l, h, i))[:, t0 * P + o:t1 * P + o], ALU.mult)
                    ins.then_inc(grid_ready, 1)
                    dve.wait_ge(grid_ready, n)
                    tick(dve, free_of(s)[0])
                    if d == 1:
                        for i in range(raw_banks(l)):
                            tick(dve, free_of(("mst", l, h, i))[0])
                elif k == "mpv":
                    _, _, h, d = s
                    acc = bank[6 + acc_at[s] % 2]
                    nt = len(tq)
                    av = acc[:, tq[0] * 97:(tq[0] + nt) * 97].rearrange("p (t e) -> p t e", e=97)
                    dve.wait_ge(pv_done, pv_at[s])
                    den = ST[:, 128:128 + nt]
                    link(dve.scalar_tensor_tensor(den, av[:, :, 96], -1.0, GC[:, 2 + d, tq[0]:tq[0] + nt, h],
                                                  ALU.mult, ALU.max))
                    link(dve.tensor_tensor(den, den, av[:, :, 96], ALU.max))
                    link(dve.reciprocal(den, den))
                    hs = HS[:, tq[0]:tq[0] + nt, h * ML_D:(h + 1) * ML_D]
                    if d == 0:
                        dve.tensor_tensor(hs, av[:, :, 0:ML_D], bcast(den, ML_D), ALU.mult).then_inc(acc_free, 1)
                        dve.wait_ge(acc_free, acc_at[s] + 1)
                    else:
                        tmp = RT[:, 0:384].rearrange("p (t e) -> p t e", t=4)[:, 0:nt, :]
                        dve.tensor_tensor(tmp, av[:, :, 0:ML_D], bcast(den, ML_D), ALU.mult).then_inc(acc_free, 1)
                        dve.wait_ge(acc_free, acc_at[s] + 1)
                        link(dve.tensor_tensor(hs, hs, tmp, ALU.add))
                elif k == "mln":
                    nt = len(tq)
                    hs = HS[:, tq[0]:tq[0] + nt, :].rearrange("p t (h e) -> p (t h) e", e=ML_D)
                    nn = nt * ML_H
                    sq = view(WORK, 2560, nn, ML_D)
                    mu = ST[:, 128:128 + nn]
                    link(dve.tensor_reduce(mu, hs, AX.X, ALU.add))
                    link(dve.tensor_scalar(mu, mu, 1.0 / ML_D, None, ALU.mult))
                    link(dve.tensor_tensor(hs, hs, bcast(mu, ML_D), ALU.subtract))
                    dve.wait_ge(pv_done, pv_at[("mpv", l, ML_H - 1, 1)])
                    link(dve.tensor_tensor(sq, hs, hs, ALU.mult))
                    link(dve.tensor_reduce(mu, sq, AX.X, ALU.add))
                    m, r = rstd(s, ML_D)
                    dve.tensor_scalar(m, mu, 1.0 / ML_D, EPS, ALU.mult, ALU.add).then_inc(mean_ready, 1)
                    dve.wait_ge(rstd_ready, rstd_at[s])
                    dve.tensor_tensor(hs, hs, bcast(r, ML_D), ALU.mult).then_inc(hn_ready, 1)
                elif k == "mlT":
                    h = s[2]
                    dve.wait_ge(*full_of(s))
                    o = MLT[:, h, c0:TOK]
                    link(dve.scalar_tensor_tensor(o, bank_of(s)[0:ML_D, c0:TOK], c96(24 * l + h),
                                                  UC[:, h, c0:TOK], ALU.mult, ALU.add))
                    tick(dve, free_of(s)[0])
                    dve.scalar_tensor_tensor(o, o, 0.5, ZS[:, h, c0:TOK], ALU.mult, ALU.mult).then_inc(mlt_ready, 1)
                    if h == ML_H - 1:
                        dve.wait_ge(mlt_ready, ML_H * (l + 1))
                elif k == "cnorm":
                    t = s[2]
                    m = ssq_cols(s)
                    mm, rr = rstd(s, 0)
                    dve.wait_ge(ssq_ready, ssq_at[s])
                    if t in tq:
                        link(dve.tensor_scalar(mm[:, 0:1], m[:, 0:1], 1.0 / Q_RANK, EPS, ALU.mult, ALU.add))
                    else:
                        link(dve.memset(mm[:, 0:1], 1.0))
                    dve.tensor_scalar(mm[:, 1:2], m[:, 1:2], 1.0 / KV_RANK, EPS, ALU.mult, ALU.add).then_inc(
                        mean_ready, 1)
                    dve.wait_ge(rstd_ready, rstd_at[s])
                    if t in tq:
                        link(dve.tensor_scalar(PRv[:, t, 0:Q_RANK], PRv[:, t, 0:Q_RANK], rr[:, 0:1], None, ALU.mult))
                    dve.tensor_scalar(PRv[:, t, Q_RANK:384], PRv[:, t, Q_RANK:384], rr[:, 1:2], None,
                                      ALU.mult).then_inc(cn_ready, 1)
                elif k == "cT":
                    t = s[2]
                    dve.wait_ge(*full_of(s))
                    for c in range(0 if t in tq else 2, 3):
                        ins = dve.tensor_scalar(CT[:, c, t * P:(t + 1) * P], bank_of(s)[:, c * P:(c + 1) * P],
                                                c2(16 + 3 * l + c), None, ALU.mult)
                    ins.then_inc(free_of(s)[0], 1)
                elif k == "uqk":
                    t = s[2]
                    kt = KTM[t % 2]
                    isq = t in tq
                    if t >= 2:
                        for key in qkT_jobs(("qkT", l, t - 2)):
                            dve.wait_ge(*full_of(key))
                    key = s + ("k", 0)
                    dve.wait_ge(*full_of(key))
                    kvv = bank_of(key)[:, 0:384].rearrange("p (h e) -> p h e", h=3)
                    dve.tensor_copy(kt[:, 0:3, 0:NOPE_D], kvv[:, :, 0:NOPE_D])
                    dve.tensor_copy(VV[:, t, 0:3, :], kvv[:, :, NOPE_D:]).then_inc(free_of(key)[0], 1)
                elif k == "uqs":
                    isq = s[2] in tq
                    key = ("uqk",) + s[1:]
                    m, r = rstd(key, 0)
                    if not isq:
                        dve.memset(m[:, 0:6], 1.0)
                    dve.wait_ge(usq_ready, uqk_n[key])
                    if isq:
                        dve.tensor_reduce(m[:, 0:6], SQU[0], AX.X, ALU.add)
                    link(dve.tensor_reduce(m[:, 6:12], SQU[1], AX.X, ALU.add))
                    dve.tensor_scalar(m, m, 1.0 / QK_D, EPS, ALU.mult, ALU.add).then_inc(mean_ready, 1)
                elif k == "uqn":
                    t = s[2]
                    q, kt = QTM[t % 2], KTM[t % 2]
                    m, r = rstd(("uqk", l, t), 0)
                    dve.wait_ge(rstd_ready, rstd_at[("uqk", l, t)])
                    both = ([(q, r[:, 0:6], bc_qg(l), SWAP[0])] if t in tq else []) + [
                        (kt, r[:, 6:12], bc_kg(l), SWAP[1])]

                    def each(op):
                        for x in both[:-1]:
                            op(*x)
                        link(op(*both[-1]))

                    each(lambda x_, rr, g_, sw: dve.tensor_tensor(x_, x_, bcast(rr, QK_D), ALU.mult))
                    gain = lambda x_, rr, g_, sw: dve.tensor_tensor(
                        x_, x_, g_.unsqueeze(1).broadcast_to([P, MLA_H, QK_D]), ALU.mult)
                    if t < 2:
                        for x in both:
                            ins = gain(*x)
                    else:
                        each(gain)
                        cos = ROv[:, t - 2, 0, :].unsqueeze(1).broadcast_to([P, MLA_H, ROPE_D])
                        sin = ROv[:, t - 2, 1, :].rearrange("p (a b c) -> p a b c", a=2, b=2)

                        def swapped(x_, rr, g_, sw):
                            x4 = x_[:, :, NOPE_D:].rearrange("p h (a b c) -> p h a b c", a=2, b=2)
                            s5 = sw.rearrange("p h (a b c) -> p h a b c", a=2, b=2)
                            for b_ in (0, 1):
                                sb_ = sin[:, :, b_, :].unsqueeze(1).broadcast_to([P, MLA_H, 2, 8])
                                o = dve.tensor_tensor(s5[:, :, :, b_, :], x4[:, :, :, 1 - b_, :], sb_, ALU.mult)
                            return o

                        each(swapped)
                        each(lambda x_, rr, g_, sw: dve.tensor_tensor(x_[:, :, NOPE_D:], x_[:, :, NOPE_D:], cos,
                                                                      ALU.mult))
                        for x_, rr, g_, sw in both:
                            ins = dve.tensor_tensor(x_[:, :, NOPE_D:], x_[:, :, NOPE_D:], sw, ALU.add)
                    ins.then_inc(qk_ready, 1)
                elif k == "qkT":
                    for key in qkT_jobs(s):
                        if key[3] == "q":
                            dve.wait_ge(*full_of(key))
                            hh = 3 * key[4]
                            dve.tensor_copy(QT[:, hh:hh + 3, s[2] * P:(s[2] + 1) * P],
                                            bank_of(key)[0:QK_D, 0:384].rearrange("p (h t) -> p h t",
                                                                                  h=3)).then_inc(free_of(key)[0], 1)
                elif k == "nan":
                    t = s[2]
                    isq = t in tq
                    dve.wait_ge(*free_of(("pP", l, "B", t)))
                    dve.wait_ge(*free_of(("pP", l, "C", t)))
                    h0 = 0 if isq else NA_H
                    x_ = PRv[:, t, PNQ + h0 * NA_D:PNV].rearrange("p (h e) -> p h e", e=NA_D)
                    nh = 2 * NA_H - h0
                    sq = SQN[:, 0:nh * NA_D].rearrange("p (h e) -> p h e", e=NA_D)
                    m, r = rstd(s, 0)
                    if not isq:
                        link(dve.memset(m[:, 0:4], 1.0))
                    link(dve.tensor_tensor(sq, x_, x_, ALU.mult))
                    link(dve.tensor_reduce(m[:, h0:8], sq, AX.X, ALU.add))
                    dve.tensor_scalar(m, m, 1.0 / NA_D, EPS, ALU.mult, ALU.add).then_inc(mean_ready, 1)
                    dve.wait_ge(rstd_ready, rstd_at[s])
                    link(dve.tensor_tensor(x_, x_, bcast(r[:, h0:8], NA_D), ALU.mult))
                    if isq:
                        xq = x_[:, 0:NA_H, :]
                        link(dve.tensor_tensor(xq, xq, bc_nq(l).unsqueeze(1).broadcast_to([P, NA_H, NA_D]),
                                               ALU.mult))
                    xk = x_[:, nh - NA_H:nh, :]
                    dve.tensor_tensor(xk, xk, bc_nk(l).unsqueeze(1).broadcast_to([P, NA_H, NA_D]),
                                      ALU.mult).then_inc(na_ready, 1)
                elif k == "S":
                    _, b, _, t, h, _ = s
                    u = UNIT_AT[s[1:]]
                    nk = keys_of(s)
                    bk = bank_of(s)
                    dve.wait_ge(*full_of(s))
                    if b == 1 and t >= 2:
                        dve.wait_ge(bias_masked, 2 * (l + 1))
                        link(dve.tensor_tensor(bk[:, L:TOK], bk[:, L:TOK], BIAS[:, t - 2, h, :], ALU.add))
                    if u >= 2:
                        dve.wait_ge(*free_of(("S",) + UNITS[u - 2]))
                    dve.tensor_reduce(neg_max(u), bk[:, 0:nk], AX.X, ALU.max, negate=True).then_inc(nmax_ready, 1)
                elif k == "ET" and s[1] == 0:
                    u = UNIT_AT[s[1:]]
                    nkt = keys_of(s) // P
                    dve.wait_ge(*full_of(s))
                    if u >= 2:
                        dve.wait_ge(pv_done, pv_at[("PV",) + UNITS[u - 2]])
                    dve.tensor_copy(PT[u % 2][:, 0:nkt, :].rearrange("p a b -> p (a b)"),
                                    bank_of(s)[:, 0:nkt * P]).then_inc(free_of(s)[0], 1)
                elif k == "OM":
                    _, b, _, t, h, _ = s
                    u = UNIT_AT[s[1:]]
                    nh = h + 1
                    s = ("OT",) + s[1:]
                    acc = bank[6 + acc_at[s] % 2]
                    dve.wait_ge(pv_done, pv_at[("PV",) + s[1:]])
                    rs = ST[:, 160:160 + nh]
                    link(dve.reciprocal(rs, exp_sums(u - h, nh)))
                    if OT_n[s] > 1:
                        dve.wait_ge(*full_of(OT_key[OT_n[s] - 1]))
                    dve.tensor_tensor(OM[:, 0:nh * 64].rearrange("p (h e) -> p h e", h=nh),
                                      acc[:, 0:nh * 64].rearrange("p (h e) -> p h e", h=nh), bcast(rs, 64),
                                      ALU.mult).then_inc(om_ready, 1)
                    dve.wait_ge(om_ready, OT_n[s])
                    tick(dve, acc_free)
                elif k == "OT":
                    _, b, _, t, h, _ = s
                    dve.wait_ge(*full_of(s))
                    dst = (MLAT, NAT)[b]
                    nc_ = (3, 2)[b]
                    dve.tensor_copy(dst[:, :, t * P:(t + 1) * P],
                                    bank_of(s)[:, 0:nc_ * P].rearrange("p (a t) -> p a t", a=nc_)).then_inc(
                        free_of(s)[0], 1)
                elif k == "wo":
                    t, n = s[2:]
                    st = t // 2
                    dve.wait_ge(*full_of(s))
                    dve.wait_ge(*free_of(("gbc", l, 1, st, n)))
                    dve.tensor_tensor(YT, bank_of(s)[:, :], GB[:, st, 512 * n:512 * n + 512], ALU.mult).then_inc(
                        free_of(s)[0], 1)
                    dve.wait_ge(*free_of(s))
                    xx = Xv[:, t, 512 * n:512 * n + 512]
                    ins = dve.tensor_tensor(xx, xx, YT, ALU.add)
                    if n:
                        ins.then_inc(resid_ready, 1)
                        dve.wait_ge(resid_ready, resid_at[s[:3]])
                    else:
                        link(ins)
                elif k == "rT":
                    nt, t0 = 2, 2 * s[2]
                    dve.wait_ge(*full_of(s))
                    aff = RT[:, 0:16 * nt]
                    sel = RT[:, 64:64 + 16 * nt]
                    dve.tensor_scalar(aff, bank_of(s)[:, 0:16 * nt], 0.5, 0.5, ALU.mult, ALU.add).then_inc(
                        free_of(s)[0], 1)
                    dve.wait_ge(*free_of(s))
                    a3 = aff.rearrange("p (t e) -> p t e", e=16)
                    s3 = sel.rearrange("p (t e) -> p t e", e=16)
                    link(dve.tensor_tensor(s3, a3, bc_rb.unsqueeze(1).broadcast_to([P, nt, 16]), ALU.add))
                    s4 = sel.rearrange("p (g e) -> p g e", e=4)
                    ng = 4 * nt
                    pr = RT[:, 128:128 + 6 * ng].rearrange("p (g e) -> p g e", e=6)
                    link(dve.tensor_tensor(pr[:, :, 0:3], s4[:, :, 0:3], s4[:, :, 1:4], ALU.add))
                    link(dve.tensor_tensor(pr[:, :, 3:5], s4[:, :, 0:2], s4[:, :, 2:4], ALU.add))
                    link(dve.tensor_tensor(pr[:, :, 5:6], s4[:, :, 0:1], s4[:, :, 3:4], ALU.add))
                    gs = RT[:, 224:224 + ng]
                    link(dve.tensor_reduce(gs, pr, AX.X, ALU.max))
                    g3 = gs.rearrange("p (t g) -> p t g", g=4)
                    mx = RT[:, 240:240 + nt]

                    def first_max(v3, m_, out3, wts, width):
                        link(dve.tensor_reduce(m_, v3, AX.X, ALU.max))
                        link(dve.tensor_tensor(out3, v3, bcast(m_, width), ALU.is_equal))
                        link(dve.tensor_tensor(out3, out3, wts, ALU.mult))
                        link(dve.tensor_reduce(m_, out3, AX.X, ALU.max))
                        link(dve.tensor_tensor(out3, out3, bcast(m_, width), ALU.is_equal))

                    wt16 = RANK.unsqueeze(1).broadcast_to([P, nt, 16])
                    wt4 = RANK[:, 12:16].unsqueeze(1).broadcast_to([P, nt, 4])
                    ing = RT[:, 244:244 + ng].rearrange("p (t g) -> p t g", g=4)
                    first_max(g3, mx, ing, wt4, 4)
                    off = RT[:, 260:260 + ng]
                    link(dve.tensor_scalar(off, RT[:, 244:244 + ng], -1.0, BIG, ALU.add, ALU.mult))
                    link(dve.tensor_tensor(s4, s4, bcast(off, 4), ALU.add))
                    oh0, oh1, gt, prod = of_tiles(OH[0], t0), of_tiles(OH[1], t0), of_tiles(RT[:, 280:], 0), of_tiles(
                        PROD, 0)
                    first_max(s3, mx, oh0, wt16, 16)
                    link(dve.scalar_tensor_tensor(s3, oh0, -4.0 * BIG, s3, ALU.mult, ALU.add))
                    first_max(s3, mx, oh1, wt16, 16)
                    link(dve.tensor_scalar(INCL, TRI[:, 0:P], 0.0, None, ALU.is_ge))
                    dve.tensor_tensor(of_tiles(ASSIGN, t0), oh0, oh1, ALU.add).then_inc(assign_ready, 1)
                    dve.wait_ge(assign_ready, pfx_n[("pfx",) + s[1:]])
                    link(dve.tensor_tensor(gt, of_tiles(ASSIGN, t0), a3, ALU.mult))
                    link(dve.tensor_reduce(mx, gt, AX.X, ALU.add))
                    link(dve.reciprocal(mx, mx))
                    link(dve.tensor_scalar(mx, mx, 0.5, None, ALU.mult))
                    gv = GATEv[:, t0:t0 + 2, :]
                    link(dve.tensor_tensor(gv, gt, bcast(mx, 16), ALU.mult))
                    for c, oh in ((0, oh0), (1, oh1)):
                        link(dve.tensor_tensor(prod, oh, gv, ALU.mult))
                        link(dve.tensor_reduce(ENT[:, t0:t0 + 2, c, 1], prod, AX.X, ALU.add))
                elif k == "pfx":
                    t0 = 2 * s[2]
                    dve.wait_ge(*full_of(s))
                    bk = bank_of(s)
                    prod, pick, most = of_tiles(PROD, 0), of_tiles(PICK, 0), RT[:, 240:241]
                    link(dve.scalar_tensor_tensor(pick, of_tiles(bk, 0), float(N_E),
                                                  RANK.unsqueeze(1).broadcast_to([P, 2, 16]), ALU.mult, ALU.subtract))
                    link(dve.tensor_reduce(most, bk[:, 64:80], AX.X, ALU.max))
                    tick(dve, free_of(s)[0])
                    for c in (0, 1):
                        link(dve.tensor_tensor(prod, of_tiles(OH[c], t0), pick, ALU.mult))
                        link(dve.tensor_reduce(SLOTF.rearrange("p (t c) -> p t c", c=2)[:, t0:t0 + 2, c], prod, AX.X,
                                               ALU.add))
                    if s[2]:
                        link(dve.tensor_scalar(OVER, most, float(CAP), None, ALU.is_gt))
                    dve.tensor_copy(SLOTU[:, 2 * t0:2 * t0 + 4], SLOTF[:, 2 * t0:2 * t0 + 4]).then_inc(route_ready, 1)
                elif k == "slots":
                    dve.wait_ge(slots_loaded, 16 * (l + 1))
                    dve.tensor_copy(TOKU, TABS[:, :, 0])
                    dve.tensor_copy(PAIRU, TABS[:, :, 2]).then_inc(index_ready, 1)
                elif k == "xT":
                    n = expert_n(l, s[2])
                    dve.wait_ge(*full_of(s + (0,)))
                    if n >= 2:
                        dve.wait_ge(*full_of(("ab",) + expert_key(n - 2)))
                    dve.tensor_copy(XGT[n % 2][:, 0:4, :].rearrange("p k t -> p (k t)"),
                                    bank_of(s + (0,))[:, :]).then_inc(free_of(s + (0,))[0], 1)
                elif k == "ab":
                    e = s[2]
                    n = ab_n[s]
                    dve.wait_ge(moe_tanh, n)
                    if n > 2:
                        dve.wait_ge(*full_of(("y",) + expert_key(n - 3) + ("T",)))
                    bk = bank_of(s)
                    link(dve.scalar_tensor_tensor(HID[n % 2], TH[n % 2], 1.0, bk[:, 0:FF], ALU.add, ALU.mult))
                    dve.scalar_tensor_tensor(HID[n % 2], HID[n % 2], TABS[:, e, 1:2], bk[:, FF:2 * FF],
                                             ALU.mult, ALU.mult).then_inc(hid_ready, 1)
                    dve.wait_ge(hid_ready, n)
                    tick(dve, free_of(s)[0])
                elif k == "y":
                    key = s + (0,)
                    n = expert_n(l, s[2])
                    dve.wait_ge(*full_of(key))
                    if n >= 2:
                        dve.wait_ge(ys_stored[n % 2], 16 * (n // 2))
                    dve.tensor_copy(YO[n % 2][:, 0:512], bank_of(key)[:, :]).then_inc(free_of(key)[0], 1)
                elif k == "comb":
                    t = s[2]
                    uses = sum(t in tiles_q(m) for m in range(l + 1))
                    dve.wait_ge(pair_loaded[t], 32 * uses)
                    link(dve.tensor_tensor(ACC[:, t, :], ACC[:, t, :], XS[:, t, :], ALU.add))
                elif k == "dense":
                    nt = len(tq)
                    d = dn[l]
                    over = dve.value_load(OVER[0:1, :])
                    with dve.If(over > 0):
                        dve.memset(ACC[:, tq[0]:T, :], 0.0).then_inc(d["zero"], 1)
                        dve.memset(XS[:, tq[0]:T, :], 0.0).then_inc(d["zero"], 1)
                        dve.wait_ge(d["zero"], 2)
                        tick(dve, d["hid"])
                        tick(dve, d["acc"])
                        gs = GATEv[:, tq[0]:T, :]
                        tmp = RT[:, 0:16 * nt].rearrange("p (t e) -> p t e", e=16)
                        with dve.Fori(0, N_E) as e:
                            for i, t in enumerate(tq):
                                dve.wait_ge(d["tanh"], e * nt + (i + 1))
                                dve.scalar_tensor_tensor(HID[0], TH[0], 1.0, bank[0][:, 0:FF], ALU.add,
                                                         ALU.mult).then_inc(d["half"], 1)
                                dve.wait_ge(d["half"], e * nt + (i + 1))
                                dve.scalar_tensor_tensor(HID[0], HID[0], GATEv[:, t, 0:1], bank[0][:, FF:2 * FF],
                                                         ALU.mult, ALU.mult).then_inc(d["hid"], 1)
                                dve.wait_ge(d["T"], e * nt + (i + 1))
                                dve.tensor_copy(HIDT[0].rearrange("p k t -> p (k t)"),
                                                bank[1][:, 0:FF]).then_inc(d["ht"], 1)
                                dve.wait_ge(d["y"], e * nt + (i + 1))
                                dve.wait_ge(d["acc"], e * nt + (i + 1))
                                for nn in (0, 1):
                                    o = ACC[:, t, 512 * nn:512 * nn + 512]
                                    ins = dve.tensor_tensor(o, o, bank[2 + nn][:, :], ALU.add)
                                ins.then_inc(d["acc"], 1)
                                dve.wait_ge(d["acc"], e * nt + (i + 2))
                            dve.tensor_copy(tmp[:, :, 0:N_E - 1], gs[:, :, 1:N_E]).then_inc(d["gate"], 1)
                            dve.wait_ge(d["gate"], e * 2 + 1)
                            dve.tensor_copy(gs[:, :, 0:N_E - 1], tmp[:, :, 0:N_E - 1]).then_inc(d["gate"], 1)
                            dve.wait_ge(d["gate"], e * 2 + 2)
                elif k == "moe_out":
                    t = s[2]
                    st = t // 2
                    if t == tq[0]:
                        for nn in (0, 1):
                            for st_ in sorted({t_ // 2 for t_ in tq}):
                                dve.wait_ge(*free_of(("gbc2", l, st_, nn)))
                    link(dve.tensor_tensor(ACC[:, t, :], ACC[:, t, :], GB[:, st, :], ALU.mult))
                    ins = dve.tensor_tensor(Xv[:, t, :], Xv[:, t, :], ACC[:, t, :], ALU.add)
                    ins.then_inc(resid_ready if l < DEPTH - 1 else out_ready, 1)


INPUTS = ["x", "c", "ctx", "c_ctx", "w_mod", "b_mod", "norm1_g", "norm2_g", "w_in", "w_out", "mla_qnorm_g",
          "mla_w_uq", "mla_kvnorm_g", "mla_w_ukv", "mla_q_g", "mla_k_g", "ml_conv_w", "ml_conv_b", "ml_w_q",
          "ml_w_k", "ml_w_v", "ml_gate_b", "ml_norm_g", "ml_skip", "na_q_g", "na_k_g", "na_rpb", "router_w",
          "router_b", "moe_w1", "moe_w3", "moe_w2"]


def shape_constants():
    t = np.arange(L)
    inv = 10000.0 ** (-np.arange(ROPE_D // 4, dtype=np.float32) / (ROPE_D // 4))
    ar = (t // GRID).astype(np.float32)[:, None] * inv
    ac = (t % GRID).astype(np.float32)[:, None] * inv
    cos = np.cos(np.concatenate([ar, ar, ac, ac], axis=-1))
    sin = np.sin(np.concatenate([-ar, ar, -ac, ac], axis=-1))
    table = np.zeros((P, 2, 2, ROPE_D), np.float32)
    for i in (0, 1):
        table[:, i, 0], table[:, i, 1] = cos[i * P:(i + 1) * P], sin[i * P:(i + 1) * P]
    rank = np.tile(np.arange(16, 0, -1, dtype=np.float32), (P, 1))
    ent = np.zeros((P, T, 2, 4), np.float32)
    tok = np.arange(P)[:, None] + P * np.arange(T)[None, :]
    for c in (0, 1):
        ent[:, :, c, 0] = tok
        ent[:, :, c, 2] = TOK * c + tok
    return np.ascontiguousarray(np.concatenate([table.reshape(P, -1), rank, ent.reshape(P, -1)],
                                               axis=1).astype(np.float32))


def kernel(**inputs):
    import numpy as _np
    import concourse.bacc as _bacc
    from concourse import mybir as _mybir
    from concourse.bass_utils import run_bass_kernel_spmd as _run

    nc = _bacc.Bacc("TRN2", target_bir_lowering=False, num_devices=1)
    arrays, aps = {}, {}
    data = {name: _np.ascontiguousarray(inputs[name]) for name in INPUTS}
    data["rope"] = shape_constants()
    for name, v in data.items():
        arrays[f"in_{name}"] = v
        aps[name] = nc.dram_tensor(f"in_{name}", v.shape, _mybir.dt.from_np(v.dtype), kind="ExternalInput").ap()
    aps["out"] = nc.dram_tensor("out_x", (1, L, D), F32, kind="ExternalOutput").ap()
    build(nc, aps)
    r = _run(nc, [arrays], core_ids=[0])
    return r.results[0]["out_x"]
```
